# Optimizing a Trainium2 kernel written in Bass

```python
import jax, jax.numpy as jnp
from jax import lax
import numpy as np

D_MODEL = 1024
BATCH = 1
SEQ = 1024
DEPTH = 1
DEC_BATCH = 1
DEC_SEQ = 32
PAST_LEN = 512

CHUNK = 64
D_MIX = D_MODEL
D_CONV = D_MIX // 2
CONV_W = 3
N_HEADS = 8
HEAD_DIM = (D_MIX - D_CONV) // N_HEADS
N_KV_HEADS = 2
GROUP = N_HEADS // N_KV_HEADS
IDX_HEADS = 8
IDX_DIM = 64
TOPK_MAX = 256
Q_BLOCK = 128
N_MEM = 256
MEM_HEADS = 4
MEM_HEAD_DIM = D_MODEL // MEM_HEADS
D_FF = 2816
ALPHA = (2.0 * DEPTH) ** 0.25
BETA = (8.0 * DEPTH) ** -0.25
LN_EPS = 1e-5
MIX_SPLITS = (D_CONV, D_CONV, D_CONV, N_HEADS * HEAD_DIM, N_KV_HEADS * HEAD_DIM,
              N_KV_HEADS * HEAD_DIM, IDX_HEADS * IDX_DIM, IDX_DIM, IDX_HEADS)
D_MIX_IN = sum(MIX_SPLITS)

kernel_name = "hybrid_conv_dsa_streaming_step"

def _layer_norm(x, g, b):
    xf = x.astype(jnp.float32)
    mu = xf.mean(-1, keepdims=True)
    var = jnp.square(xf - mu).mean(-1, keepdims=True)
    y = (xf - mu) * lax.rsqrt(var + LN_EPS) * g.astype(jnp.float32) + b.astype(jnp.float32)
    return y.astype(x.dtype)

def _swiglu(x, w_gate, w_up, w_down):
    return (jax.nn.silu(x @ w_gate) * (x @ w_up)) @ w_down

def _dsa_attention(q, k, v, qi, ki, wi, q_pos, k_pos, top_k):
    b, t = q.shape[:2]
    qb = min(Q_BLOCK, t)
    nb = t // qb
    k_chunk = k_pos // CHUNK
    gather = jax.vmap(lambda rows, ids: rows[ids])

    def blocks(a):
        return a.reshape((b, nb, qb) + a.shape[2:]).swapaxes(0, 1)

    def one_block(args):
        q_b, qi_b, wi_b, qpos_b = args
        q_chunk = qpos_b // CHUNK
        logits = jnp.einsum('bqhd,bsd->bqsh', qi_b, ki)
        score = jnp.einsum('bqsh,bqh->bqs', jax.nn.relu(logits), wi_b).astype(jnp.float32)
        admissible = k_chunk[None, :] <= q_chunk[:, None]
        score = jnp.where(admissible[None], score, -jnp.inf)
        _, idx = lax.top_k(score, top_k)
        k_sel = gather(k, idx)
        v_sel = gather(v, idx)
        valid = k_chunk[idx] <= q_chunk[None, :, None]
        s = jnp.einsum('bqhgd,bqkhd->bqhgk', q_b, k_sel).astype(jnp.float32) * (HEAD_DIM ** -0.5)
        s = jnp.where(valid[:, :, None, None, :], s, -jnp.inf)
        p = jax.nn.softmax(s, axis=-1).astype(v.dtype)
        return jnp.einsum('bqhgk,bqkhd->bqhgd', p, v_sel)

    out = lax.map(one_block, (blocks(q), blocks(qi), blocks(wi), q_pos.reshape(nb, qb)))
    return out.swapaxes(0, 1).reshape(q.shape)

def _mem_attention(x, mem_k, mem_v, w_q, w_o):
    b, t, _ = x.shape
    q = (x @ w_q).reshape(b, t, MEM_HEADS, MEM_HEAD_DIM)
    s = jnp.einsum('bthd,bmhd->bhtm', q, mem_k).astype(jnp.float32) * (MEM_HEAD_DIM ** -0.5)
    p = jax.nn.softmax(s, axis=-1).astype(mem_v.dtype)
    o = jnp.einsum('bhtm,bmhd->bthd', p, mem_v).reshape(b, t, MEM_HEADS * MEM_HEAD_DIM)
    return o @ w_o

def _layer(x, conv_prev, k_past, v_past, ik_past, mem_k, mem_v, pos0, top_k, p):
    b, t, _ = x.shape
    x = _layer_norm(ALPHA * x + 0.5 * _swiglu(x, p['ffn1_gate'], p['ffn1_up'], p['ffn1_down']),
                    p['ln1_g'], p['ln1_b'])
    proj = x @ p['w_mix_in']
    h, gate_b, gate_c, q, k, v, qi, ki, wi = jnp.split(
        proj, np.cumsum(MIX_SPLITS)[:-1].tolist(), axis=-1)
    u = gate_c * h
    u_pad = jnp.concatenate([conv_prev, u], axis=1)
    w = p['conv_w']
    conv = sum(w[j] * u_pad[:, j:j + t] for j in range(CONV_W))
    y_conv = gate_b * conv
    new_conv = u_pad[:, -(CONV_W - 1):]
    q = q.reshape(b, t, N_KV_HEADS, GROUP, HEAD_DIM)
    k = k.reshape(b, t, N_KV_HEADS, HEAD_DIM)
    v = v.reshape(b, t, N_KV_HEADS, HEAD_DIM)
    qi = qi.reshape(b, t, IDX_HEADS, IDX_DIM)
    wi = wi * ((IDX_HEADS * IDX_DIM) ** -0.5)
    k_all = jnp.concatenate([k_past, k], axis=1)
    v_all = jnp.concatenate([v_past, v], axis=1)
    ki_all = jnp.concatenate([ik_past, ki], axis=1)
    q_pos = pos0 + jnp.arange(t)
    k_pos = jnp.arange(k_all.shape[1])
    y_attn = _dsa_attention(q, k_all, v_all, qi, ki_all, wi, q_pos, k_pos, top_k)
    y_attn = y_attn.reshape(b, t, N_HEADS * HEAD_DIM)
    mix = jnp.concatenate([y_conv, y_attn], axis=-1) @ p['w_mix_out']
    x = _layer_norm(ALPHA * x + mix, p['ln2_g'], p['ln2_b'])
    x = _layer_norm(ALPHA * x + _mem_attention(x, mem_k, mem_v, p['w_mem_q'], p['w_mem_o']),
                    p['ln3_g'], p['ln3_b'])
    x = _layer_norm(ALPHA * x + 0.5 * _swiglu(x, p['ffn2_gate'], p['ffn2_up'], p['ffn2_down']),
                    p['ln4_g'], p['ln4_b'])
    return x, new_conv, k, v, ki

def setup_inputs(seed: int = 0) -> dict:
    key = jax.random.key(seed)
    ks = iter(jax.random.split(key, 40))
    f32 = jnp.float32

    def nrm(shape, scale=1.0):
        return jax.random.normal(next(ks), shape, f32) * scale

    def gain():
        return 1.0 + nrm((DEPTH, D_MODEL), 0.05)

    def bias():
        return nrm((DEPTH, D_MODEL), 0.02)

    return {
        "x_prompt": nrm((BATCH, SEQ, D_MODEL)),
        "x_sample": nrm((DEC_BATCH, DEC_SEQ, D_MODEL)),
        "cache_conv": nrm((DEPTH, DEC_BATCH, CONV_W - 1, D_CONV)),
        "cache_k": nrm((DEPTH, DEC_BATCH, PAST_LEN, N_KV_HEADS, HEAD_DIM)),
        "cache_v": nrm((DEPTH, DEC_BATCH, PAST_LEN, N_KV_HEADS, HEAD_DIM)),
        "cache_idx_k": nrm((DEPTH, DEC_BATCH, PAST_LEN, IDX_DIM)),
        "cache_mem_k": nrm((DEPTH, DEC_BATCH, N_MEM, MEM_HEADS, MEM_HEAD_DIM)),
        "cache_mem_v": nrm((DEPTH, DEC_BATCH, N_MEM, MEM_HEADS, MEM_HEAD_DIM)),
        "mem_prompt": nrm((BATCH, N_MEM, D_MODEL)),
        "ffn1_gate": nrm((DEPTH, D_MODEL, D_FF), D_MODEL ** -0.5),
        "ffn1_up": nrm((DEPTH, D_MODEL, D_FF), D_MODEL ** -0.5),
        "ffn1_down": nrm((DEPTH, D_FF, D_MODEL), BETA * D_FF ** -0.5),
        "ln1_g": gain(), "ln1_b": bias(),
        "w_mix_in": nrm((DEPTH, D_MODEL, D_MIX_IN), D_MODEL ** -0.5),
        "conv_w": nrm((DEPTH, CONV_W, D_CONV), CONV_W ** -0.5),
        "w_mix_out": nrm((DEPTH, D_MIX, D_MODEL), BETA * D_MIX ** -0.5),
        "ln2_g": gain(), "ln2_b": bias(),
        "w_mem_q": nrm((DEPTH, D_MODEL, MEM_HEADS * MEM_HEAD_DIM), D_MODEL ** -0.5),
        "w_mem_k": nrm((DEPTH, D_MODEL, MEM_HEADS * MEM_HEAD_DIM), D_MODEL ** -0.5),
        "w_mem_v": nrm((DEPTH, D_MODEL, MEM_HEADS * MEM_HEAD_DIM), D_MODEL ** -0.5),
        "w_mem_o": nrm((DEPTH, MEM_HEADS * MEM_HEAD_DIM, D_MODEL), BETA * D_MODEL ** -0.5),
        "ln3_g": gain(), "ln3_b": bias(),
        "ffn2_gate": nrm((DEPTH, D_MODEL, D_FF), D_MODEL ** -0.5),
        "ffn2_up": nrm((DEPTH, D_MODEL, D_FF), D_MODEL ** -0.5),
        "ffn2_down": nrm((DEPTH, D_FF, D_MODEL), BETA * D_FF ** -0.5),
        "ln4_g": gain(), "ln4_b": bias(),
    }

def reference(x_prompt, x_sample, cache_conv, cache_k, cache_v, cache_idx_k, cache_mem_k, cache_mem_v,
              mem_prompt, ffn1_gate, ffn1_up, ffn1_down, ln1_g, ln1_b, w_mix_in, conv_w, w_mix_out,
              ln2_g, ln2_b, w_mem_q, w_mem_k, w_mem_v, w_mem_o, ln3_g, ln3_b,
              ffn2_gate, ffn2_up, ffn2_down, ln4_g, ln4_b):
    b_p, t_p, _ = x_prompt.shape
    top_k_prompt = min(TOPK_MAX, t_p // 4)
    top_k_sample = min(TOPK_MAX, (cache_k.shape[2] + x_sample.shape[1]) // 4)
    past = cache_k.shape[2]
    y_p, y_s = x_prompt, x_sample
    conv_p, k_p, v_p, ik_p, mk_p, mv_p = [], [], [], [], [], []
    conv_s, k_s, v_s, ik_s = [], [], [], []
    for l in range(DEPTH):
        p = dict(ffn1_gate=ffn1_gate[l], ffn1_up=ffn1_up[l], ffn1_down=ffn1_down[l],
                 ln1_g=ln1_g[l], ln1_b=ln1_b[l], w_mix_in=w_mix_in[l], conv_w=conv_w[l],
                 w_mix_out=w_mix_out[l], ln2_g=ln2_g[l], ln2_b=ln2_b[l],
                 w_mem_q=w_mem_q[l], w_mem_o=w_mem_o[l], ln3_g=ln3_g[l], ln3_b=ln3_b[l],
                 ffn2_gate=ffn2_gate[l], ffn2_up=ffn2_up[l], ffn2_down=ffn2_down[l],
                 ln4_g=ln4_g[l], ln4_b=ln4_b[l])
        mem_k = (mem_prompt @ w_mem_k[l]).reshape(b_p, N_MEM, MEM_HEADS, MEM_HEAD_DIM)
        mem_v = (mem_prompt @ w_mem_v[l]).reshape(b_p, N_MEM, MEM_HEADS, MEM_HEAD_DIM)
        dt = x_prompt.dtype
        y_p, c_new, k_new, v_new, ik_new = _layer(
            y_p, jnp.zeros((b_p, CONV_W - 1, D_CONV), dt),
            jnp.zeros((b_p, 0, N_KV_HEADS, HEAD_DIM), dt), jnp.zeros((b_p, 0, N_KV_HEADS, HEAD_DIM), dt),
            jnp.zeros((b_p, 0, IDX_DIM), dt), mem_k, mem_v, 0, top_k_prompt, p)
        conv_p.append(c_new); k_p.append(k_new); v_p.append(v_new); ik_p.append(ik_new)
        mk_p.append(mem_k); mv_p.append(mem_v)
        y_s, c_new, k_new, v_new, ik_new = _layer(
            y_s, cache_conv[l], cache_k[l], cache_v[l], cache_idx_k[l],
            cache_mem_k[l], cache_mem_v[l], past, top_k_sample, p)
        conv_s.append(c_new); k_s.append(k_new); v_s.append(v_new); ik_s.append(ik_new)
    return (y_p, y_s,
            jnp.stack(conv_p), jnp.stack(k_p), jnp.stack(v_p), jnp.stack(ik_p),
            jnp.stack(mk_p), jnp.stack(mv_p),
            jnp.stack(conv_s), jnp.stack(k_s), jnp.stack(v_s), jnp.stack(ik_s))


_drawn_inputs = setup_inputs


def setup_inputs(seed=0):
    import zlib

    import numpy as np

    out = dict(_drawn_inputs(seed))
    spreads = {}
    factors = {'ln2_b': 2.865, 'ln3_b': 2.827, 'ln4_b': 2.93}
    for name, (base, spread) in spreads.items():
        noise = np.random.default_rng([zlib.crc32(name.encode()), seed]).standard_normal(out[name].shape)
        drawn = base * np.exp(spread * noise) if base else spread * noise
        out[name] = __import__('jax').numpy.asarray(drawn.astype(out[name].dtype))
    for name, factor in factors.items():
        out[name] = (out[name] * factor).astype(out[name].dtype)
    return out
```

```python
from contextlib import ExitStack

import concourse.bass as bass
from concourse import mybir

F32 = mybir.dt.float32
F32R = mybir.dt.float32r
ALU = mybir.AluOpType
ACT = mybir.ActivationFunctionType
AX_X = mybir.AxisListType.X

P = 128
D = 1024
KD = D // P
F = 2816
SEQ = 1024
DEC = 32
PAST = 512
HALF = SEQ // 2
SKEYS = PAST + DEC
CHUNK = 64
DH = 64
HEADS = 8
N_MEM = 256
DCONV = 512
KC = DCONV // P
EPS = 1e-5
ALPHA = 2.0 ** 0.25
ATT_SCALE = DH ** -0.5
MEM_SCALE = 256.0 ** -0.5
WI_SCALE = (8 * 64) ** -0.5
TAKEN = -3.0e38
CLOSED = -2.0e38
CUT = -2.5e38
FAR = -1.0e30

FFN_PARTS = [(0, 8), (8, 8), (16, 6)]
RING = 4
AHEAD = 2


class Group:
    def __init__(self, index):
        self.index = index
        self.sample = index == 0
        self.cols = HALF + (DEC if self.sample else 0)
        self.parts = 2 if self.sample else 1
        self.width = self.cols // self.parts
        self.tiles = [(128 * t, 128) for t in range(4)] + ([(HALF, DEC)] if self.sample else [])

    def folded(self, ap):
        return ap.rearrange("p (a b) -> p a b", a=self.parts)


GROUPS = [Group(0), Group(1)]


def score_tiles(g):
    if g.sample:
        return [(2, 128, 384, 32), (3, 128, 512, 32), (4, DEC, SKEYS, (SKEYS // 4) // 8)]
    return [(t, 128, 128 * (5 + t), 32) for t in range(4)]


def att_tiles(g):
    out = []
    for t, (col, rows) in enumerate(g.tiles):
        out.append((t, col, rows, SKEYS if rows == DEC else 128 * (4 * g.index + t + 1)))
    return out


SCORE_AT = {}
_at = 0
for _g in GROUPS:
    for _t, _r, _n, _k in score_tiles(_g):
        SCORE_AT[(_g.index, _t)] = _at
        _at += _n
SCORE_COLS = _at

OFF_H, OFF_B, OFF_C = 0, DCONV, 2 * DCONV
OFF_Q = 3 * DCONV
OFF_K = OFF_Q + 512
OFF_V = OFF_K + 128
OFF_QI = OFF_V + 128
OFF_KI = OFF_QI + 512
KIW = 72
MIX_TILES = [("kiw", 0, OFF_KI, KIW), ("k", 0, OFF_K, 128), ("v", 0, OFF_V, 128)]
MIX_TILES += [("qi", i, OFF_QI + P * i, P) for i in range(4)]
MIX_TILES += [("q", i, OFF_Q + P * i, P) for i in range(4)]
for _i in range(KC):
    MIX_TILES += [("h", _i, OFF_H + P * _i, P), ("c", _i, OFF_C + P * _i, P), ("b", _i, OFF_B + P * _i, P)]

FRONT = ["loadx", "ffn", "ln", "mix", "idx", "spill"]
BACK = ["reload", "att", "mixout", "ln", "memq", "mematt", "memo", "ln", "ffn", "ln"]


def schedule():
    plan = [("memload", None, 0), ("memkv", None, 0)]
    for g in (0, 1):
        plan += [(s, g, 1 if s == "ffn" else (1 if s == "ln" else 0)) for s in FRONT]
    for g in (0, 1):
        which = {"ffn": iter([2]), "ln": iter([2, 3, 4])}
        plan += [(s, g, next(which[s]) if s in which else 0) for s in BACK]
    stages = []
    at = dict(n=0, back=0, fwd=0, s=0, pt=0, o=0, idx=0, tok=0, mult=0, half=0, conv=0, load0=0, load1=0, store0=0, store1=0)
    for name, index, which in plan:
        g = GROUPS[index] if index is not None else None
        stages.append(dict(name=name, g=g, which=which, **at))
        tiles = len(g.tiles) if g else 2
        if name in ("memload", "loadx", "ln") and (name, which) != ("ln", 4):
            at["back"] += tiles
        if name in ("memload", "loadx"):
            at["load0"] += (tiles + 1) // 2
            at["load1"] += tiles // 2
        if name == "ln":
            at["fwd"] += tiles
            if which == 4:
                at["store0"] += (tiles + 1) // 2
                at["store1"] += tiles // 2
        if name == "ffn":
            at["mult"] += F // P
            at["half"] += KD * len(FFN_PARTS)
            at["n"] += 2 * (F // P) + KD * len(FFN_PARTS)
        if name == "memkv":
            at["n"] += 2 * KD
            at["pt"] += 3
        if name == "mix":
            at["n"] += len(MIX_TILES)
            at["tok"] += tiles
            at["conv"] += KC
        if name in ("mixout", "memq", "memo"):
            at["n"] += KD
        if name == "idx":
            at["idx"] += sum(HEADS * ((keys + 511) // 512) for _, _, keys, _ in score_tiles(g))
        if name == "att":
            at["s"] += len(att_jobs(g))
            at["pt"] += len(att_jobs(g))
            at["o"] += len(att_jobs(g)) // 4
        if name == "mematt":
            at["s"] += 4 + 4 * g.sample
            at["pt"] += 4 + 8 * g.sample
            at["o"] += 8 + 4 * g.sample
    return stages, at["n"]


def att_jobs(g):
    return [(t, col, rows, keys, kvg, hh) for t, col, rows, keys in att_tiles(g)
            for kvg in range(2) for hh in (0, 2, 1, 3)]


def half(i, m):
    return i * 2 + m // 2


def encoder_step(nc, ins, outs):
    STAGES, NT = schedule()
    ctx = ExitStack()
    with ctx:
        at = [(nc.sbuf_base + 31) // 32 * 32]

        def region(size):
            start = at[0]
            at[0] += (size + 31) // 32 * 32
            return start

        def place(name, shape, dtype, offset):
            return nc.alloc_sbuf_tensor_at(name, shape, dtype, offset=offset)

        GC = 544
        r_xh = region(KD * GC * 4)
        r_xl = region(KD * GC * 4)
        r_hh = region(KD * GC * 4)
        r_hl = region(KD * GC * 4)
        r_y = region(KD * GC * 4)
        XH = place("XH", [P, KD, GC], F32R, r_xh)
        XL = place("XL", [P, KD, GC], F32R, r_xl)
        HH = place("HH", [P, KD, GC], F32R, r_hh)
        HL = place("HL", [P, KD, GC], F32R, r_hl)
        Y = place("Y", [P, KD, GC], F32, r_y)
        QX = place("QX", [P, KD, GC], F32, r_hh)
        YCH = place("YCH", [P, KC, GC], F32R, r_hl)
        YCL = place("YCL", [P, KC, GC], F32R, r_hl + KC * GC * 4)
        QA = place("QA", [P, KC, GC], F32, r_xh)
        PR = place("PR", [P, 2, 1024], F32, r_xh + KC * GC * 4)
        PT = place("PT", [P, 8, 4, P], F32, r_xl)
        QM = place("QM", [P, KD, GC], F32, r_hh)
        PTM = place("PTM", [P, 2, 4, GC], F32, r_hl)
        MKTOK = place("MKTOK", [P, 2, D], F32, r_hh)

        WRAW = place("WRAW", [P, 2, KD, P], F32, region(2 * D * 4))
        WH = place("WH", [P, RING, KD, P], F32R, region(RING * D * 4))
        WL = place("WL", [P, RING, KD, P], F32R, region(RING * D * 4))
        KPA = place("KPA", [P, SEQ], F32, region(SEQ * 4))
        KPB = place("KPB", [P, SEQ], F32, region(SEQ * 4))
        KSA = place("KSA", [P, SKEYS], F32, region(SKEYS * 4))
        KSB = place("KSB", [P, SKEYS], F32, region(SKEYS * 4))
        KIP = place("KIP", [P, SEQ], F32, region(SEQ * 4))
        KIS = place("KIS", [P, SKEYS], F32, region(SKEYS * 4))
        VP = place("VP", [P, 8, P], F32, region(SEQ * 4))
        VS = place("VS", [P, 5, P], F32, region(5 * P * 4))
        MKT = place("MKT", [P, KD, N_MEM], F32, region(KD * N_MEM * 4))
        MV = place("MV", [P, 2, D], F32, region(2 * D * 4))
        SC = place("SC", [P, SCORE_COLS], F32, region(SCORE_COLS * 4))
        r_t = region(16384)
        XT = place("XT", [P, 2, D], F32, r_t)
        GB = place("GB", [P, 2, D], F32, r_t + 8192)
        FG = place("FG", [P, 2, GC], F32, r_t)
        FP_ = place("FP", [P, GC], F32, r_t + 2 * GC * 4)
        KVT = place("KVT", [P, 3, GC], F32, r_t)
        TOK = place("TOK", [P, 2, 328], F32, r_t + 3 * GC * 4)
        HB = place("HB", [P, GC], F32, r_t + 9152)
        UB = place("UB", [P, 548], F32, r_t + 9152 + 2176)
        CB = place("CB", [P, 548], F32, r_t + 9152 + 2176 + 2208)
        RB = place("RB", [P, 4, 512], F32, r_t)
        CK = place("CK", [P, 4, 192], F32, r_t)
        PM = place("PM", [P, 2, 4, N_MEM], F32, r_t)
        MKS = place("MKS", [P, 2, 256], F32, r_t + 8192)
        MVS = place("MVS", [P, 2, 256], F32, r_t + 8192 + 2048)
        MKTS = place("MKTS", [P, 2, 256], F32, r_t + 8192 + 4096)

        ident = place("ident", [P, P], F32, region(512))
        DM = place("DM", [P, 256], F32, region(1024))
        WI = place("WI", [P, 5, 8], F32, region(160))
        CW = place("CW", [P, 3, KC], F32, region(64))
        CPREV = place("CPREV", [P, KC, 2], F32, region(32))
        TAILP = place("TAILP", [P, KC, 2], F32, region(32))
        TAILS = place("TAILS", [P, KC, 2], F32, region(32))
        ST = place("ST", [P, 2, 12], F32, region(96))
        MVAR = place("MVAR", [P, 2, 2], F32, region(32))
        VE = place("VE", [P, 2], F32, region(32))
        RSTD = place("RSTD", [P, 2], F32, region(32))
        MHALF = place("MHALF", [P, 1], F32, region(32))
        M8 = place("M8", [P, 8], F32, region(32))
        MX = place("MX", [P, 2, 4], F32, region(32))
        NM = place("NM", [P, 2, 4], F32, region(32))
        RS = place("RS", [P, 2, 4], F32, region(32))
        RR = place("RR", [P, 2, 4], F32, region(32))
        assert at[0] <= nc.sbuf_usable_end, (at[0], nc.sbuf_usable_end)

        LIN = ctx.enter_context(nc.psum_tensor("LIN", [P, 2, 2, 512], F32))
        TR = ctx.enter_context(nc.psum_tensor("TR", [P, 2, 1024], F32))

        spill_q = [nc.dram_tensor(f"spill_q{i}", [P, KC, GC], F32, kind="Internal").ap() for i in range(2)]
        spill_y = [nc.dram_tensor(f"spill_y{i}", [P, KD, GC], F32, kind="Internal").ap() for i in range(2)]
        spill_ch = [nc.dram_tensor(f"spill_ch{i}", [P, KC, GC], F32, kind="Internal").ap() for i in range(2)]
        spill_cl = [nc.dram_tensor(f"spill_cl{i}", [P, KC, GC], F32, kind="Internal").ap() for i in range(2)]

        def sem(name):
            return ctx.enter_context(nc.semaphore(name))

        raw_loaded = [sem(f"raw_loaded{i}") for i in range(2)]
        hi_split = sem("hi_split")
        lo_split = sem("lo_split")
        product = sem("product")
        product_read = [sem(f"product_read{i}") for i in range(2)]
        pe_end = sem("pe_end")
        act_end = sem("act_end")
        dve_end = sem("dve_end")
        pool_end = sem("pool_end")
        consts = sem("consts")
        masks = sem("masks")
        moved = sem("moved")
        stored = sem("stored")
        xt_loaded = [sem(f"xt_loaded{i}") for i in range(2)]
        xt_stored = [sem(f"xt_stored{i}") for i in range(2)]
        back_done = sem("back_done")
        back_hi = sem("back_hi")
        back_lo = sem("back_lo")
        fwd_done = sem("fwd_done")
        fwd_read = sem("fwd_read")
        var_ready = sem("var_ready")
        rstd_ready = sem("rstd_ready")
        xt_ready = sem("xt_ready")
        gated = sem("gated")
        multiplied = sem("multiplied")
        hidden_hi = sem("hidden_hi")
        hidden_lo = sem("hidden_lo")
        halved = sem("halved")
        added = sem("added")
        dve_step = sem("dve_step")
        act_step = sem("act_step")
        pool_step = sem("pool_step")
        tok_done = sem("tok_done")
        tok_read = sem("tok_read")
        tok_stored = [sem(f"tok_stored{i}") for i in range(2)]
        yc_ready = sem("yc_ready")
        yc_hi = sem("yc_hi")
        yc_lo = sem("yc_lo")
        h_read = sem("h_read")
        idx_done = sem("idx_done")
        relu_done = sem("relu_done")
        idx_added = sem("idx_added")
        s_done = sem("s_done")
        nm_ready = sem("nm_ready")
        exp_done = sem("exp_done")
        p_ready = sem("p_ready")
        pt_done = sem("pt_done")
        pt_read = sem("pt_read")
        o_done = sem("o_done")
        o_hi = sem("o_hi")
        o_lo = sem("o_lo")
        ck_loaded = sem("ck_loaded")
        head_loaded = sem("head_loaded")

        block = ctx.enter_context(nc.Block())

        gate_w = [ins[f"ffn{k}_gate"][0].rearrange("(c p) f -> p c f", p=P) for k in (1, 2)]
        up_w = [ins[f"ffn{k}_up"][0].rearrange("(c p) f -> p c f", p=P) for k in (1, 2)]
        down_w = [ins[f"ffn{k}_down"][0].rearrange("(c p) d -> p c d", p=P) for k in (1, 2)]
        mix_w = ins["w_mix_in"][0].rearrange("(c p) f -> p c f", p=P)

        def square(name):
            return ins[name][0].rearrange("(c p) f -> p c f", p=P)

        x_tok = [ins["x_prompt"][0], ins["x_sample"][0]]

        @block.sync
        def _(sp):
            def load(i, m, src, nk=KD, cols=P):
                if m >= 2:
                    sp.wait_ge(lo_split, i * 4 + (m - 1))
                sp.dma_start(WRAW[:, m % 2, 0:nk, 0:cols], src).then_inc(raw_loaded[m % 2], 16)

            for st in STAGES:
                n0, name = st["n"], st["name"]
                if name == "memkv":
                    for j in range(16):
                        load(0, j, square(("w_mem_k", "w_mem_v")[j // 8])[:, :, bass.ts(j % 8, P)])
                elif name == "mix":
                    for j, (_, _, c0, m) in enumerate(MIX_TILES):
                        load(0, n0 + j, mix_w[:, :, c0:c0 + m], cols=m)
                elif name in ("mixout", "memq", "memo"):
                    w = square({"mixout": "w_mix_out", "memq": "w_mem_q", "memo": "w_mem_o"}[name])
                    for j in range(8):
                        load(0, n0 + j, w[:, :, bass.ts(j, P)])
                elif name == "ffn":
                    k = st["which"] - 1
                    n = n0
                    for f0, nf in FFN_PARTS:
                        with sp.Fori(0, nf // 2) as i:
                            for j in range(4):
                                w = (gate_w, up_w)[j % 2][k]
                                load(i, n + j, w[:, :, bass.ts(i * 2 + (f0 + j // 2), P)])
                        n += 2 * nf
                        with sp.Fori(0, KD // 4) as i:
                            for j in range(4):
                                load(i, n + j,
                                     down_w[k][:, f0:f0 + nf, bass.ts(i * 4 + j, P)], nk=nf)
                        n += KD

        @block.tensor
        def _(pe):
            def begin(s):
                if s:
                    pe.wait_ge(act_end, s)
                    pe.wait_ge(dve_end, s)
                    pe.wait_ge(pool_end, s)

            def linear(g, i, n, nk, hi, lo, m=P):
                w, slot = n % RING, n % 2
                pe.wait_ge(lo_split, i * 4 + (n + 1))
                pe.wait_ge(product_read[slot], half(i, n))
                last = None
                for c in range(nk):
                    for wt, x in ((WH, hi), (WH, lo), (WL, hi)):
                        for a in range(g.parts):
                            last = pe.matmul(LIN[0:m, slot, a, 0:g.width], wt[:, w, c, 0:m],
                                             x[:, c, a * g.width:(a + 1) * g.width],
                                             start=(c == 0 and wt is WH and x is hi),
                                             stop=(c == nk - 1 and wt is WL))
                last.then_inc(product, 1)

            def to_feature(b, rows, slot):
                if b >= 1:
                    pe.wait_ge(back_lo, b)
                for d in range(KD):
                    last = pe.transpose(TR[:, 1, d * P:d * P + rows], XT[0:rows, slot, d * P:(d + 1) * P],
                                        ident[0:rows, 0:rows])
                last.then_inc(back_done, 1)

            base = dict(idx=0, tok=0)
            for s, st in enumerate(STAGES):
                begin(s)
                name, g, n0 = st["name"], st["g"], st["n"]
                if name == "memload":
                    pe.wait_ge(consts, 3)
                if name in ("memload", "loadx"):
                    tiles = [(0, P), (P, P)] if name == "memload" else g.tiles
                    for t, (col, rows) in enumerate(tiles):
                        b = st["back"] + t
                        pe.wait_ge(xt_loaded[t % 2], 16 * (st[f"load{t % 2}"] + t // 2 + 1))
                        to_feature(b, rows, t % 2)
                elif name == "memkv":
                    for j in range(16):
                        pe.wait_ge(lo_split, j + 1)
                        if j >= 2:
                            pe.wait_ge(product_read[j % 2], j // 2)
                        for mt in range(2):
                            for c in range(KD):
                                for x, wt in ((XH, WH), (XH, WL), (XL, WH)):
                                    last = pe.matmul(LIN[:, j % 2, mt, 0:P], x[:, c, mt * P:(mt + 1) * P],
                                                     wt[:, j % RING, c, :], start=(c == 0 and x is XH and wt is WH),
                                                     stop=(c == KD - 1 and x is XL))
                        last.then_inc(product, 1)
                    pe.wait_ge(product_read[1], 8)
                    pe.wait_ge(product_read[0], 8)
                    for h in range(2):
                        for q in range(8):
                            last = pe.transpose(TR[:, h, q * P:(q + 1) * P],
                                                MKTOK[:, q % 2, (4 * h + q // 2) * P:(4 * h + q // 2 + 1) * P], ident[:, :])
                        last.then_inc(pt_done, 1)
                    pe.wait_ge(ck_loaded, 32)
                    pe.wait_ge(pt_read, 2)
                    for q in range(4):
                        pe.transpose(TR[:, 0, q * P:(q + 1) * P], CK[:, q, 0:P], ident[:, :])
                        last = pe.transpose(TR[0:64, 1, q * P:(q + 1) * P], CK[:, q, P:P + 64], ident[:, :])
                    last.then_inc(pt_done, 1)
                elif name == "ffn":
                    n = n0
                    for f0, nf in FFN_PARTS:
                        with pe.Fori(0, nf // 2) as i:
                            for j in range(4):
                                linear(g, i, n + j, KD, XH, XL)
                        n += 2 * nf
                        pe.wait_ge(hidden_lo, st["mult"] + f0 + nf)
                        with pe.Fori(0, KD // 4) as i:
                            for j in range(4):
                                linear(g, i, n + j, nf, HH, HL)
                        n += KD
                elif name == "ln":
                    k = len(g.tiles)
                    for t in range(k + 1):
                        if t < k:
                            col, rows = g.tiles[t]
                            if st["fwd"] + t >= 1:
                                pe.wait_ge(fwd_read, st["fwd"] + t)
                            for d in range(KD):
                                last = pe.transpose(TR[0:rows, 0, d * P:(d + 1) * P], Y[:, d, col:col + rows], ident[:, :])
                            last.then_inc(fwd_done, 1)
                        if t >= 1 and st["which"] != 4:
                            pe.wait_ge(xt_ready, st["fwd"] + t)
                            to_feature(st["back"] + t - 1, g.tiles[t - 1][1], (t - 1) % 2)
                elif name == "mix":
                    for j, (kind, i, _, m) in enumerate(MIX_TILES):
                        linear(g, 0, n0 + j, KD, XH, XL, m)
                        if j == 10:
                            pe.wait_ge(product_read[(n0 + 1) % 2], (n0 + 1) // 2 + 1)
                            pe.wait_ge(product_read[n0 % 2], (n0 + 2) // 2 + 1)
                            for t, (col, rows) in enumerate(g.tiles):
                                k = base["tok"]
                                if k >= 1:
                                    pe.wait_ge(tok_read, k)
                                pe.transpose(TR[0:rows, 0, 0:P], KVT[:, 1, col:col + rows], ident[:, :])
                                pe.transpose(TR[0:rows, 0, P:2 * P], KVT[:, 2, col:col + rows], ident[:, :])
                                pe.transpose(TR[0:rows, 0, 2 * P:2 * P + KIW], KVT[0:KIW, 0, col:col + rows],
                                             ident[0:KIW, 0:KIW]).then_inc(tok_done, 1)
                                base["tok"] += 1
                elif name == "idx":
                    for t, rows, keys, _ in score_tiles(g):
                        kmat = KIS if rows == DEC else KIP
                        for k0 in range(0, keys, 512):
                            w = min(512, keys - k0)
                            for h in range(HEADS):
                                k = base["idx"]
                                if k >= 4:
                                    pe.wait_ge(relu_done, k - 3)
                                lo = 64 * (h % 2)
                                pe.matmul(LIN[0:rows, (k % 4) // 2, k % 2, 0:w],
                                          QX[lo:lo + 64, 4 + h // 2, g.tiles[t][0]:g.tiles[t][0] + rows],
                                          kmat[lo:lo + 64, k0:k0 + w], start=True, stop=True).then_inc(idx_done, 1)
                                base["idx"] += 1
                elif name == "att":
                    s0, pt0, o0 = st["s"], st["pt"], st["o"]
                    jobs = att_jobs(g)

                    def scores(a):
                        t, col, rows, keys, kvg, hh = jobs[a]
                        h, lo = 4 * kvg + hh, 64 * (hh % 2)
                        if a >= 2:
                            pe.wait_ge(nm_ready, s0 + a - 1)
                        same = (kvg == 0) == (lo == 0)
                        kmat = (KSA if same else KSB) if rows == DEC else (KPA if same else KPB)
                        for k0 in range(0, keys, 512):
                            w = min(512, keys - k0)
                            last = pe.matmul(LIN[0:rows, a % 2, k0 // 512, 0:w],
                                             QA[lo:lo + 64, h // 2, col:col + rows],
                                             kmat[lo:lo + 64, k0:k0 + w], start=True, stop=True)
                        last.then_inc(s_done, 1)

                    def turn(a):
                        t, col, rows, keys, kvg, hh = jobs[a]
                        pe.wait_ge(p_ready, s0 + a + 1)
                        pe.wait_ge(pt_read, pt0 + a)
                        for kb in range(0, keys, P):
                            w = min(P, keys - kb)
                            last = pe.transpose(TR[0:w, 0, kb:kb + rows],
                                                PR[0:rows, a % 2, kb:kb + w], ident[0:rows, 0:rows])
                        last.then_inc(pt_done, 1)

                    def values(q):
                        t, col, rows, keys, kvg, _ = jobs[4 * q]
                        pe.wait_ge(pt_read, pt0 + 4 * q + 4)
                        if q >= 2:
                            pe.wait_ge(o_lo, o0 + q - 1)
                        vmat = VS if rows == DEC else VP
                        nb = (keys + P - 1) // P
                        for kb in range(nb):
                            w = min(P, keys - kb * P)
                            for odd in range(2):
                                last = pe.matmul(TR[64 * odd:64 * odd + 64, 1, 512 * (q % 2):512 * (q % 2) + 2 * rows]
                                                 .rearrange("p (a b) -> p a b", a=2),
                                                 vmat[0:w, kb, 64 * kvg:64 * kvg + 64],
                                                 PT[0:w, kb, 2 * odd:2 * odd + 2, 0:rows],
                                                 start=(kb == 0), stop=(kb == nb - 1))
                        last.then_inc(o_done, 1)

                    scores(0)
                    for a in range(len(jobs)):
                        if a + 1 < len(jobs):
                            scores(a + 1)
                        if a % 4 == 0 and a:
                            values(a // 4 - 1)
                        turn(a)
                    values(len(jobs) // 4 - 1)
                elif name in ("mixout", "memq", "memo"):
                    src = (HH, HL) if name == "mixout" else (XH, XL)
                    for j in range(8):
                        linear(g, 0, n0 + j, KD, *src)
                elif name == "mematt":
                    c = dict(s=st["s"], nm=st["s"], exp=st["s"], p=st["s"], pt=st["pt"], o=st["o"])
                    for t in range(5):
                        if t < 4:
                            if t >= 2:
                                pe.wait_ge(exp_done, c["exp"] + t - 1)
                            for h in range(4):
                                for e in range(2):
                                    last = pe.matmul(LIN[:, t % 2, h // 2, 256 * (h % 2):256 * (h % 2) + 256],
                                                     QM[:, 2 * h + e, t * P:(t + 1) * P], MKT[:, 2 * h + e, :],
                                                     start=(e == 0), stop=(e == 1))
                            last.then_inc(s_done, 1)
                        if t >= 1:
                            u = t - 1
                            pe.wait_ge(p_ready, c["p"] + u + 1)
                            if u >= 2:
                                pe.wait_ge(pt_read, c["pt"] + u - 1)
                            for q in range(8):
                                last = pe.transpose(TR[:, u % 2, q * P:(q + 1) * P],
                                                    PM[:, u % 2, q % 4, (q // 4) * P:(q // 4 + 1) * P], ident[:, :])
                            last.then_inc(pt_done, 1)
                    pe.wait_ge(pt_read, c["pt"] + 4)
                    for o in range(8):
                        if o >= 2:
                            pe.wait_ge(o_lo, c["o"] + o - 1)
                        else:
                            pe.wait_ge(exp_done, c["exp"] + 4)
                        for mb in range(2):
                            last = pe.matmul(LIN[:, o % 2, 0, :], MV[:, mb, o * P:(o + 1) * P],
                                             PTM[:, mb, o // 2, 0:HALF], start=(mb == 0), stop=(mb == 1))
                        last.then_inc(o_done, 1)
                    if g.sample:
                        for h in range(4):
                            pe.wait_ge(head_loaded, 32 * (h + 1))
                            pe.wait_ge(pt_read, c["pt"] + 4 + 2 * h)
                            for q in range(4):
                                last = pe.transpose(TR[:, 0, q * P:(q + 1) * P],
                                                    MKS[:, q % 2, (q // 2) * P:(q // 2 + 1) * P], ident[:, :])
                            last.then_inc(pt_done, 1)
                            pe.wait_ge(pt_read, c["pt"] + 5 + 2 * h)
                            pe.wait_ge(o_lo, c["o"] + 8 + h)
                            for e in range(2):
                                last = pe.matmul(LIN[0:DEC, 0, 0, 0:256], QM[:, 2 * h + e, HALF:HALF + DEC],
                                                 MKTS[:, e, :], start=(e == 0), stop=(e == 1))
                            last.then_inc(s_done, 1)
                            pe.wait_ge(p_ready, c["p"] + 5 + h)
                            for mb in range(2):
                                last = pe.transpose(TR[:, 1, mb * P:mb * P + DEC], PM[0:DEC, 0, h, mb * P:(mb + 1) * P],
                                                    ident[0:DEC, 0:DEC])
                            last.then_inc(pt_done, 1)
                            pe.wait_ge(pt_read, c["pt"] + 6 + 2 * h)
                            for e in range(2):
                                for mb in range(2):
                                    last = pe.matmul(LIN[:, 1, e, 0:DEC], MVS[:, mb, e * P:(e + 1) * P],
                                                     PTM[:, mb, h, HALF:HALF + DEC], start=(mb == 0), stop=(mb == 1))
                            last.then_inc(o_done, 1)
                pe.drain().then_inc(pe_end, 1)

        @block.scalar
        def _(act):
            moves = [0]

            def begin(s):
                if s:
                    act.wait_ge(pe_end, s)
                    act.wait_ge(dve_end, s)
                    act.wait_ge(pool_end, s)

            def move(dst, src):
                act.dma_start(dst, src).then_inc(moved, 16)
                moves[0] += 16

            def all_moved():
                act.wait_ge(moved, moves[0])

            def split_hi(i, n):
                if n >= NT:
                    return
                act.wait_ge(raw_loaded[n % 2], half(i, n) * 16 + 16)
                if n >= RING:
                    act.wait_ge(product, i * 4 + (n - RING + 1))
                act.activation(WH[:, n % RING, :, :], WRAW[:, n % 2, :, :], ACT.Copy).then_inc(hi_split, 1)

            def evac(g, i, n, dst, m=P, func=ACT.Copy, scale=1.0):
                act.wait_ge(product, i * 4 + (n + 1))
                return act.activation(g.folded(dst), LIN[0:m, n % 2, 0:g.parts, 0:g.width], func, scale=scale)

            def from_feature(b, col, rows):
                act.wait_ge(back_done, b + 1)
                src = TR[:, 1, :].rearrange("p (d t) -> p d t", d=KD)[:, :, 0:rows]
                act.activation(XH[:, :, col:col + rows], src, ACT.Copy)
                act.activation(Y[:, :, col:col + rows], src, ACT.Copy, scale=ALPHA).then_inc(back_hi, 1)

            def load_ln(which):
                for r, nm in enumerate(("g", "b")):
                    move(GB[:, r, :], ins[f"ln{which}_{nm}"][0:1, :].to_broadcast([P, D]))

            base = dict(idx=0, tok=0)
            for s, st in enumerate(STAGES):
                begin(s)
                name, g, n0, which = st["name"], st["g"], st["n"], st["which"]
                if name in ("memload", "loadx"):
                    if name == "memload":
                        tiles = [(0, P, ins["mem_prompt"][0, t * P:(t + 1) * P, :]) for t in range(2)]
                        tiles = [(t * P, P, src) for t, (_, _, src) in enumerate(tiles)]
                    else:
                        tiles = [(col, rows, x_tok[1] if rows == DEC else
                                  x_tok[0][g.index * HALF + col:g.index * HALF + col + rows, :])
                                 for col, rows in g.tiles]

                    def load_tile(t):
                        col, rows, src = tiles[t]
                        act.dma_start(XT[0:rows, t % 2, :], src).then_inc(xt_loaded[t % 2], 16)

                    load_tile(0)
                    load_tile(1)
                    if name == "memload":
                        for i in range(4):
                            act.dma_start(VS[:, i, :], ins["cache_v"][0, 0, i * P:(i + 1) * P].rearrange("p h d -> p (h d)"))\
                                .then_inc(moved, 16)
                            moves[0] += 16
                        with nc.allow_non_contiguous_dma("small constants"):
                            for i in range(KC):
                                move(CW[:, :, i], ins["conv_w"][0, :, i * P:(i + 1) * P].rearrange("j p -> p j"))
                                move(CPREV[:, i, :], ins["cache_conv"][0, 0, :, i * P:(i + 1) * P].rearrange("r p -> p r"))
                    for t, (col, rows, _) in enumerate(tiles):
                        b = st["back"] + t
                        from_feature(b, col, rows)
                        if t + 2 < len(tiles):
                            load_tile(t + 2)
                    if name == "memload":
                        for j in range(AHEAD):
                            split_hi(0, j)
                        all_moved()
                elif name == "memkv":
                    act.dma_start(CK[:, :, 0:P], ins["cache_k"][0, 0].rearrange("(q p) h d -> p q (h d)", p=P)).then_inc(ck_loaded, 16)
                    act.dma_start(CK[:, :, P:P + 64], ins["cache_idx_k"][0, 0].rearrange("(q p) d -> p q d", p=P)).then_inc(ck_loaded, 16)
                    for j in range(16):
                        split_hi(0, j + AHEAD)
                        act.wait_ge(product, j + 1)
                        dst = (MKTOK if j < 8 else MV)[:, :, (j % 8) * P:(j % 8 + 1) * P]
                        act.activation(dst, LIN[:, j % 2, :, 0:P], ACT.Copy).then_inc(product_read[j % 2], 1)
                    act.wait_ge(product_read[0], 8)
                    act.wait_ge(product_read[1], 8)
                    for buf, out in ((MKTOK, outs["mem_k"]), (MV, outs["mem_v"])):
                        move(out[0, 0].rearrange("(b p) h d -> p b (h d)", p=P), buf[:, :, :])
                    for h in range(2):
                        act.wait_ge(pt_done, h + 1)
                        act.activation(MKT[:, 4 * h:4 * h + 4, :], TR[:, h, :].rearrange("p (a b) -> p a b", a=4),
                                       ACT.Copy).then_inc(pt_read, 1)
                    act.wait_ge(pt_done, 3)
                    act.activation(KSA[:, 0:PAST], TR[:, 0, 0:PAST], ACT.Copy)
                    act.activation(KIS[0:64, 0:PAST], TR[0:64, 1, 0:PAST], ACT.Copy).then_inc(pt_read, 1)
                    act.wait_ge(pt_read, 3)
                    move(KSB[0:64, 0:PAST], KSA[64:128, 0:PAST])
                    move(KSB[64:128, 0:PAST], KSA[0:64, 0:PAST])
                    move(KIS[64:128, 0:PAST], KIS[0:64, 0:PAST])
                    all_moved()
                elif name == "ffn":
                    load_ln(1 if which == 1 else 4)
                    n = n0
                    for part, (f0, nf) in enumerate(FFN_PARTS):
                        halves = st["half"] + KD * part
                        if halves:
                            act.wait_ge(added, halves)

                        with act.Fori(0, nf // 2) as i:
                            for j in range(4):
                                split_hi(i, n + j + AHEAD)
                                evac(g, i, n + j, FG[:, j % 2, 0:g.cols], func=ACT.Copy if j % 2 else ACT.Silu)\
                                    .then_inc(product_read[(n + j) % 2], 1)
                                if j % 2:
                                    act.wait_ge(multiplied, i * 2 + (st["mult"] + f0 + j // 2 + 1))
                                    act.activation(HH[:, bass.ds(i * 2 + j // 2, 1), 0:g.cols].rearrange("p a b -> p (a b)"),
                                                   FP_[:, 0:g.cols], ACT.Copy).then_inc(hidden_hi, 1)
                        n += 2 * nf

                        def down(i, n, halves):
                            for j in range(4):
                                split_hi(i, n + j + AHEAD)
                                if halves + j >= 2:
                                    act.wait_ge(added, i * 4 + (halves + j - 1))
                                evac(g, i, n + j, FG[:, j % 2, 0:g.cols], scale=0.5)\
                                    .then_inc(product_read[(n + j) % 2], 1)

                        if halves == 0 or n + KD + AHEAD > NT:
                            for k in range(KD // 4):
                                down(0, n + 4 * k, halves + 4 * k)
                        else:
                            with act.Fori(0, KD // 4) as i:
                                down(i, n, halves)
                        n += KD
                    all_moved()
                elif name == "ln":
                    if which != 4:
                        for t, (col, rows) in enumerate(g.tiles):
                            from_feature(st["back"] + t, col, rows)
                    else:
                        for t, (col, rows) in enumerate(g.tiles):
                            k = st["fwd"] + t
                            act.wait_ge(xt_ready, k + 1)
                            dst = outs["y_sample"][0] if rows == DEC else \
                                outs["y_prompt"][0, g.index * HALF + col:g.index * HALF + col + rows, :]
                            act.dma_start(dst, XT[0:rows, t % 2, :]).then_inc(xt_stored[t % 2], 16)
                        for k2 in range(2):
                            act.wait_ge(xt_stored[k2], 16 * (st[f"store{k2}"] + (len(g.tiles) + 1 - k2) // 2))
                elif name == "mix":
                    c0 = g.index * HALF
                    for j, (kind, i, _, m) in enumerate(MIX_TILES):
                        n = n0 + j
                        split_hi(0, n + AHEAD)
                        if kind in ("kiw", "k", "v"):
                            evac(g, 0, n, KVT[0:m, j, 0:g.cols], m).then_inc(product_read[n % 2], 1)
                            act.wait_ge(product_read[n % 2], n // 2 + 1)
                            if kind == "kiw":
                                for b in (0, 64):
                                    move(KIP[b:b + 64, c0:c0 + HALF], KVT[0:64, 0, 0:HALF])
                                    if g.sample:
                                        move(KIS[b:b + 64, PAST:SKEYS], KVT[0:64, 0, HALF:])
                            if kind == "k":
                                move(KPA[:, c0:c0 + HALF], KVT[:, 1, 0:HALF])
                                for b in (0, 64):
                                    move(KPB[b:b + 64, c0:c0 + HALF], KVT[64 - b:128 - b, 1, 0:HALF])
                                    if g.sample:
                                        move(KSB[b:b + 64, PAST:SKEYS], KVT[64 - b:128 - b, 1, HALF:])
                                if g.sample:
                                    move(KSA[:, PAST:SKEYS], KVT[:, 1, HALF:])
                        elif kind == "qi":
                            evac(g, 0, n, QX[:, 4 + i, 0:g.cols]).then_inc(product_read[n % 2], 1)
                        elif kind == "q":
                            evac(g, 0, n, QX[:, i, 0:g.cols]).then_inc(product_read[n % 2], 1)
                        elif kind == "h":
                            q = KC * g.index + i
                            if q >= 1:
                                act.wait_ge(yc_lo, q)
                            evac(g, 0, n, HB[:, 0:g.cols]).then_inc(product_read[n % 2], 1)
                        elif kind == "b":
                            q = KC * g.index + i
                            act.wait_ge(product_read[n % 2], n // 2 + 1)
                            act.activation(YCH[:, i, 0:g.cols], HB[:, 0:g.cols], ACT.Copy).then_inc(yc_hi, 1)
                        if j == 10:
                            for t, (col, rows) in enumerate(g.tiles):
                                k = base["tok"]
                                act.wait_ge(tok_done, k + 1)
                                if k >= 2:
                                    act.wait_ge(tok_stored[k % 2], 48 * (k // 2))
                                act.activation(TOK[0:rows, k % 2, :], TR[0:rows, 0, 0:328], ACT.Copy)
                                v = VS[0:rows, 4, :] if rows == DEC else VP[:, 4 * g.index + t, :]
                                act.activation(v, TR[0:rows, 0, P:2 * P], ACT.Copy)
                                act.activation(WI[0:rows, t, :], TR[0:rows, 0, 320:328], ACT.Copy, scale=WI_SCALE)\
                                    .then_inc(tok_read, 1)
                                act.wait_ge(tok_read, k + 1)
                                sfx = "sample" if rows == DEC else "prompt"
                                r0 = 0 if rows == DEC else c0 + col
                                act.dma_start(outs[f"k_{sfx}"][0, 0, r0:r0 + rows].rearrange("t h d -> t (h d)"),
                                              TOK[0:rows, k % 2, 0:P]).then_inc(tok_stored[k % 2], 16)
                                act.dma_start(outs[f"v_{sfx}"][0, 0, r0:r0 + rows].rearrange("t h d -> t (h d)"),
                                              TOK[0:rows, k % 2, P:2 * P]).then_inc(tok_stored[k % 2], 16)
                                act.dma_start(outs[f"ik_{sfx}"][0, 0, r0:r0 + rows],
                                              TOK[0:rows, k % 2, 2 * P:2 * P + 64]).then_inc(tok_stored[k % 2], 16)
                                base["tok"] += 1
                    k = base["tok"]
                    act.wait_ge(tok_stored[0], 48 * ((k + 1) // 2))
                    act.wait_ge(tok_stored[1], 48 * (k // 2))
                    all_moved()
                elif name == "idx":
                    for t, rows, keys, _ in score_tiles(g):
                        for k0 in range(0, keys, 512):
                            w = min(512, keys - k0)
                            for h in range(HEADS):
                                k = base["idx"]
                                act.wait_ge(idx_done, k + 1)
                                if k >= 4:
                                    act.wait_ge(idx_added, k - 3)
                                act.activation(RB[0:rows, k % 4, 0:w], LIN[0:rows, (k % 4) // 2, k % 2, 0:w],
                                               ACT.Relu).then_inc(relu_done, 1)
                                base["idx"] += 1
                elif name == "spill":
                    move(spill_q[g.index][:, :, 0:g.cols], QX[:, 0:KC, 0:g.cols])
                    move(spill_y[g.index][:, :, 0:g.cols], Y[:, :, 0:g.cols])
                    move(spill_ch[g.index][:, :, 0:g.cols], YCH[:, :, 0:g.cols].bitcast(F32))
                    move(spill_cl[g.index][:, :, 0:g.cols], YCL[:, :, 0:g.cols].bitcast(F32))
                    with nc.allow_non_contiguous_dma("two rows of the conv input"):
                        for i in range(KC):
                            if g.sample:
                                move(outs["conv_sample"][0, 0, :, i * P:(i + 1) * P].rearrange("r p -> p r"), TAILS[:, i, :])
                            else:
                                move(outs["conv_prompt"][0, 0, :, i * P:(i + 1) * P].rearrange("r p -> p r"), TAILP[:, i, :])
                    all_moved()
                elif name == "reload":
                    move(QA[:, :, 0:g.cols], spill_q[g.index][:, :, 0:g.cols])
                    move(Y[:, :, 0:g.cols], spill_y[g.index][:, :, 0:g.cols])
                    move(HH[:, 0:KC, 0:g.cols].bitcast(F32), spill_ch[g.index][:, :, 0:g.cols])
                    move(HL[:, 0:KC, 0:g.cols].bitcast(F32), spill_cl[g.index][:, :, 0:g.cols])
                    all_moved()
                elif name == "att":
                    s0, pt0, o0 = st["s"], st["pt"], st["o"]
                    jobs = att_jobs(g)

                    def exponent(a):
                        t, col, rows, keys, kvg, hh = jobs[a]
                        q = a % 2
                        act.wait_ge(nm_ready, s0 + a + 1)
                        act.activation(PR[0:rows, q, 0:keys], PR[0:rows, q, 0:keys], ACT.Exp, bias=NM[0:rows, q, 0:1],
                                       scale=ATT_SCALE, accum_out=RS[0:rows, q, 0:1]).then_inc(exp_done, 1)

                    def out_hi(q):
                        t, col, rows, keys, kvg, _ = jobs[4 * q]
                        act.wait_ge(o_done, o0 + q + 1)
                        o = TR[:, 1, 512 * (q % 2):512 * (q % 2) + 2 * rows].rearrange("p (a b) -> p a b", a=2)
                        act.activation(HH[:, 4 + 2 * kvg:6 + 2 * kvg, col:col + rows], o, ACT.Copy).then_inc(o_hi, 1)

                    exponent(0)
                    for a in range(len(jobs)):
                        if a + 1 < len(jobs):
                            exponent(a + 1)
                        if a % 4 == 0 and a:
                            out_hi(a // 4 - 1)
                        t, col, rows, keys, kvg, hh = jobs[a]
                        act.wait_ge(pt_done, pt0 + a + 1)
                        slot = (0, 2, 1, 3)[hh]
                        full = keys // P
                        src = TR[:, 0, :].rearrange("p (k q) -> p k q", k=8)
                        last = act.activation(PT[:, 0:full, slot, 0:rows], src[:, 0:full, 0:rows], ACT.Copy)
                        if keys % P:
                            last = act.activation(PT[0:keys % P, full, slot, 0:rows], src[0:keys % P, full, 0:rows], ACT.Copy)
                        last.then_inc(pt_read, 1)
                    out_hi(len(jobs) // 4 - 1)
                elif name in ("mixout", "memo"):
                    load_ln(2 if name == "mixout" else 3)
                    for j in range(8):
                        split_hi(0, n0 + j + AHEAD)
                    all_moved()
                elif name == "memq":
                    for j in range(8):
                        n = n0 + j
                        split_hi(0, n + AHEAD)
                        evac(g, 0, n, QM[:, j, 0:g.cols]).then_inc(product_read[n % 2], 1)
                elif name == "mematt":
                    c = dict(s=st["s"], nm=st["s"], exp=st["s"], p=st["s"], pt=st["pt"], o=st["o"])

                    def load_head(h):
                        for buf, src in ((MKS, "cache_mem_k"), (MVS, "cache_mem_v")):
                            act.dma_start(buf[:, :, :], ins[src][0, 0, :, h, :].rearrange("(b p) d -> p b d", p=P))\
                                .then_inc(head_loaded, 16)

                    if g.sample:
                        load_head(0)
                    for t in range(5):
                        if t < 4:
                            act.wait_ge(nm_ready, c["nm"] + t + 1)
                            for h in range(4):
                                last = act.activation(PM[:, t % 2, h, :], LIN[:, t % 2, h // 2, 256 * (h % 2):256 * (h % 2) + 256],
                                                      ACT.Exp, bias=NM[:, t % 2, h:h + 1], scale=MEM_SCALE,
                                                      accum_out=RS[:, t % 2, h:h + 1])
                            last.then_inc(exp_done, 1)
                        if t >= 1:
                            u = t - 1
                            act.wait_ge(pt_done, c["pt"] + u + 1)
                            act.activation(PTM[:, :, :, u * P:(u + 1) * P].rearrange("p a b q -> p (a b) q"),
                                           TR[:, u % 2, :].rearrange("p (k q) -> p k q", k=8), ACT.Copy).then_inc(pt_read, 1)
                    for o in range(8):
                        act.wait_ge(o_done, c["o"] + o + 1)
                        act.activation(XH[:, o, 0:HALF], LIN[:, o % 2, 0, :], ACT.Copy).then_inc(o_hi, 1)
                    if g.sample:
                        for h in range(4):
                            act.wait_ge(pt_done, c["pt"] + 5 + 2 * h)
                            act.activation(MKTS[:, :, :].rearrange("p a b -> p (a b)"), TR[:, 0, 0:512], ACT.Copy).then_inc(pt_read, 1)
                            act.wait_ge(nm_ready, c["nm"] + 5 + h)
                            act.activation(PM[0:DEC, 0, h, :], LIN[0:DEC, 0, 0, 0:256], ACT.Exp, bias=NM[0:DEC, 0, h:h + 1],
                                           scale=MEM_SCALE, accum_out=RS[0:DEC, 0, h:h + 1]).then_inc(exp_done, 1)
                            act.wait_ge(pt_done, c["pt"] + 6 + 2 * h)
                            act.activation(PTM[:, :, h, HALF:HALF + DEC],
                                           TR[:, 1, 0:256].rearrange("p (k q) -> p k q", k=2)[:, :, 0:DEC], ACT.Copy)\
                                .then_inc(pt_read, 1)
                            act.wait_ge(o_done, c["o"] + 9 + h)
                            act.activation(XH[:, 2 * h:2 * h + 2, HALF:HALF + DEC], LIN[:, 1, :, 0:DEC], ACT.Copy).then_inc(o_hi, 1)
                            if h < 3:
                                load_head(h + 1)
                act.drain().then_inc(act_end, 1)

        @block.vector
        def _(dve):
            steps = [0]

            def begin(s):
                if s:
                    dve.wait_ge(pe_end, s)
                    dve.wait_ge(act_end, s)
                    dve.wait_ge(pool_end, s)

            def link(ins_):
                steps[0] += 1
                ins_.then_inc(dve_step, 1)
                dve.wait_ge(dve_step, steps[0])

            def low(b, col, rows):
                dve.wait_ge(back_hi, b + 1)
                src = TR[:, 1, :].rearrange("p (d t) -> p d t", d=KD)[:, :, 0:rows]
                dve.tensor_tensor(XL[:, :, col:col + rows], src, XH[:, :, col:col + rows].bitcast(F32), ALU.subtract)\
                    .then_inc(back_lo, 1)

            def select(g):
                for t, rows, keys, rounds in score_tiles(g):
                    at_ = SCORE_AT[(g.index, t)]
                    sc = SC[0:rows, at_:at_ + keys]
                    with dve.Fori(0, rounds):
                        dve.max(M8[0:rows, :], sc)
                        dve.drain()
                        dve.match_replace(sc, M8[0:rows, :], sc, TAKEN)
                        dve.drain()
                    dve.tensor_scalar(sc, sc, CUT, FAR, ALU.is_gt, ALU.mult)

            base = dict(idx=0)
            for s, st in enumerate(STAGES):
                begin(s)
                name, g, n0, which = st["name"], st["g"], st["n"], st["which"]
                if name == "memload":
                    for t in range(2):
                        low(st["back"] + t, t * P, P)
                elif name == "loadx":
                    for t, (col, rows) in enumerate(g.tiles):
                        low(st["back"] + t, col, rows)
                elif name == "ffn":
                    if which == 1 and g.index == 1:
                        select(GROUPS[0])
                    if which == 2 and g.index == 0:
                        select(GROUPS[1])
                elif name == "ln":
                    for t, (col, rows) in enumerate(g.tiles):
                        k = st["fwd"] + t
                        q = t % 2
                        dve.wait_ge(fwd_done, k + 1)
                        for h in range(2):
                            last = dve.bn_stats(ST[0:rows, q, 6 * h:6 * h + 6], TR[0:rows, 0, 512 * h:512 * h + 512])
                        link(last)
                        link(dve.bn_aggr(MVAR[0:rows, q, :], ST[0:rows, q, :]))
                        dve.tensor_scalar(VE[0:rows, q:q + 1], MVAR[0:rows, q, 1:2], EPS, None, ALU.add).then_inc(var_ready, 1)
                        if which == 4 and t >= 2:
                            dve.wait_ge(xt_stored[q], 16 * (st[f"store{q}"] + t // 2))
                        elif which != 4 and t >= 2:
                            dve.wait_ge(back_done, st["back"] + t - 1)
                        dve.scalar_tensor_tensor(XT[0:rows, q, :], TR[0:rows, 0, :], MVAR[0:rows, q, 0:1], GB[0:rows, 0, :],
                                                 ALU.subtract, ALU.mult).then_inc(fwd_read, 1)
                        dve.wait_ge(fwd_read, k + 1)
                        dve.wait_ge(rstd_ready, k + 1)
                        dve.scalar_tensor_tensor(XT[0:rows, q, :], XT[0:rows, q, :], RSTD[0:rows, q:q + 1], GB[0:rows, 1, :],
                                                 ALU.mult, ALU.add).then_inc(xt_ready, 1)
                        if which != 4 and t >= 1:
                            low(st["back"] + t - 1, *g.tiles[t - 1])
                    if which != 4:
                        low(st["back"] + len(g.tiles) - 1, *g.tiles[-1])
                elif name == "mix":
                    if g.sample:
                        link(dve.memset(UB[:, 0:2], 0.0))
                    for j, (kind, i, _, m) in enumerate(MIX_TILES):
                        n = n0 + j
                        q = KC * g.index + i
                        ps = LIN[:, n % 2, :, :]
                        if kind == "c":
                            if g.sample:
                                if i:
                                    link(dve.memset(UB[:, 0:2], 0.0))
                                link(dve.tensor_copy(UB[:, 514:516], CPREV[:, i, :]))
                            else:
                                link(dve.tensor_copy(UB[:, 0:2], TAILP[:, i, :]))
                            dve.wait_ge(product, n + 1)
                            dve.wait_ge(product_read[(n - 1) % 2], (n - 1) // 2 + 1)
                            if g.sample:
                                dve.tensor_tensor(UB[:, 2:274], ps[:, 0, 0:272], HB[:, 0:272], ALU.mult)
                                dve.tensor_tensor(UB[:, 274:514], ps[:, 1, 0:240], HB[:, 272:512], ALU.mult)
                                last = dve.tensor_tensor(UB[:, 516:548], ps[:, 1, 240:272], HB[:, 512:544], ALU.mult)
                                wc = 546
                            else:
                                last = dve.tensor_tensor(UB[:, 2:514], ps[:, 0, 0:512], HB[:, 0:512], ALU.mult)
                                wc = 512
                            last.then_inc(product_read[n % 2], 1)
                            dve.wait_ge(product_read[n % 2], n // 2 + 1)
                            if g.sample:
                                dve.tensor_copy(TAILS[:, i, :], UB[:, 546:548])
                            dve.tensor_copy(TAILP[:, i, :], UB[:, 512:514])
                            link(dve.tensor_scalar(CB[:, 0:wc], UB[:, 0:wc], CW[:, 0, i:i + 1], None, ALU.mult))
                            for tap in (1, 2):
                                link(dve.scalar_tensor_tensor(CB[:, 0:wc], UB[:, tap:tap + wc], CW[:, tap, i:i + 1],
                                                              CB[:, 0:wc], ALU.mult, ALU.add))
                        elif kind == "b":
                            dve.wait_ge(product, n + 1)
                            if g.sample:
                                dve.tensor_tensor(HB[:, 0:272], ps[:, 0, 0:272], CB[:, 0:272], ALU.mult)
                                dve.tensor_tensor(HB[:, 272:512], ps[:, 1, 0:240], CB[:, 272:512], ALU.mult)
                                last = dve.tensor_tensor(HB[:, 512:544], ps[:, 1, 240:272], CB[:, 514:546], ALU.mult)
                            else:
                                last = dve.tensor_tensor(HB[:, 0:512], ps[:, 0, 0:512], CB[:, 0:512], ALU.mult)
                            last.then_inc(product_read[n % 2], 1)
                            dve.wait_ge(yc_hi, q + 1)
                            dve.tensor_tensor(YCL[:, i, 0:g.cols], HB[:, 0:g.cols], YCH[:, i, 0:g.cols].bitcast(F32),
                                              ALU.subtract).then_inc(yc_lo, 1)
                elif name == "idx":
                    for t, rows, keys, _ in score_tiles(g):
                        at_ = SCORE_AT[(g.index, t)]
                        for k0 in range(0, keys, 512):
                            w = min(512, keys - k0)
                            sc = SC[0:rows, at_ + k0:at_ + k0 + w]
                            for h in range(HEADS):
                                k = base["idx"]
                                dve.wait_ge(relu_done, k + 1)
                                wt = WI[0:rows, t, h:h + 1]
                                if h == 0:
                                    ins_ = dve.tensor_scalar(sc, RB[0:rows, k % 4, 0:w], wt, None, ALU.mult)
                                else:
                                    dve.wait_ge(idx_added, k)
                                    ins_ = dve.scalar_tensor_tensor(sc, RB[0:rows, k % 4, 0:w], wt, sc, ALU.mult, ALU.add)
                                ins_.then_inc(idx_added, 1)
                                base["idx"] += 1
                        if rows == P:
                            dve.wait_ge(idx_added, base["idx"])
                            dve.memset(SC[0:CHUNK, at_ + keys - CHUNK:at_ + keys], CLOSED)
                elif name == "att":
                    s0, pt0, o0 = st["s"], st["pt"], st["o"]
                    jobs = att_jobs(g)

                    def peak(a):
                        t, col, rows, keys, kvg, hh = jobs[a]
                        q = a % 2
                        if (g.index, t) in SCORE_AT:
                            at_ = SCORE_AT[(g.index, t)]
                            mask = SC[0:rows, at_:at_ + keys]
                        else:
                            mask = DM[:, 256 - keys:256]
                        dve.wait_ge(s_done, s0 + a + 1)
                        if a >= 2:
                            dve.wait_ge(pt_done, pt0 + a - 1)
                        link(dve.tensor_tensor_reduce(
                            PR[0:rows, q, 0:keys], LIN[0:rows, q, :, :].rearrange("p a b -> p (a b)")[:, 0:keys], mask,
                            1.0, -3.0e38, ALU.add, ALU.max, MX[0:rows, q, 0:1]))
                        dve.tensor_scalar(NM[0:rows, q, 0:1], MX[0:rows, q, 0:1], -ATT_SCALE, None, ALU.mult).then_inc(nm_ready, 1)

                    def out_lo(q):
                        t, col, rows, keys, kvg, _ = jobs[4 * q]
                        dve.wait_ge(o_hi, o0 + q + 1)
                        o = TR[:, 1, 512 * (q % 2):512 * (q % 2) + 2 * rows].rearrange("p (a b) -> p a b", a=2)
                        dve.tensor_tensor(HL[:, 4 + 2 * kvg:6 + 2 * kvg, col:col + rows], o,
                                          HH[:, 4 + 2 * kvg:6 + 2 * kvg, col:col + rows].bitcast(F32), ALU.subtract)\
                            .then_inc(o_lo, 1)

                    peak(0)
                    for a in range(len(jobs)):
                        if a + 1 < len(jobs):
                            peak(a + 1)
                        t, col, rows, keys, kvg, hh = jobs[a]
                        q = a % 2
                        dve.wait_ge(exp_done, s0 + a + 1)
                        link(dve.reciprocal(RR[0:rows, q, 0:1], RS[0:rows, q, 0:1]))
                        dve.tensor_scalar(PR[0:rows, q, 0:keys], PR[0:rows, q, 0:keys], RR[0:rows, q, 0:1], None, ALU.mult)\
                            .then_inc(p_ready, 1)
                        if a % 4 == 0 and a:
                            out_lo(a // 4 - 1)
                    out_lo(len(jobs) // 4 - 1)
                elif name in ("mixout", "memo"):
                    for j in range(8):
                        n = n0 + j
                        dve.wait_ge(product, n + 1)
                        y = g.folded(Y[:, j, 0:g.cols])
                        dve.tensor_tensor(y, LIN[:, n % 2, 0:g.parts, 0:g.width], y, ALU.add).then_inc(product_read[n % 2], 1)
                elif name == "mematt":
                    c = dict(s=st["s"], nm=st["s"], exp=st["s"], p=st["s"], pt=st["pt"], o=st["o"])

                    def norm(rows, q, hs):
                        link(dve.reciprocal(RR[0:rows, q, hs:hs + 1] if hs is not None else RR[:, q, :],
                                            RS[0:rows, q, hs:hs + 1] if hs is not None else RS[:, q, :]))
                        for h in range(4) if hs is None else [hs]:
                            last = dve.tensor_scalar(PM[0:rows, q, h, :], PM[0:rows, q, h, :], RR[0:rows, q, h:h + 1], None, ALU.mult)
                        last.then_inc(p_ready, 1)

                    for t in range(5):
                        if t < 4:
                            dve.wait_ge(s_done, c["s"] + t + 1)
                            if t >= 2:
                                dve.wait_ge(exp_done, c["exp"] + t - 1)
                                dve.wait_ge(pt_done, c["pt"] + t - 1)
                            link(dve.tensor_reduce(MX[:, t % 2, :], LIN[:, t % 2, :, :].rearrange("p a (b c) -> p (a b) c", b=2),
                                                   AX_X, ALU.max))
                            dve.tensor_scalar(NM[:, t % 2, :], MX[:, t % 2, :], -MEM_SCALE, None, ALU.mult).then_inc(nm_ready, 1)
                        if t >= 1:
                            dve.wait_ge(exp_done, c["exp"] + t)
                            norm(P, (t - 1) % 2, None)
                    for o in range(8):
                        dve.wait_ge(o_hi, c["o"] + o + 1)
                        dve.tensor_tensor(XL[:, o, 0:HALF], LIN[:, o % 2, 0, :], XH[:, o, 0:HALF].bitcast(F32), ALU.subtract)\
                            .then_inc(o_lo, 1)
                    if g.sample:
                        for h in range(4):
                            dve.wait_ge(s_done, c["s"] + 5 + h)
                            link(dve.tensor_reduce(MX[0:DEC, 0, h:h + 1], LIN[0:DEC, 0, 0, 0:256], AX_X, ALU.max))
                            dve.tensor_scalar(NM[0:DEC, 0, h:h + 1], MX[0:DEC, 0, h:h + 1], -MEM_SCALE, None, ALU.mult).then_inc(nm_ready, 1)
                            dve.wait_ge(exp_done, c["exp"] + 5 + h)
                            norm(DEC, 0, h)
                            dve.wait_ge(o_hi, c["o"] + 9 + h)
                            dve.tensor_tensor(XL[:, 2 * h:2 * h + 2, HALF:HALF + DEC], LIN[:, 1, :, 0:DEC],
                                              XH[:, 2 * h:2 * h + 2, HALF:HALF + DEC].bitcast(F32), ALU.subtract).then_inc(o_lo, 1)
                dve.drain().then_inc(dve_end, 1)

        @block.gpsimd
        def _(pool):
            def begin(s):
                if s:
                    pool.wait_ge(pe_end, s)
                    pool.wait_ge(act_end, s)
                    pool.wait_ge(dve_end, s)

            def split_lo(i, n):
                if n >= NT:
                    return
                pool.wait_ge(hi_split, i * 4 + (n + 1))
                pool.tensor_tensor(WL[:, n % RING, :, :], WRAW[:, n % 2, :, :], WH[:, n % RING, :, :].bitcast(F32),
                                   ALU.subtract).then_inc(lo_split, 1)

            pool.memset(ident[:, :], 0.0).then_inc(consts, 1)
            pool.memset(DM[:, :], 0.0).then_inc(consts, 1)
            pool.wait_ge(consts, 2)
            pool.affine_select(out=ident[:, :], in_=ident[:, :], compare_op=ALU.not_equal, fill=1.0, base=0,
                               pattern=[[-1, P]], channel_multiplier=1).then_inc(consts, 1)
            pool.memset(DM[0:CHUNK, 256 - CHUNK:256], FAR).then_inc(masks, 1)
            pool.memset(MHALF[:, :], -0.5).then_inc(masks, 1)
            pool.wait_ge(masks, 2)
            for s, st in enumerate(STAGES):
                begin(s)
                name, g, n0, which = st["name"], st["g"], st["n"], st["which"]
                if name == "memload":
                    for j in range(AHEAD):
                        split_lo(0, j)
                elif name in ("memkv", "mix", "mixout", "memq", "memo"):
                    for j in range({"memkv": 16, "mix": len(MIX_TILES)}.get(name, 8)):
                        split_lo(0, n0 + j + AHEAD)
                elif name == "ffn":
                    n = n0
                    for part, (f0, nf) in enumerate(FFN_PARTS):
                        with pool.Fori(0, nf // 2) as i:
                            for f in range(2):
                                split_lo(i, n + 2 * f + AHEAD)
                                split_lo(i, n + 2 * f + 1 + AHEAD)
                                pool.wait_ge(product_read[(n + 1) % 2], half(i, n + 2 * f + 1) + 1)
                                pool.tensor_tensor(FP_[:, 0:g.cols], FG[:, 0, 0:g.cols], FG[:, 1, 0:g.cols], ALU.mult)\
                                    .then_inc(multiplied, 1)
                                pool.wait_ge(hidden_hi, i * 2 + (st["mult"] + f0 + f + 1))
                                pool.tensor_tensor(HL[:, bass.ds(i * 2 + f, 1), 0:g.cols].rearrange("p a b -> p (a b)"),
                                                   FP_[:, 0:g.cols],
                                                   HH[:, bass.ds(i * 2 + f, 1), 0:g.cols].rearrange("p a b -> p (a b)")
                                                   .bitcast(F32), ALU.subtract).then_inc(hidden_lo, 1)
                                pool.wait_ge(hidden_lo, i * 2 + (st["mult"] + f0 + f + 1))
                        n += 2 * nf

                        def down(i, n, d):
                            for j in range(4):
                                split_lo(i, n + j + AHEAD)
                                pool.wait_ge(product_read[(n + j) % 2], half(i, n + j) + 1)
                                y = Y[:, bass.ds(i * 4 + (d + j), 1), 0:g.cols].rearrange("p a b -> p (a b)")
                                pool.tensor_tensor(y, FG[:, j % 2, 0:g.cols], y, ALU.add).then_inc(added, 1)

                        if n + KD + AHEAD > NT:
                            for k in range(KD // 4):
                                down(0, n + 4 * k, 4 * k)
                        else:
                            with pool.Fori(0, KD // 4) as i:
                                down(i, n, 0)
                        n += KD
                elif name == "ln":
                    for t, (col, rows) in enumerate(g.tiles):
                        k = st["fwd"] + t
                        pool.wait_ge(var_ready, k + 1)
                        pool.tensor_tensor(RSTD[0:rows, t % 2:t % 2 + 1], VE[0:rows, t % 2:t % 2 + 1], MHALF[0:rows, :], ALU.pow)\
                            .then_inc(rstd_ready, 1)
                pool.drain().then_inc(pool_end, 1)


_INS = ["x_prompt", "x_sample", "cache_conv", "cache_k", "cache_v", "cache_idx_k", "cache_mem_k", "cache_mem_v",
        "mem_prompt", "ffn1_gate", "ffn1_up", "ffn1_down", "ln1_g", "ln1_b", "w_mix_in", "conv_w", "w_mix_out",
        "ln2_g", "ln2_b", "w_mem_q", "w_mem_k", "w_mem_v", "w_mem_o", "ln3_g", "ln3_b",
        "ffn2_gate", "ffn2_up", "ffn2_down", "ln4_g", "ln4_b"]
_OUTS = [("y_prompt", (1, SEQ, D)), ("y_sample", (1, DEC, D)), ("conv_prompt", (1, 1, 2, DCONV)),
         ("k_prompt", (1, 1, SEQ, 2, DH)), ("v_prompt", (1, 1, SEQ, 2, DH)), ("ik_prompt", (1, 1, SEQ, DH)),
         ("mem_k", (1, 1, N_MEM, 4, 256)), ("mem_v", (1, 1, N_MEM, 4, 256)), ("conv_sample", (1, 1, 2, DCONV)),
         ("k_sample", (1, 1, DEC, 2, DH)), ("v_sample", (1, 1, DEC, 2, DH)), ("ik_sample", (1, 1, DEC, DH))]


def kernel(**inputs):
    import numpy as _np
    import concourse.bacc as _bacc
    from concourse.bass_utils import run_bass_kernel_spmd as _run

    nc = _bacc.Bacc("TRN2", target_bir_lowering=False, num_devices=1)
    arrays, ins, outs = {}, {}, {}
    for name in _INS:
        a = _np.ascontiguousarray(inputs[name])
        arrays[f"in_{name}"] = a
        ins[name] = nc.dram_tensor(f"in_{name}", a.shape, mybir.dt.from_np(a.dtype), kind="ExternalInput").ap()
    for name, shape in _OUTS:
        outs[name] = nc.dram_tensor(f"out_{name}", shape, F32, kind="ExternalOutput").ap()
    encoder_step(nc, ins, outs)
    r = _run(nc, [arrays], core_ids=[0])
    return tuple(r.results[0][f"out_{name}"] for name, _ in _OUTS)
```

```python
from contextlib import ExitStack

import concourse.bass as bass
from concourse import mybir

F32 = mybir.dt.float32
F32R = mybir.dt.float32r
ALU = mybir.AluOpType
ACT = mybir.ActivationFunctionType
AX_X = mybir.AxisListType.X

P = 128
D = 1024
KD = D // P
F = 2816
SEQ = 1024
DEC = 32
PAST = 512
HALF = SEQ // 2
SKEYS = PAST + DEC
CHUNK = 64
DH = 64
HEADS = 8
N_MEM = 256
DCONV = 512
KC = DCONV // P
EPS = 1e-5
ALPHA = 2.0 ** 0.25
ATT_SCALE = DH ** -0.5
MEM_SCALE = 256.0 ** -0.5
WI_SCALE = (8 * 64) ** -0.5
TAKEN = -3.0e38
CLOSED = -2.0e38
CUT = -2.5e38
FAR = -1.0e30

FFN_PARTS = [(0, 8), (8, 8), (16, 6)]
RING = 4
AHEAD = 2


class Group:
    def __init__(self, index):
        self.index = index
        self.sample = index == 0
        self.cols = HALF + (DEC if self.sample else 0)
        self.parts = 2 if self.sample else 1
        self.width = self.cols // self.parts
        self.tiles = [(128 * t, 128) for t in range(4)] + ([(HALF, DEC)] if self.sample else [])

    def folded(self, ap):
        return ap.rearrange("p (a b) -> p a b", a=self.parts)


GROUPS = [Group(0), Group(1)]


class Memory:
    cols, parts, width = N_MEM, 1, N_MEM

    @staticmethod
    def folded(ap):
        return ap.rearrange("p (a b) -> p a b", a=1)


MEMORY = Memory()


def score_tiles(g):
    if g.sample:
        return [(2, 128, 384, 32), (3, 128, 512, 32), (4, DEC, SKEYS, (SKEYS // 4) // 8)]
    return [(t, 128, 128 * (5 + t), 32) for t in range(4)]


def att_tiles(g):
    out = []
    for t, (col, rows) in enumerate(g.tiles):
        out.append((t, col, rows, SKEYS if rows == DEC else 128 * (4 * g.index + t + 1)))
    return out


SCORE_AT = {}
_at = 0
for _g in GROUPS:
    for _t, _r, _n, _k in score_tiles(_g):
        SCORE_AT[(_g.index, _t)] = _at
        _at += _n
SCORE_COLS = _at

OFF_H, OFF_B, OFF_C = 0, DCONV, 2 * DCONV
OFF_Q = 3 * DCONV
OFF_K = OFF_Q + 512
OFF_V = OFF_K + 128
OFF_QI = OFF_V + 128
OFF_KI = OFF_QI + 512
KIW = 72
MIX_TILES = [("kiw", 0, OFF_KI, KIW), ("k", 0, OFF_K, 128), ("v", 0, OFF_V, 128)]
MIX_TILES += [("qi", i, OFF_QI + P * i, P) for i in range(4)]
MIX_TILES += [("q", i, OFF_Q + P * i, P) for i in range(4)]
for _i in range(KC):
    MIX_TILES += [("h", _i, OFF_H + P * _i, P), ("c", _i, OFF_C + P * _i, P), ("b", _i, OFF_B + P * _i, P)]

FRONT = ["loadx", "ffn", "ln", "mix", "idx"]
BACK = ["att", "mixout", "ln", "memq", "mematt", "memo", "ln", "ffn", "ln"]


def schedule():
    plan = []
    for g in (0, 1):
        plan += [(s, g, 1 if s in ("ffn", "ln") else 0) for s in FRONT]
    plan.insert(1, ("memkv", None, 0))
    for g in (0, 1):
        which = {"ffn": iter([2]), "ln": iter([2, 3, 4])}
        plan += [(s, g, next(which[s]) if s in which else 0) for s in BACK]
    stages = []
    at = dict(n=0, back=0, fwd=0, s=0, pt=0, o=0, idx=0, tok=0, mult=0, half=0, conv=0, store0=0, store1=0)
    for name, index, which in plan:
        g = GROUPS[index] if index is not None else None
        stages.append(dict(name=name, g=g, which=which, **at))
        tiles = len(g.tiles) if g else 0
        if name == "loadx":
            at["back"] += len(load_tiles(g))
        if name == "ln" and which != 4:
            at["back"] += tiles
        if name == "ln":
            at["fwd"] += tiles
            if which == 4:
                at["store0"] += (tiles + 1) // 2
                at["store1"] += tiles // 2
        if name == "ffn":
            at["mult"] += F // P
            at["half"] += KD * len(FFN_PARTS)
            at["n"] += 2 * (F // P) + KD * len(FFN_PARTS)
        if name == "memkv":
            at["n"] += 2 * KD
            at["pt"] += 5
        if name == "mix":
            at["n"] += len(MIX_TILES)
            at["tok"] += tiles
            at["conv"] += KC
        if name in ("mixout", "memq", "memo"):
            at["n"] += KD
        if name == "idx":
            at["idx"] += sum(HEADS * ((keys + 511) // 512) for _, _, keys, _ in score_tiles(g))
        if name == "att":
            at["s"] += len(att_jobs(g))
            at["pt"] += len(att_jobs(g))
            at["o"] += len(att_jobs(g)) // 4
        if name == "mematt":
            at["s"] += 4 + 4 * g.sample
            at["pt"] += 4 + 8 * g.sample
            at["o"] += 8 + 4 * g.sample
    return stages, at["n"]


def att_jobs(g):
    return [(t, col, rows, keys, kvg, hh) for t, col, rows, keys in att_tiles(g)
            for kvg in range(2) for hh in (0, 2, 1, 3)]


def load_tiles(g):
    rows0 = g.index * HALF
    memory = [("mem_prompt", t * P, P, t * P) for t in range(N_MEM // P)] if g.sample else []
    return memory + [("x_sample", 0, rows, col) if rows == DEC else ("x_prompt", rows0 + col, rows, col)
                     for col, rows in g.tiles]


def half(i, m):
    return i * 2 + m // 2


def encoder_step(nc, ins, outs):
    STAGES, NT = schedule()
    ctx = ExitStack()
    with ctx:
        at = [(nc.sbuf_base + 31) // 32 * 32]

        def region(size):
            start = at[0]
            at[0] += (size + 31) // 32 * 32
            return start

        def place(name, shape, dtype, offset):
            return nc.alloc_sbuf_tensor_at(name, shape, dtype, offset=offset)

        GC = 544
        r_xh = region(KD * GC * 4)
        r_xl = region(KD * GC * 4)
        r_hh = region(KD * GC * 4)
        r_hl = region(KD * GC * 4)
        r_y = region(KD * GC * 4)
        XH = place("XH", [P, KD, GC], F32R, r_xh)
        XL = place("XL", [P, KD, GC], F32R, r_xl)
        HH = place("HH", [P, KD, GC], F32R, r_hh)
        HL = place("HL", [P, KD, GC], F32R, r_hl)
        Y = place("Y", [P, KD, GC], F32, r_y)
        QX = place("QX", [P, KD, GC], F32, r_hh)
        YCH = place("YCH", [P, KC, GC], F32R, r_hl)
        YCL = place("YCL", [P, KC, GC], F32R, r_hl + KC * GC * 4)
        QA = place("QA", [P, KC, GC], F32, r_xh)
        PT = place("PT", [P, 8, 4, P], F32, r_xl)
        QM = place("QM", [P, KD, GC], F32, r_hh)
        PTM = place("PTM", [P, 2, 4, GC], F32, r_hl)

        WRAW = place("WRAW", [P, 2, KD, P], F32, region(2 * D * 4))
        WH = place("WH", [P, RING, KD, P], F32R, region(RING * D * 4))
        WL = place("WL", [P, RING, KD, P], F32R, region(RING * D * 4))
        KPA = place("KPA", [P, SEQ], F32, region(SEQ * 4))
        KPB = place("KPB", [P, SEQ], F32, region(SEQ * 4))
        KSA = place("KSA", [P, SKEYS], F32, region(SKEYS * 4))
        KSB = place("KSB", [P, SKEYS], F32, region(SKEYS * 4))
        KIP = place("KIP", [P, SEQ], F32, region(SEQ * 4))
        KIS = place("KIS", [P, SKEYS], F32, region(SKEYS * 4))
        VP = place("VP", [P, 8, P], F32, region(SEQ * 4))
        VS = place("VS", [P, 5, P], F32, region(5 * P * 4))
        MKT = place("MKT", [P, KD, N_MEM], F32, region(KD * N_MEM * 4))
        MV = place("MV", [P, 2, D], F32, region(2 * D * 4))
        r_sc = region(SCORE_COLS * 4)
        SC = place("SC", [P, SCORE_COLS], F32, r_sc)
        r_t = region(16384)
        PR = place("PR", [P, 4, 1024], F32, r_t)
        XT = place("XT", [P, 4, D], F32, r_t)
        GB = place("GB", [P, 2, D], F32, r_t + 8192)
        FG = place("FG", [P, 2, GC], F32, r_t)
        FP_ = place("FP", [P, GC], F32, r_t + 2 * GC * 4)
        KVT = place("KVT", [P, 3, GC], F32, r_t)
        TOK = place("TOK", [P, 2, 328], F32, r_t + 3 * GC * 4)
        HB = place("HB", [P, GC], F32, r_t + 9152)
        UB = place("UB", [P, 548], F32, r_t + 9152 + 2176)
        CB = place("CB", [P, 548], F32, r_t + 9152 + 2176 + 2208)
        RB = place("RB", [P, 4, 512], F32, r_t)
        MKTOK = place("MKTOK", [P, 2, D], F32, r_t)
        MVT = place("MVT", [P, KD, N_MEM], F32, r_sc)
        CK = place("CK", [P, 4, 192], F32, r_sc + 8192)
        PM = place("PM", [P, 2, 4, N_MEM], F32, r_t)
        MKS = place("MKS", [P, 2, 256], F32, r_t + 8192)
        MVS = place("MVS", [P, 2, 256], F32, r_t + 8192 + 2048)
        MKTS = place("MKTS", [P, 2, 256], F32, r_t + 8192 + 4096)

        ident = place("ident", [P, P], F32, region(512))
        DM = place("DM", [P, 256], F32, region(1024))
        WI = place("WI", [P, 5, 8], F32, region(160))
        CW = place("CW", [P, 3, KC], F32, region(64))
        CPREV = place("CPREV", [P, KC, 2], F32, region(32))
        TAILP = place("TAILP", [P, KC, 2], F32, region(32))
        TAILS = place("TAILS", [P, KC, 2], F32, region(32))
        ST = place("ST", [P, 2, 12], F32, region(96))
        MVAR = place("MVAR", [P, 2, 2], F32, region(32))
        VE = place("VE", [P, 2], F32, region(32))
        RSTD = place("RSTD", [P, 2], F32, region(32))
        MHALF = place("MHALF", [P, 1], F32, region(32))
        M8 = place("M8", [P, 8], F32, region(32))
        MX = place("MX", [P, 2, 4], F32, region(32))
        NM = place("NM", [P, 2, 4], F32, region(32))
        RS = place("RS", [P, 2, 4], F32, region(32))
        RR = place("RR", [P, 2, 4], F32, region(32))
        assert at[0] <= nc.sbuf_usable_end, (at[0], nc.sbuf_usable_end)

        LIN = ctx.enter_context(nc.psum_tensor("LIN", [P, 2, 2, 512], F32))
        TR = ctx.enter_context(nc.psum_tensor("TR", [P, 2, 1024], F32))

        spill_q = [nc.dram_tensor(f"spill_q{i}", [P, KC, GC], F32, kind="Internal").ap() for i in range(2)]
        spill_y = [nc.dram_tensor(f"spill_y{i}", [P, KD, GC], F32, kind="Internal").ap() for i in range(2)]
        spill_ch = [nc.dram_tensor(f"spill_ch{i}", [P, KC, GC], F32, kind="Internal").ap() for i in range(2)]
        spill_cl = [nc.dram_tensor(f"spill_cl{i}", [P, KC, GC], F32, kind="Internal").ap() for i in range(2)]

        def sem(name):
            return ctx.enter_context(nc.semaphore(name))

        raw_loaded = [sem(f"raw_loaded{i}") for i in range(2)]
        hi_split = sem("hi_split")
        lo_split = sem("lo_split")
        product = sem("product")
        product_read = [sem(f"product_read{i}") for i in range(2)]
        pe_end = sem("pe_end")
        act_end = sem("act_end")
        dve_end = sem("dve_end")
        pool_end = sem("pool_end")
        consts = sem("consts")
        masks = sem("masks")
        moved = sem("moved")
        spilled = sem("spilled")
        stored = sem("stored")
        xt_loaded = [sem(f"xt_loaded{i}") for i in range(4)]
        xt_stored = [sem(f"xt_stored{i}") for i in range(2)]
        back_done = sem("back_done")
        back_hi = sem("back_hi")
        back_lo = sem("back_lo")
        fwd_done = sem("fwd_done")
        fwd_read = sem("fwd_read")
        var_ready = sem("var_ready")
        rstd_ready = sem("rstd_ready")
        xt_ready = sem("xt_ready")
        gated = sem("gated")
        multiplied = sem("multiplied")
        hidden_hi = sem("hidden_hi")
        hidden_lo = sem("hidden_lo")
        halved = sem("halved")
        added = sem("added")
        dve_step = sem("dve_step")
        act_step = sem("act_step")
        pool_step = sem("pool_step")
        tok_done = sem("tok_done")
        tok_read = sem("tok_read")
        tok_stored = [sem(f"tok_stored{i}") for i in range(2)]
        yc_ready = sem("yc_ready")
        yc_hi = sem("yc_hi")
        yc_lo = sem("yc_lo")
        h_read = sem("h_read")
        idx_done = sem("idx_done")
        relu_done = sem("relu_done")
        idx_added = sem("idx_added")
        s_done = sem("s_done")
        nm_ready = sem("nm_ready")
        exp_done = sem("exp_done")
        p_ready = sem("p_ready")
        pt_done = sem("pt_done")
        pt_read = sem("pt_read")
        o_done = sem("o_done")
        o_hi = sem("o_hi")
        o_lo = sem("o_lo")
        ck_loaded = sem("ck_loaded")
        head_loaded = sem("head_loaded")

        block = ctx.enter_context(nc.Block())

        gate_w = [ins[f"ffn{k}_gate"][0].rearrange("(c p) f -> p c f", p=P) for k in (1, 2)]
        up_w = [ins[f"ffn{k}_up"][0].rearrange("(c p) f -> p c f", p=P) for k in (1, 2)]
        down_w = [ins[f"ffn{k}_down"][0].rearrange("(c p) d -> p c d", p=P) for k in (1, 2)]
        mix_w = ins["w_mix_in"][0].rearrange("(c p) f -> p c f", p=P)

        def square(name):
            return ins[name][0].rearrange("(c p) f -> p c f", p=P)

        x_tok = [ins["x_prompt"][0], ins["x_sample"][0]]

        @block.sync
        def _(sp):
            def load(i, m, src, nk=KD, cols=P):
                if m >= 2:
                    sp.wait_ge(lo_split, i * 4 + (m - 1))
                sp.dma_start(WRAW[:, m % 2, 0:nk, 0:cols], src).then_inc(raw_loaded[m % 2], 16)

            for st in STAGES:
                n0, name = st["n"], st["name"]
                if name == "memkv":
                    for j in range(16):
                        load(0, j, square(("w_mem_k", "w_mem_v")[j // 8])[:, :, bass.ts(j % 8, P)])
                elif name == "mix":
                    for j, (_, _, c0, m) in enumerate(MIX_TILES):
                        load(0, n0 + j, mix_w[:, :, c0:c0 + m], cols=m)
                elif name in ("mixout", "memq", "memo"):
                    w = square({"mixout": "w_mix_out", "memq": "w_mem_q", "memo": "w_mem_o"}[name])
                    for j in range(8):
                        load(0, n0 + j, w[:, :, bass.ts(j, P)])
                elif name == "ffn":
                    k = st["which"] - 1
                    n = n0
                    for f0, nf in FFN_PARTS:
                        with sp.Fori(0, nf // 2) as i:
                            for j in range(4):
                                w = (gate_w, up_w)[j % 2][k]
                                load(i, n + j, w[:, :, bass.ts(i * 2 + (f0 + j // 2), P)])
                        n += 2 * nf
                        with sp.Fori(0, KD // 4) as i:
                            for j in range(4):
                                load(i, n + j,
                                     down_w[k][:, f0:f0 + nf, bass.ts(i * 4 + j, P)], nk=nf)
                        n += KD

        @block.tensor
        def _(pe):
            def begin(s):
                if s:
                    pe.wait_ge(act_end, s)
                    pe.wait_ge(dve_end, s)
                    pe.wait_ge(pool_end, s)

            def linear(g, i, n, nk, hi, lo, m=P, hidden=None):
                w, slot = n % RING, n % 2
                pe.wait_ge(lo_split, i * 4 + (n + 1))
                pe.wait_ge(product_read[slot], half(i, n))
                for c in range(nk):
                    if hidden is not None:
                        pe.wait_ge(hidden_lo, hidden + c + 1)
                    for wt, x in ((WH, hi), (WH, lo), (WL, hi)):
                        for a in range(g.parts):
                            last = pe.matmul(LIN[0:m, slot, a, 0:g.width], wt[:, w, c, 0:m],
                                             x[:, c, a * g.width:(a + 1) * g.width],
                                             start=(c == 0 and wt is WH and x is hi),
                                             stop=(c == nk - 1 and wt is WL))
                last.then_inc(product, 1)

            def loads_of(b):
                loaded = [st["back"] + t for st in STAGES if st["name"] == "loadx" for t in range(len(load_tiles(st["g"])))]
                return sum(1 for x in loaded if x <= b and x % 4 == b % 4)

            def to_feature(b, rows, slot):
                if b >= 2:
                    pe.wait_ge(back_lo, b - 1)
                for d in range(KD):
                    last = pe.transpose(TR[:, b % 2, d * P:d * P + rows], XT[0:rows, slot, d * P:(d + 1) * P],
                                        ident[0:rows, 0:rows])
                last.then_inc(back_done, 1)

            base = dict(idx=0, tok=0)
            for s, st in enumerate(STAGES):
                begin(s)
                name, g, n0 = st["name"], st["g"], st["n"]
                if s == 0:
                    pe.wait_ge(consts, 3)
                if name == "loadx":
                    for t, (_, _, rows, _) in enumerate(load_tiles(g)):
                        b = st["back"] + t
                        pe.wait_ge(xt_loaded[b % 4], 16 * loads_of(b))
                        to_feature(b, rows, b % 4)
                elif name == "memkv":
                    for j in range(16):
                        linear(MEMORY, 0, j, KD, HH, HL)
                    for k in range(4):
                        if k == 0:
                            pe.wait_ge(product_read[1], KD // 2)
                            pe.wait_ge(product_read[0], KD // 2)
                        if k == 2:
                            pe.wait_ge(product_read[1], KD)
                            pe.wait_ge(product_read[0], KD)
                            pe.wait_ge(pt_read, 1)
                        if k == 3:
                            pe.wait_ge(pt_read, 2)
                        src = MKT if k < 2 else MVT
                        for d in range(KD):
                            last = pe.transpose(TR[:, k % 2, d * P:(d + 1) * P], src[:, d, (k % 2) * P:(k % 2 + 1) * P],
                                                ident[:, :])
                        last.then_inc(pt_done, 1)
                    pe.wait_ge(ck_loaded, 32)
                    pe.wait_ge(pt_read, 4)
                    for q in range(4):
                        pe.transpose(TR[:, 0, q * P:(q + 1) * P], CK[:, q, 0:P], ident[:, :])
                        last = pe.transpose(TR[0:64, 1, q * P:(q + 1) * P], CK[:, q, P:P + 64], ident[:, :])
                    last.then_inc(pt_done, 1)
                elif name == "ffn":
                    n = n0
                    for f0, nf in FFN_PARTS:
                        with pe.Fori(0, nf // 2) as i:
                            for j in range(4):
                                linear(g, i, n + j, KD, XH, XL)
                        n += 2 * nf
                        with pe.Fori(0, KD // 4) as i:
                            for j in range(4):
                                linear(g, i, n + j, nf, HH, HL, hidden=st["mult"] + f0)
                        n += KD
                elif name == "ln":
                    k = len(g.tiles)
                    for t in range(k + 1):
                        if t < k:
                            col, rows = g.tiles[t]
                            if t >= 2:
                                pe.wait_ge(fwd_read, st["fwd"] + t - 1)
                            for d in range(KD):
                                last = pe.transpose(LIN[0:rows, t % 2, d // 4, (d % 4) * P:(d % 4 + 1) * P],
                                                    Y[:, d, col:col + rows], ident[:, :])
                            last.then_inc(fwd_done, 1)
                        if t >= 1 and st["which"] != 4:
                            pe.wait_ge(xt_ready, st["fwd"] + t)
                            to_feature(st["back"] + t - 1, g.tiles[t - 1][1], (t - 1) % 2)
                elif name == "mix":
                    for j, (kind, i, _, m) in enumerate(MIX_TILES):
                        linear(g, 0, n0 + j, KD, XH, XL, m)
                        if j == 10:
                            pe.wait_ge(product_read[(n0 + 1) % 2], (n0 + 1) // 2 + 1)
                            pe.wait_ge(product_read[n0 % 2], (n0 + 2) // 2 + 1)
                            for t, (col, rows) in enumerate(g.tiles):
                                k = base["tok"]
                                if k >= 1:
                                    pe.wait_ge(tok_read, k)
                                pe.transpose(TR[0:rows, 0, 0:P], KVT[:, 1, col:col + rows], ident[:, :])
                                pe.transpose(TR[0:rows, 0, P:2 * P], KVT[:, 2, col:col + rows], ident[:, :])
                                pe.transpose(TR[0:rows, 0, 2 * P:2 * P + KIW], KVT[0:KIW, 0, col:col + rows],
                                             ident[0:KIW, 0:KIW]).then_inc(tok_done, 1)
                                base["tok"] += 1
                elif name == "idx":
                    for t, rows, keys, _ in score_tiles(g):
                        kmat = KIS if rows == DEC else KIP
                        for k0 in range(0, keys, 512):
                            w = min(512, keys - k0)
                            for h in range(HEADS):
                                k = base["idx"]
                                if k >= 4:
                                    pe.wait_ge(relu_done, k - 3)
                                lo = 64 * (h % 2)
                                pe.matmul(LIN[0:rows, (k % 4) // 2, k % 2, 0:w],
                                          QX[lo:lo + 64, 4 + h // 2, g.tiles[t][0]:g.tiles[t][0] + rows],
                                          kmat[lo:lo + 64, k0:k0 + w], start=True, stop=True).then_inc(idx_done, 1)
                                base["idx"] += 1
                elif name == "att":
                    s0, pt0, o0 = st["s"], st["pt"], st["o"]
                    jobs = att_jobs(g)

                    def scores(a):
                        t, col, rows, keys, kvg, hh = jobs[a]
                        h, lo = 4 * kvg + hh, 64 * (hh % 2)
                        if a >= 2:
                            pe.wait_ge(nm_ready, s0 + a - 1)
                        same = (kvg == 0) == (lo == 0)
                        kmat = (KSA if same else KSB) if rows == DEC else (KPA if same else KPB)
                        for k0 in range(0, keys, 512):
                            w = min(512, keys - k0)
                            last = pe.matmul(LIN[0:rows, a % 2, k0 // 512, 0:w],
                                             QA[lo:lo + 64, h // 2, col:col + rows],
                                             kmat[lo:lo + 64, k0:k0 + w], start=True, stop=True)
                        last.then_inc(s_done, 1)

                    def turn(a):
                        t, col, rows, keys, kvg, hh = jobs[a]
                        pe.wait_ge(p_ready, s0 + a + 1)
                        pe.wait_ge(pt_read, pt0 + a)
                        for kb in range(0, keys, P):
                            w = min(P, keys - kb)
                            last = pe.transpose(TR[0:w, 0, kb:kb + rows],
                                                PR[0:rows, a % 4, kb:kb + w], ident[0:rows, 0:rows])
                        last.then_inc(pt_done, 1)

                    def values(q):
                        t, col, rows, keys, kvg, _ = jobs[4 * q]
                        pe.wait_ge(pt_read, pt0 + 4 * q + 4)
                        if q >= 2:
                            pe.wait_ge(o_lo, o0 + q - 1)
                        vmat = VS if rows == DEC else VP
                        nb = (keys + P - 1) // P
                        for kb in range(nb):
                            w = min(P, keys - kb * P)
                            for odd in range(2):
                                last = pe.matmul(TR[64 * odd:64 * odd + 64, 1, 512 * (q % 2):512 * (q % 2) + 2 * rows]
                                                 .rearrange("p (a b) -> p a b", a=2),
                                                 vmat[0:w, kb, 64 * kvg:64 * kvg + 64],
                                                 PT[0:w, kb, 2 * odd:2 * odd + 2, 0:rows],
                                                 start=(kb == 0), stop=(kb == nb - 1))
                        last.then_inc(o_done, 1)

                    scores(0)
                    scores(1)
                    for a in range(len(jobs)):
                        if a + 2 < len(jobs):
                            scores(a + 2)
                        if a % 4 == 0 and a:
                            values(a // 4 - 1)
                        turn(a)
                    values(len(jobs) // 4 - 1)
                elif name in ("mixout", "memq", "memo"):
                    src = (HH, HL) if name == "mixout" else (XH, XL)
                    for j in range(8):
                        linear(g, 0, n0 + j, KD, *src)
                elif name == "mematt":
                    c = dict(s=st["s"], nm=st["s"], exp=st["s"], p=st["s"], pt=st["pt"], o=st["o"])
                    for t in range(5):
                        if t < 4:
                            if t >= 2:
                                pe.wait_ge(exp_done, c["exp"] + t - 1)
                            for h in range(4):
                                for e in range(2):
                                    last = pe.matmul(LIN[:, t % 2, h // 2, 256 * (h % 2):256 * (h % 2) + 256],
                                                     QM[:, 2 * h + e, t * P:(t + 1) * P], MKT[:, 2 * h + e, :],
                                                     start=(e == 0), stop=(e == 1))
                            last.then_inc(s_done, 1)
                        if t >= 1:
                            u = t - 1
                            pe.wait_ge(p_ready, c["p"] + u + 1)
                            if u >= 2:
                                pe.wait_ge(pt_read, c["pt"] + u - 1)
                            for q in range(8):
                                last = pe.transpose(TR[:, u % 2, q * P:(q + 1) * P],
                                                    PM[:, u % 2, q % 4, (q // 4) * P:(q // 4 + 1) * P], ident[:, :])
                            last.then_inc(pt_done, 1)
                    pe.wait_ge(pt_read, c["pt"] + 4)
                    for o in range(8):
                        if o >= 2:
                            pe.wait_ge(o_lo, c["o"] + o - 1)
                        else:
                            pe.wait_ge(exp_done, c["exp"] + 4)
                        for mb in range(2):
                            last = pe.matmul(LIN[:, o % 2, 0, :], MV[:, mb, o * P:(o + 1) * P],
                                             PTM[:, mb, o // 2, 0:HALF], start=(mb == 0), stop=(mb == 1))
                        last.then_inc(o_done, 1)
                    if g.sample:
                        for h in range(4):
                            pe.wait_ge(head_loaded, 32 * (h + 1))
                            pe.wait_ge(pt_read, c["pt"] + 4 + 2 * h)
                            for q in range(4):
                                last = pe.transpose(TR[:, 0, q * P:(q + 1) * P],
                                                    MKS[:, q % 2, (q // 2) * P:(q // 2 + 1) * P], ident[:, :])
                            last.then_inc(pt_done, 1)
                            pe.wait_ge(pt_read, c["pt"] + 5 + 2 * h)
                            pe.wait_ge(o_lo, c["o"] + 8 + h)
                            for e in range(2):
                                last = pe.matmul(LIN[0:DEC, 0, 0, 0:256], QM[:, 2 * h + e, HALF:HALF + DEC],
                                                 MKTS[:, e, :], start=(e == 0), stop=(e == 1))
                            last.then_inc(s_done, 1)
                            pe.wait_ge(p_ready, c["p"] + 5 + h)
                            for mb in range(2):
                                last = pe.transpose(TR[:, 1, mb * P:mb * P + DEC], PM[0:DEC, 0, h, mb * P:(mb + 1) * P],
                                                    ident[0:DEC, 0:DEC])
                            last.then_inc(pt_done, 1)
                            pe.wait_ge(pt_read, c["pt"] + 6 + 2 * h)
                            for e in range(2):
                                for mb in range(2):
                                    last = pe.matmul(LIN[:, 1, e, 0:DEC], MVS[:, mb, e * P:(e + 1) * P],
                                                     PTM[:, mb, h, HALF:HALF + DEC], start=(mb == 0), stop=(mb == 1))
                            last.then_inc(o_done, 1)
                pe.drain().then_inc(pe_end, 1)

        @block.scalar
        def _(act):
            moves = [0]

            def begin(s):
                if s:
                    act.wait_ge(pe_end, s)
                    act.wait_ge(dve_end, s)
                    act.wait_ge(pool_end, s)

            def move(dst, src):
                act.dma_start(dst, src).then_inc(moved, 16)
                moves[0] += 16

            def all_moved():
                act.wait_ge(moved, moves[0])

            def split_hi(i, n):
                if n >= NT:
                    return
                act.wait_ge(raw_loaded[n % 2], half(i, n) * 16 + 16)
                if n >= RING:
                    act.wait_ge(product, i * 4 + (n - RING + 1))
                act.activation(WH[:, n % RING, :, :], WRAW[:, n % 2, :, :], ACT.Copy).then_inc(hi_split, 1)

            def evac(g, i, n, dst, m=P, func=ACT.Copy, scale=1.0):
                act.wait_ge(product, i * 4 + (n + 1))
                return act.activation(g.folded(dst), LIN[0:m, n % 2, 0:g.parts, 0:g.width], func, scale=scale)

            def from_feature(b, col, rows, memory=False):
                act.wait_ge(back_done, b + 1)
                src = TR[:, b % 2, :].rearrange("p (d t) -> p d t", d=KD)[:, :, 0:rows]
                if memory:
                    act.activation(HH[:, :, col:col + rows], src, ACT.Copy).then_inc(back_hi, 1)
                    return
                act.activation(XH[:, :, col:col + rows], src, ACT.Copy)
                act.activation(Y[:, :, col:col + rows], src, ACT.Copy, scale=ALPHA).then_inc(back_hi, 1)

            def load_ln(which):
                for r, nm in enumerate(("g", "b")):
                    move(GB[:, r, :], ins[f"ln{which}_{nm}"][0:1, :].to_broadcast([P, D]))

            base = dict(idx=0, tok=0)
            for s, st in enumerate(STAGES):
                begin(s)
                name, g, n0, which = st["name"], st["g"], st["n"], st["which"]
                if name == "loadx":
                    tiles = load_tiles(g)

                    def load_tile(t):
                        src, row, rows, _ = tiles[t]
                        b = st["back"] + t
                        act.dma_start(XT[0:rows, b % 4, :], ins[src][0, row:row + rows, :]).then_inc(xt_loaded[b % 4], 16)

                    for t in range(4):
                        load_tile(t)
                    if s == 0:
                        for j in range(AHEAD):
                            split_hi(0, j)
                    for t, (src, _, rows, col) in enumerate(tiles):
                        from_feature(st["back"] + t, col, rows, src == "mem_prompt")
                        if t + 4 < len(tiles):
                            load_tile(t + 4)
                elif name == "memkv":
                    act.dma_start(CK[:, :, 0:P], ins["cache_k"][0, 0].rearrange("(q p) h d -> p q (h d)", p=P)).then_inc(ck_loaded, 16)
                    act.dma_start(CK[:, :, P:P + 64], ins["cache_idx_k"][0, 0].rearrange("(q p) d -> p q d", p=P)).then_inc(ck_loaded, 16)
                    for i in range(4):
                        move(VS[:, i, :], ins["cache_v"][0, 0, i * P:(i + 1) * P].rearrange("p h d -> p (h d)"))
                    with nc.allow_non_contiguous_dma("small constants"):
                        for i in range(KC):
                            move(CW[:, :, i], ins["conv_w"][0, :, i * P:(i + 1) * P].rearrange("j p -> p j"))
                            move(CPREV[:, i, :], ins["cache_conv"][0, 0, :, i * P:(i + 1) * P].rearrange("r p -> p r"))
                    for j in range(16):
                        split_hi(0, j + AHEAD)
                        evac(MEMORY, 0, j, (MKT if j < KD else MVT)[:, j % KD, :]).then_inc(product_read[j % 2], 1)
                    for k in range(4):
                        act.wait_ge(pt_done, k + 1)
                        act.activation((MKTOK if k < 2 else MV)[:, k % 2, :], TR[:, k % 2, :], ACT.Copy).then_inc(pt_read, 1)
                    act.wait_ge(pt_read, 4)
                    for buf, out in ((MKTOK, outs["mem_k"]), (MV, outs["mem_v"])):
                        move(out[0, 0].rearrange("(b p) h d -> p b (h d)", p=P), buf[:, :, :])
                    act.wait_ge(pt_done, 5)
                    act.activation(KSA[:, 0:PAST], TR[:, 0, 0:PAST], ACT.Copy)
                    act.activation(KIS[0:64, 0:PAST], TR[0:64, 1, 0:PAST], ACT.Copy).then_inc(pt_read, 1)
                    act.wait_ge(pt_read, 5)
                    move(KSB[0:64, 0:PAST], KSA[64:128, 0:PAST])
                    move(KSB[64:128, 0:PAST], KSA[0:64, 0:PAST])
                    move(KIS[64:128, 0:PAST], KIS[0:64, 0:PAST])
                    all_moved()
                elif name == "ffn":
                    load_ln(1 if which == 1 else 4)
                    n = n0
                    for part, (f0, nf) in enumerate(FFN_PARTS):
                        halves = st["half"] + KD * part
                        if halves:
                            act.wait_ge(added, halves)

                        with act.Fori(0, nf // 2) as i:
                            for j in range(4):
                                split_hi(i, n + j + AHEAD)
                                evac(g, i, n + j, FG[:, j % 2, 0:g.cols], func=ACT.Copy if j % 2 else ACT.Silu)\
                                    .then_inc(product_read[(n + j) % 2], 1)
                                if j % 2:
                                    act.wait_ge(multiplied, i * 2 + (st["mult"] + f0 + j // 2 + 1))
                                    act.activation(HH[:, bass.ds(i * 2 + j // 2, 1), 0:g.cols].rearrange("p a b -> p (a b)"),
                                                   FP_[:, 0:g.cols], ACT.Copy).then_inc(hidden_hi, 1)
                        n += 2 * nf

                        def down(i, n, halves):
                            for j in range(4):
                                split_hi(i, n + j + AHEAD)
                                if halves + j >= 2:
                                    act.wait_ge(added, i * 4 + (halves + j - 1))
                                evac(g, i, n + j, FG[:, j % 2, 0:g.cols], scale=0.5)\
                                    .then_inc(product_read[(n + j) % 2], 1)

                        if halves == 0 or n + KD + AHEAD > NT:
                            for k in range(KD // 4):
                                down(0, n + 4 * k, halves + 4 * k)
                        else:
                            with act.Fori(0, KD // 4) as i:
                                down(i, n, halves)
                        n += KD
                    all_moved()
                elif name == "ln":
                    if which != 4:
                        for t, (col, rows) in enumerate(g.tiles):
                            from_feature(st["back"] + t, col, rows)
                    else:
                        for t, (col, rows) in enumerate(g.tiles):
                            k = st["fwd"] + t
                            act.wait_ge(xt_ready, k + 1)
                            dst = outs["y_sample"][0] if rows == DEC else \
                                outs["y_prompt"][0, g.index * HALF + col:g.index * HALF + col + rows, :]
                            act.dma_start(dst, XT[0:rows, t % 2, :]).then_inc(xt_stored[t % 2], 16)
                        for k2 in range(2):
                            act.wait_ge(xt_stored[k2], 16 * (st[f"store{k2}"] + (len(g.tiles) + 1 - k2) // 2))
                elif name == "mix":
                    c0 = g.index * HALF
                    for j, (kind, i, _, m) in enumerate(MIX_TILES):
                        n = n0 + j
                        split_hi(0, n + AHEAD)
                        if kind in ("kiw", "k", "v"):
                            evac(g, 0, n, KVT[0:m, j, 0:g.cols], m).then_inc(product_read[n % 2], 1)
                            act.wait_ge(product_read[n % 2], n // 2 + 1)
                            if kind == "kiw":
                                for b in (0, 64):
                                    move(KIP[b:b + 64, c0:c0 + HALF], KVT[0:64, 0, 0:HALF])
                                    if g.sample:
                                        move(KIS[b:b + 64, PAST:SKEYS], KVT[0:64, 0, HALF:])
                            if kind == "k":
                                move(KPA[:, c0:c0 + HALF], KVT[:, 1, 0:HALF])
                                for b in (0, 64):
                                    move(KPB[b:b + 64, c0:c0 + HALF], KVT[64 - b:128 - b, 1, 0:HALF])
                                    if g.sample:
                                        move(KSB[b:b + 64, PAST:SKEYS], KVT[64 - b:128 - b, 1, HALF:])
                                if g.sample:
                                    move(KSA[:, PAST:SKEYS], KVT[:, 1, HALF:])
                        elif kind == "qi":
                            evac(g, 0, n, QX[:, 4 + i, 0:g.cols]).then_inc(product_read[n % 2], 1)
                        elif kind == "q":
                            evac(g, 0, n, QX[:, i, 0:g.cols]).then_inc(product_read[n % 2], 1)
                        elif kind == "h":
                            q = KC * g.index + i
                            if q >= 1:
                                act.wait_ge(yc_lo, q)
                            evac(g, 0, n, HB[:, 0:g.cols]).then_inc(product_read[n % 2], 1)
                        elif kind == "b":
                            q = KC * g.index + i
                            act.wait_ge(product_read[n % 2], n // 2 + 1)
                            act.activation(YCH[:, i, 0:g.cols], HB[:, 0:g.cols], ACT.Copy).then_inc(yc_hi, 1)
                        if j == 10:
                            for t, (col, rows) in enumerate(g.tiles):
                                k = base["tok"]
                                act.wait_ge(tok_done, k + 1)
                                if k >= 2:
                                    act.wait_ge(tok_stored[k % 2], 48 * (k // 2))
                                act.activation(TOK[0:rows, k % 2, :], TR[0:rows, 0, 0:328], ACT.Copy)
                                v = VS[0:rows, 4, :] if rows == DEC else VP[:, 4 * g.index + t, :]
                                act.activation(v, TR[0:rows, 0, P:2 * P], ACT.Copy)
                                act.activation(WI[0:rows, t, :], TR[0:rows, 0, 320:328], ACT.Copy, scale=WI_SCALE)\
                                    .then_inc(tok_read, 1)
                                act.wait_ge(tok_read, k + 1)
                                sfx = "sample" if rows == DEC else "prompt"
                                r0 = 0 if rows == DEC else c0 + col
                                act.dma_start(outs[f"k_{sfx}"][0, 0, r0:r0 + rows].rearrange("t h d -> t (h d)"),
                                              TOK[0:rows, k % 2, 0:P]).then_inc(tok_stored[k % 2], 16)
                                act.dma_start(outs[f"v_{sfx}"][0, 0, r0:r0 + rows].rearrange("t h d -> t (h d)"),
                                              TOK[0:rows, k % 2, P:2 * P]).then_inc(tok_stored[k % 2], 16)
                                act.dma_start(outs[f"ik_{sfx}"][0, 0, r0:r0 + rows],
                                              TOK[0:rows, k % 2, 2 * P:2 * P + 64]).then_inc(tok_stored[k % 2], 16)
                                base["tok"] += 1
                    k = base["tok"]
                    act.wait_ge(tok_stored[0], 48 * ((k + 1) // 2))
                    act.wait_ge(tok_stored[1], 48 * (k // 2))
                    all_moved()
                elif name == "idx":
                    tail = "sample" if g.sample else "prompt"
                    with nc.allow_non_contiguous_dma("two rows of the conv input"):
                        for i in range(KC):
                            move(outs[f"conv_{tail}"][0, 0, :, i * P:(i + 1) * P].rearrange("r p -> p r"),
                                 (TAILS if g.sample else TAILP)[:, i, :])
                    for t, rows, keys, _ in score_tiles(g):
                        for k0 in range(0, keys, 512):
                            w = min(512, keys - k0)
                            for h in range(HEADS):
                                k = base["idx"]
                                act.wait_ge(idx_done, k + 1)
                                if k >= 4:
                                    act.wait_ge(idx_added, k - 3)
                                act.activation(RB[0:rows, k % 4, 0:w], LIN[0:rows, (k % 4) // 2, k % 2, 0:w],
                                               ACT.Relu).then_inc(relu_done, 1)
                                base["idx"] += 1
                    all_moved()
                elif name == "att":
                    s0, pt0, o0 = st["s"], st["pt"], st["o"]
                    jobs = att_jobs(g)

                    def exponent(a):
                        t, col, rows, keys, kvg, hh = jobs[a]
                        q = a % 2
                        act.wait_ge(nm_ready, s0 + a + 1)
                        act.activation(PR[0:rows, a % 4, 0:keys], PR[0:rows, a % 4, 0:keys], ACT.Exp, bias=NM[0:rows, q, 0:1],
                                       scale=ATT_SCALE, accum_out=RS[0:rows, q, 0:1]).then_inc(exp_done, 1)

                    def out_hi(q):
                        t, col, rows, keys, kvg, _ = jobs[4 * q]
                        act.wait_ge(o_done, o0 + q + 1)
                        o = TR[:, 1, 512 * (q % 2):512 * (q % 2) + 2 * rows].rearrange("p (a b) -> p a b", a=2)
                        act.activation(HH[:, 4 + 2 * kvg:6 + 2 * kvg, col:col + rows], o, ACT.Copy).then_inc(o_hi, 1)

                    exponent(0)
                    for a in range(len(jobs)):
                        if a + 1 < len(jobs):
                            exponent(a + 1)
                        if a % 4 == 0 and a:
                            out_hi(a // 4 - 1)
                        t, col, rows, keys, kvg, hh = jobs[a]
                        act.wait_ge(pt_done, pt0 + a + 1)
                        slot = (0, 2, 1, 3)[hh]
                        full = keys // P
                        src = TR[:, 0, :].rearrange("p (k q) -> p k q", k=8)
                        last = act.activation(PT[:, 0:full, slot, 0:rows], src[:, 0:full, 0:rows], ACT.Copy)
                        if keys % P:
                            last = act.activation(PT[0:keys % P, full, slot, 0:rows], src[0:keys % P, full, 0:rows], ACT.Copy)
                        last.then_inc(pt_read, 1)
                    out_hi(len(jobs) // 4 - 1)
                elif name in ("mixout", "memo"):
                    load_ln(2 if name == "mixout" else 3)
                    for j in range(8):
                        split_hi(0, n0 + j + AHEAD)
                    all_moved()
                elif name == "memq":
                    for j in range(8):
                        n = n0 + j
                        split_hi(0, n + AHEAD)
                        evac(g, 0, n, QM[:, j, 0:g.cols]).then_inc(product_read[n % 2], 1)
                elif name == "mematt":
                    c = dict(s=st["s"], nm=st["s"], exp=st["s"], p=st["s"], pt=st["pt"], o=st["o"])

                    def load_head(h):
                        for buf, src in ((MKS, "cache_mem_k"), (MVS, "cache_mem_v")):
                            act.dma_start(buf[:, :, :], ins[src][0, 0, :, h, :].rearrange("(b p) d -> p b d", p=P))\
                                .then_inc(head_loaded, 16)

                    if g.sample:
                        load_head(0)
                    for t in range(5):
                        if t < 4:
                            act.wait_ge(nm_ready, c["nm"] + t + 1)
                            for h in range(4):
                                last = act.activation(PM[:, t % 2, h, :], LIN[:, t % 2, h // 2, 256 * (h % 2):256 * (h % 2) + 256],
                                                      ACT.Exp, bias=NM[:, t % 2, h:h + 1], scale=MEM_SCALE,
                                                      accum_out=RS[:, t % 2, h:h + 1])
                            last.then_inc(exp_done, 1)
                        if t >= 1:
                            u = t - 1
                            act.wait_ge(pt_done, c["pt"] + u + 1)
                            act.activation(PTM[:, :, :, u * P:(u + 1) * P].rearrange("p a b q -> p (a b) q"),
                                           TR[:, u % 2, :].rearrange("p (k q) -> p k q", k=8), ACT.Copy).then_inc(pt_read, 1)
                    for o in range(8):
                        act.wait_ge(o_done, c["o"] + o + 1)
                        act.activation(XH[:, o, 0:HALF], LIN[:, o % 2, 0, :], ACT.Copy).then_inc(o_hi, 1)
                    if g.sample:
                        for h in range(4):
                            act.wait_ge(pt_done, c["pt"] + 5 + 2 * h)
                            act.activation(MKTS[:, :, :].rearrange("p a b -> p (a b)"), TR[:, 0, 0:512], ACT.Copy).then_inc(pt_read, 1)
                            act.wait_ge(nm_ready, c["nm"] + 5 + h)
                            act.activation(PM[0:DEC, 0, h, :], LIN[0:DEC, 0, 0, 0:256], ACT.Exp, bias=NM[0:DEC, 0, h:h + 1],
                                           scale=MEM_SCALE, accum_out=RS[0:DEC, 0, h:h + 1]).then_inc(exp_done, 1)
                            act.wait_ge(pt_done, c["pt"] + 6 + 2 * h)
                            act.activation(PTM[:, :, h, HALF:HALF + DEC],
                                           TR[:, 1, 0:256].rearrange("p (k q) -> p k q", k=2)[:, :, 0:DEC], ACT.Copy)\
                                .then_inc(pt_read, 1)
                            act.wait_ge(o_done, c["o"] + 9 + h)
                            act.activation(XH[:, 2 * h:2 * h + 2, HALF:HALF + DEC], LIN[:, 1, :, 0:DEC], ACT.Copy).then_inc(o_hi, 1)
                            if h < 3:
                                load_head(h + 1)
                act.drain().then_inc(act_end, 1)

        @block.vector
        def _(dve):
            steps = [0]

            def begin(s):
                if s:
                    dve.wait_ge(pe_end, s)
                    dve.wait_ge(act_end, s)
                    dve.wait_ge(pool_end, s)

            def link(ins_):
                steps[0] += 1
                ins_.then_inc(dve_step, 1)
                dve.wait_ge(dve_step, steps[0])

            def low(b, col, rows, memory=False):
                dve.wait_ge(back_hi, b + 1)
                src = TR[:, b % 2, :].rearrange("p (d t) -> p d t", d=KD)[:, :, 0:rows]
                hi, lo = (HH, HL) if memory else (XH, XL)
                dve.tensor_tensor(lo[:, :, col:col + rows], src, hi[:, :, col:col + rows].bitcast(F32), ALU.subtract)\
                    .then_inc(back_lo, 1)

            def select(g):
                for t, rows, keys, rounds in score_tiles(g):
                    at_ = SCORE_AT[(g.index, t)]
                    sc = SC[0:rows, at_:at_ + keys]
                    with dve.Fori(0, rounds):
                        dve.max(M8[0:rows, :], sc)
                        dve.drain()
                        dve.match_replace(sc, M8[0:rows, :], sc, TAKEN)
                        dve.drain()
                    dve.tensor_scalar(sc, sc, CUT, FAR, ALU.is_gt, ALU.mult)

            base = dict(idx=0)
            for s, st in enumerate(STAGES):
                begin(s)
                name, g, n0, which = st["name"], st["g"], st["n"], st["which"]
                if name == "loadx":
                    for t, (src, _, rows, col) in enumerate(load_tiles(g)):
                        low(st["back"] + t, col, rows, src == "mem_prompt")
                elif name == "ffn":
                    if which == 1 and g.index == 1:
                        select(GROUPS[0])
                    if which == 2 and g.index == 0:
                        select(GROUPS[1])
                elif name == "ln":
                    for t, (col, rows) in enumerate(g.tiles):
                        k = st["fwd"] + t
                        q = t % 2
                        dve.wait_ge(fwd_done, k + 1)
                        for h in range(2):
                            last = dve.bn_stats(ST[0:rows, q, 6 * h:6 * h + 6], LIN[0:rows, q, h, :])
                        link(last)
                        link(dve.bn_aggr(MVAR[0:rows, q, :], ST[0:rows, q, :]))
                        dve.tensor_scalar(VE[0:rows, q:q + 1], MVAR[0:rows, q, 1:2], EPS, None, ALU.add).then_inc(var_ready, 1)
                        if which == 4 and t >= 2:
                            dve.wait_ge(xt_stored[q], 16 * (st[f"store{q}"] + t // 2))
                        elif which != 4 and t >= 2:
                            dve.wait_ge(back_done, st["back"] + t - 1)
                        dve.scalar_tensor_tensor(XT[0:rows, q, :], LIN[0:rows, q, :, :].rearrange("p a b -> p (a b)"), MVAR[0:rows, q, 0:1], GB[0:rows, 0, :],
                                                 ALU.subtract, ALU.mult).then_inc(fwd_read, 1)
                        dve.wait_ge(fwd_read, k + 1)
                        dve.wait_ge(rstd_ready, k + 1)
                        dve.scalar_tensor_tensor(XT[0:rows, q, :], XT[0:rows, q, :], RSTD[0:rows, q:q + 1], GB[0:rows, 1, :],
                                                 ALU.mult, ALU.add).then_inc(xt_ready, 1)
                        if which != 4 and t >= 1:
                            low(st["back"] + t - 1, *g.tiles[t - 1])
                    if which != 4:
                        low(st["back"] + len(g.tiles) - 1, *g.tiles[-1])
                elif name == "mix":
                    if g.sample:
                        link(dve.memset(UB[:, 0:2], 0.0))
                    for j, (kind, i, _, m) in enumerate(MIX_TILES):
                        n = n0 + j
                        q = KC * g.index + i
                        ps = LIN[:, n % 2, :, :]
                        if kind == "c":
                            if g.sample:
                                if i:
                                    link(dve.memset(UB[:, 0:2], 0.0))
                                link(dve.tensor_copy(UB[:, 514:516], CPREV[:, i, :]))
                            else:
                                link(dve.tensor_copy(UB[:, 0:2], TAILP[:, i, :]))
                            dve.wait_ge(product, n + 1)
                            dve.wait_ge(product_read[(n - 1) % 2], (n - 1) // 2 + 1)
                            if g.sample:
                                dve.tensor_tensor(UB[:, 2:274], ps[:, 0, 0:272], HB[:, 0:272], ALU.mult)
                                dve.tensor_tensor(UB[:, 274:514], ps[:, 1, 0:240], HB[:, 272:512], ALU.mult)
                                last = dve.tensor_tensor(UB[:, 516:548], ps[:, 1, 240:272], HB[:, 512:544], ALU.mult)
                                wc = 546
                            else:
                                last = dve.tensor_tensor(UB[:, 2:514], ps[:, 0, 0:512], HB[:, 0:512], ALU.mult)
                                wc = 512
                            last.then_inc(product_read[n % 2], 1)
                            dve.wait_ge(product_read[n % 2], n // 2 + 1)
                            if g.sample:
                                dve.tensor_copy(TAILS[:, i, :], UB[:, 546:548])
                            dve.tensor_copy(TAILP[:, i, :], UB[:, 512:514])
                            link(dve.tensor_scalar(CB[:, 0:wc], UB[:, 0:wc], CW[:, 0, i:i + 1], None, ALU.mult))
                            for tap in (1, 2):
                                link(dve.scalar_tensor_tensor(CB[:, 0:wc], UB[:, tap:tap + wc], CW[:, tap, i:i + 1],
                                                              CB[:, 0:wc], ALU.mult, ALU.add))
                        elif kind == "b":
                            dve.wait_ge(product, n + 1)
                            if g.sample:
                                dve.tensor_tensor(HB[:, 0:272], ps[:, 0, 0:272], CB[:, 0:272], ALU.mult)
                                dve.tensor_tensor(HB[:, 272:512], ps[:, 1, 0:240], CB[:, 272:512], ALU.mult)
                                last = dve.tensor_tensor(HB[:, 512:544], ps[:, 1, 240:272], CB[:, 514:546], ALU.mult)
                            else:
                                last = dve.tensor_tensor(HB[:, 0:512], ps[:, 0, 0:512], CB[:, 0:512], ALU.mult)
                            last.then_inc(product_read[n % 2], 1)
                            dve.wait_ge(yc_hi, q + 1)
                            dve.tensor_tensor(YCL[:, i, 0:g.cols], HB[:, 0:g.cols], YCH[:, i, 0:g.cols].bitcast(F32),
                                              ALU.subtract).then_inc(yc_lo, 1)
                elif name == "idx":
                    for t, rows, keys, _ in score_tiles(g):
                        at_ = SCORE_AT[(g.index, t)]
                        for k0 in range(0, keys, 512):
                            w = min(512, keys - k0)
                            sc = SC[0:rows, at_ + k0:at_ + k0 + w]
                            for h in range(HEADS):
                                k = base["idx"]
                                dve.wait_ge(relu_done, k + 1)
                                wt = WI[0:rows, t, h:h + 1]
                                if h == 0:
                                    ins_ = dve.tensor_scalar(sc, RB[0:rows, k % 4, 0:w], wt, None, ALU.mult)
                                else:
                                    dve.wait_ge(idx_added, k)
                                    ins_ = dve.scalar_tensor_tensor(sc, RB[0:rows, k % 4, 0:w], wt, sc, ALU.mult, ALU.add)
                                ins_.then_inc(idx_added, 1)
                                base["idx"] += 1
                        if rows == P:
                            dve.wait_ge(idx_added, base["idx"])
                            dve.memset(SC[0:CHUNK, at_ + keys - CHUNK:at_ + keys], CLOSED)
                elif name == "att":
                    s0, pt0, o0 = st["s"], st["pt"], st["o"]
                    jobs = att_jobs(g)

                    def peak(a):
                        t, col, rows, keys, kvg, hh = jobs[a]
                        q = a % 2
                        if (g.index, t) in SCORE_AT:
                            at_ = SCORE_AT[(g.index, t)]
                            mask = SC[0:rows, at_:at_ + keys]
                        else:
                            mask = DM[:, 256 - keys:256]
                        dve.wait_ge(s_done, s0 + a + 1)
                        if a >= 4:
                            dve.wait_ge(pt_done, pt0 + a - 3)
                        link(dve.tensor_tensor_reduce(
                            PR[0:rows, a % 4, 0:keys], LIN[0:rows, q, :, :].rearrange("p a b -> p (a b)")[:, 0:keys], mask,
                            1.0, -3.0e38, ALU.add, ALU.max, MX[0:rows, q, 0:1]))
                        dve.tensor_scalar(NM[0:rows, q, 0:1], MX[0:rows, q, 0:1], -ATT_SCALE, None, ALU.mult).then_inc(nm_ready, 1)

                    def out_lo(q):
                        t, col, rows, keys, kvg, _ = jobs[4 * q]
                        dve.wait_ge(o_hi, o0 + q + 1)
                        o = TR[:, 1, 512 * (q % 2):512 * (q % 2) + 2 * rows].rearrange("p (a b) -> p a b", a=2)
                        dve.tensor_tensor(HL[:, 4 + 2 * kvg:6 + 2 * kvg, col:col + rows], o,
                                          HH[:, 4 + 2 * kvg:6 + 2 * kvg, col:col + rows].bitcast(F32), ALU.subtract)\
                            .then_inc(o_lo, 1)

                    peak(0)
                    peak(1)
                    for a in range(len(jobs)):
                        t, col, rows, keys, kvg, hh = jobs[a]
                        q = a % 2
                        dve.wait_ge(exp_done, s0 + a + 1)
                        link(dve.reciprocal(RR[0:rows, q, 0:1], RS[0:rows, q, 0:1]))
                        dve.tensor_scalar(PR[0:rows, a % 4, 0:keys], PR[0:rows, a % 4, 0:keys], RR[0:rows, q, 0:1], None, ALU.mult)\
                            .then_inc(p_ready, 1)
                        if a + 2 < len(jobs):
                            peak(a + 2)
                        if a % 4 == 0 and a:
                            out_lo(a // 4 - 1)
                    out_lo(len(jobs) // 4 - 1)
                elif name in ("mixout", "memo"):
                    for j in range(8):
                        n = n0 + j
                        dve.wait_ge(product, n + 1)
                        y = g.folded(Y[:, j, 0:g.cols])
                        dve.tensor_tensor(y, LIN[:, n % 2, 0:g.parts, 0:g.width], y, ALU.add).then_inc(product_read[n % 2], 1)
                elif name == "mematt":
                    c = dict(s=st["s"], nm=st["s"], exp=st["s"], p=st["s"], pt=st["pt"], o=st["o"])

                    def norm(rows, q, hs):
                        link(dve.reciprocal(RR[0:rows, q, hs:hs + 1] if hs is not None else RR[:, q, :],
                                            RS[0:rows, q, hs:hs + 1] if hs is not None else RS[:, q, :]))
                        for h in range(4) if hs is None else [hs]:
                            last = dve.tensor_scalar(PM[0:rows, q, h, :], PM[0:rows, q, h, :], RR[0:rows, q, h:h + 1], None, ALU.mult)
                        last.then_inc(p_ready, 1)

                    for t in range(5):
                        if t < 4:
                            dve.wait_ge(s_done, c["s"] + t + 1)
                            if t >= 2:
                                dve.wait_ge(exp_done, c["exp"] + t - 1)
                                dve.wait_ge(pt_done, c["pt"] + t - 1)
                            link(dve.tensor_reduce(MX[:, t % 2, :], LIN[:, t % 2, :, :].rearrange("p a (b c) -> p (a b) c", b=2),
                                                   AX_X, ALU.max))
                            dve.tensor_scalar(NM[:, t % 2, :], MX[:, t % 2, :], -MEM_SCALE, None, ALU.mult).then_inc(nm_ready, 1)
                        if t >= 1:
                            dve.wait_ge(exp_done, c["exp"] + t)
                            norm(P, (t - 1) % 2, None)
                    for o in range(8):
                        dve.wait_ge(o_hi, c["o"] + o + 1)
                        dve.tensor_tensor(XL[:, o, 0:HALF], LIN[:, o % 2, 0, :], XH[:, o, 0:HALF].bitcast(F32), ALU.subtract)\
                            .then_inc(o_lo, 1)
                    if g.sample:
                        for h in range(4):
                            dve.wait_ge(s_done, c["s"] + 5 + h)
                            link(dve.tensor_reduce(MX[0:DEC, 0, h:h + 1], LIN[0:DEC, 0, 0, 0:256], AX_X, ALU.max))
                            dve.tensor_scalar(NM[0:DEC, 0, h:h + 1], MX[0:DEC, 0, h:h + 1], -MEM_SCALE, None, ALU.mult).then_inc(nm_ready, 1)
                            dve.wait_ge(exp_done, c["exp"] + 5 + h)
                            norm(DEC, 0, h)
                            dve.wait_ge(o_hi, c["o"] + 9 + h)
                            dve.tensor_tensor(XL[:, 2 * h:2 * h + 2, HALF:HALF + DEC], LIN[:, 1, :, 0:DEC],
                                              XH[:, 2 * h:2 * h + 2, HALF:HALF + DEC].bitcast(F32), ALU.subtract).then_inc(o_lo, 1)
                dve.drain().then_inc(dve_end, 1)

        @block.gpsimd
        def _(pool):
            def begin(s):
                if s:
                    pool.wait_ge(pe_end, s)
                    pool.wait_ge(act_end, s)
                    pool.wait_ge(dve_end, s)

            def split_lo(i, n):
                if n >= NT:
                    return
                pool.wait_ge(hi_split, i * 4 + (n + 1))
                pool.tensor_tensor(WL[:, n % RING, :, :], WRAW[:, n % 2, :, :], WH[:, n % RING, :, :].bitcast(F32),
                                   ALU.subtract).then_inc(lo_split, 1)

            pool.memset(ident[:, :], 0.0).then_inc(consts, 1)
            pool.memset(DM[:, :], 0.0).then_inc(consts, 1)
            pool.wait_ge(consts, 2)
            pool.affine_select(out=ident[:, :], in_=ident[:, :], compare_op=ALU.not_equal, fill=1.0, base=0,
                               pattern=[[-1, P]], channel_multiplier=1).then_inc(consts, 1)
            pool.memset(DM[0:CHUNK, 256 - CHUNK:256], FAR).then_inc(masks, 1)
            pool.memset(MHALF[:, :], -0.5).then_inc(masks, 1)
            pool.wait_ge(masks, 2)
            moves = [0]

            def move(dst, src):
                pool.dma_start(dst, src).then_inc(spilled, 16)
                moves[0] += 16

            def all_moved():
                pool.wait_ge(spilled, moves[0])

            def reload_queries(g):
                move(QA[:, :, 0:g.cols], spill_q[g.index][:, :, 0:g.cols])

            for s, st in enumerate(STAGES):
                begin(s)
                name, g, n0, which = st["name"], st["g"], st["n"], st["which"]
                if s == 0:
                    for j in range(AHEAD):
                        split_lo(0, j)
                elif name == "idx":
                    move(spill_q[g.index][:, :, 0:g.cols], QX[:, 0:KC, 0:g.cols])
                    move(spill_y[g.index][:, :, 0:g.cols], Y[:, :, 0:g.cols])
                    move(spill_ch[g.index][:, :, 0:g.cols], YCH[:, :, 0:g.cols].bitcast(F32))
                    move(spill_cl[g.index][:, :, 0:g.cols], YCL[:, :, 0:g.cols].bitcast(F32))
                    if not g.sample:
                        reload_queries(GROUPS[0])
                    all_moved()
                elif name == "att":
                    move(Y[:, :, 0:g.cols], spill_y[g.index][:, :, 0:g.cols])
                    move(HH[:, 0:KC, 0:g.cols].bitcast(F32), spill_ch[g.index][:, :, 0:g.cols])
                    move(HL[:, 0:KC, 0:g.cols].bitcast(F32), spill_cl[g.index][:, :, 0:g.cols])
                    all_moved()
                elif name in ("memkv", "mix", "mixout", "memq", "memo"):
                    for j in range({"memkv": 16, "mix": len(MIX_TILES)}.get(name, 8)):
                        split_lo(0, n0 + j + AHEAD)
                elif name == "ffn":
                    n = n0
                    for part, (f0, nf) in enumerate(FFN_PARTS):
                        with pool.Fori(0, nf // 2) as i:
                            for f in range(2):
                                split_lo(i, n + 2 * f + AHEAD)
                                split_lo(i, n + 2 * f + 1 + AHEAD)
                                pool.wait_ge(product_read[(n + 1) % 2], half(i, n + 2 * f + 1) + 1)
                                pool.tensor_tensor(FP_[:, 0:g.cols], FG[:, 0, 0:g.cols], FG[:, 1, 0:g.cols], ALU.mult)\
                                    .then_inc(multiplied, 1)
                                pool.wait_ge(hidden_hi, i * 2 + (st["mult"] + f0 + f + 1))
                                pool.tensor_tensor(HL[:, bass.ds(i * 2 + f, 1), 0:g.cols].rearrange("p a b -> p (a b)"),
                                                   FP_[:, 0:g.cols],
                                                   HH[:, bass.ds(i * 2 + f, 1), 0:g.cols].rearrange("p a b -> p (a b)")
                                                   .bitcast(F32), ALU.subtract).then_inc(hidden_lo, 1)
                                pool.wait_ge(hidden_lo, i * 2 + (st["mult"] + f0 + f + 1))
                        n += 2 * nf

                        def down(i, n, d):
                            for j in range(4):
                                split_lo(i, n + j + AHEAD)
                                pool.wait_ge(product_read[(n + j) % 2], half(i, n + j) + 1)
                                y = Y[:, bass.ds(i * 4 + (d + j), 1), 0:g.cols].rearrange("p a b -> p (a b)")
                                pool.tensor_tensor(y, FG[:, j % 2, 0:g.cols], y, ALU.add).then_inc(added, 1)

                        if n + KD + AHEAD > NT:
                            for k in range(KD // 4):
                                down(0, n + 4 * k, 4 * k)
                        else:
                            with pool.Fori(0, KD // 4) as i:
                                down(i, n, 0)
                        n += KD
                elif name == "ln":
                    if which == 4 and g.sample:
                        reload_queries(GROUPS[1])
                    for t, (col, rows) in enumerate(g.tiles):
                        k = st["fwd"] + t
                        pool.wait_ge(var_ready, k + 1)
                        pool.tensor_tensor(RSTD[0:rows, t % 2:t % 2 + 1], VE[0:rows, t % 2:t % 2 + 1], MHALF[0:rows, :], ALU.pow)\
                            .then_inc(rstd_ready, 1)
                    all_moved()
                pool.drain().then_inc(pool_end, 1)


_INS = ["x_prompt", "x_sample", "cache_conv", "cache_k", "cache_v", "cache_idx_k", "cache_mem_k", "cache_mem_v",
        "mem_prompt", "ffn1_gate", "ffn1_up", "ffn1_down", "ln1_g", "ln1_b", "w_mix_in", "conv_w", "w_mix_out",
        "ln2_g", "ln2_b", "w_mem_q", "w_mem_k", "w_mem_v", "w_mem_o", "ln3_g", "ln3_b",
        "ffn2_gate", "ffn2_up", "ffn2_down", "ln4_g", "ln4_b"]
_OUTS = [("y_prompt", (1, SEQ, D)), ("y_sample", (1, DEC, D)), ("conv_prompt", (1, 1, 2, DCONV)),
         ("k_prompt", (1, 1, SEQ, 2, DH)), ("v_prompt", (1, 1, SEQ, 2, DH)), ("ik_prompt", (1, 1, SEQ, DH)),
         ("mem_k", (1, 1, N_MEM, 4, 256)), ("mem_v", (1, 1, N_MEM, 4, 256)), ("conv_sample", (1, 1, 2, DCONV)),
         ("k_sample", (1, 1, DEC, 2, DH)), ("v_sample", (1, 1, DEC, 2, DH)), ("ik_sample", (1, 1, DEC, DH))]


def kernel(**inputs):
    import numpy as _np
    import concourse.bacc as _bacc
    from concourse.bass_utils import run_bass_kernel_spmd as _run

    nc = _bacc.Bacc("TRN2", target_bir_lowering=False, num_devices=1)
    arrays, ins, outs = {}, {}, {}
    for name in _INS:
        a = _np.ascontiguousarray(inputs[name])
        arrays[f"in_{name}"] = a
        ins[name] = nc.dram_tensor(f"in_{name}", a.shape, mybir.dt.from_np(a.dtype), kind="ExternalInput").ap()
    for name, shape in _OUTS:
        outs[name] = nc.dram_tensor(f"out_{name}", shape, F32, kind="ExternalOutput").ap()
    encoder_step(nc, ins, outs)
    r = _run(nc, [arrays], core_ids=[0])
    return tuple(r.results[0][f"out_{name}"] for name, _ in _OUTS)
```

```python
from contextlib import ExitStack

import concourse.bass as bass
from concourse import mybir

F32 = mybir.dt.float32
F32R = mybir.dt.float32r
ALU = mybir.AluOpType
ACT = mybir.ActivationFunctionType
AX_X = mybir.AxisListType.X

P = 128
D = 1024
KD = D // P
F = 2816
SEQ = 1024
DEC = 32
PAST = 512
HALF = SEQ // 2
SKEYS = PAST + DEC
CHUNK = 64
DH = 64
HEADS = 8
N_MEM = 256
DCONV = 512
KC = DCONV // P
EPS = 1e-5
ALPHA = 2.0 ** 0.25
ATT_SCALE = DH ** -0.5
MEM_SCALE = 256.0 ** -0.5
WI_SCALE = (8 * 64) ** -0.5
TAKEN = -3.0e38
CLOSED = -2.0e38
CUT = -2.5e38
FAR = -1.0e30

DVE_LOW = [0, 7]
POOL_LOW = [1, 2, 3, 4, 5, 6]
MEAN_AT, POWER_AT = 0, 8

FFN_PARTS = [(0, 8), (8, 8), (16, 6)]
RING = 4
AHEAD = 3


class Group:
    def __init__(self, index):
        self.index = index
        self.sample = index == 0
        self.cols = HALF + (DEC if self.sample else 0)
        self.parts = 2 if self.sample else 1
        self.width = self.cols // self.parts
        self.tiles = [(128 * t, 128) for t in range(4)] + ([(HALF, DEC)] if self.sample else [])
        self.full_tiles = [128 * t for t in range(4)] + ([self.cols - P] if self.sample else [])

    def folded(self, ap):
        return ap.rearrange("p (a b) -> p a b", a=self.parts)


GROUPS = [Group(0), Group(1)]


class Memory:
    cols, parts, width = N_MEM, 1, N_MEM

    @staticmethod
    def folded(ap):
        return ap.rearrange("p (a b) -> p a b", a=1)


MEMORY = Memory()


def score_tiles(g):
    if g.sample:
        return [(2, 128, 384, 32), (3, 128, 512, 32), (4, DEC, SKEYS, (SKEYS // 4) // 8)]
    return [(t, 128, 128 * (5 + t), 32) for t in range(4)]


def att_tiles(g):
    out = []
    for t, (col, rows) in enumerate(g.tiles):
        out.append((t, col, rows, SKEYS if rows == DEC else 128 * (4 * g.index + t + 1)))
    return out


def key_chunks(keys):
    n = (keys + 511) // 512
    return [(k * (keys // n), keys // n) for k in range(n)]


def idx_jobs(g):
    chunks = [(t, rows, k0, w) for t, rows, keys, _ in score_tiles(g) for k0, w in key_chunks(keys)]
    return [(*chunk, h) for c in range(0, len(chunks), 2) for h in range(HEADS) for chunk in chunks[c:c + 2]]


SCORE_AT = {}
_at = 0
for _g in GROUPS:
    for _t, _r, _n, _k in score_tiles(_g):
        SCORE_AT[(_g.index, _t)] = _at
        _at += _n
SCORE_COLS = _at

OFF_H, OFF_B, OFF_C = 0, DCONV, 2 * DCONV
OFF_Q = 3 * DCONV
OFF_K = OFF_Q + 512
OFF_V = OFF_K + 128
OFF_QI = OFF_V + 128
OFF_KI = OFF_QI + 512
KIW = 72
MIX_TILES = [("kiw", 0, OFF_KI, KIW), ("k", 0, OFF_K, 128), ("v", 0, OFF_V, 128)]
MIX_TILES += [("qi", i, OFF_QI + P * i, P) for i in range(4)]
MIX_TILES += [("q", i, OFF_Q + P * i, P) for i in range(4)]
for _i in range(KC):
    MIX_TILES += [("h", _i, OFF_H + P * _i, P), ("c", _i, OFF_C + P * _i, P), ("b", _i, OFF_B + P * _i, P)]

FRONT = ["loadx", "ffn", "ln", "mix", "idx"]
BACK = ["att", "mixout", "ln", "memq", "mematt", "memo", "ln", "ffn", "ln"]


def schedule():
    plan = []
    for g in (0, 1):
        plan += [(s, g, 1 if s in ("ffn", "ln") else 0) for s in FRONT]
    plan.insert(1, ("memkv", None, 0))
    for g in (0, 1):
        which = {"ffn": iter([2]), "ln": iter([2, 3, 4])}
        plan += [(s, g, next(which[s]) if s in which else 0) for s in (BACK if g else BACK[:-1])]
    stages = []
    at = dict(n=0, p=0, norm=0, diag=0, back=0, fwd=0, s=0, pt=0, o=0, idx=0, tok=0, mult=0, half=0)
    for name, index, which in plan:
        g = GROUPS[index] if index is not None else None
        stages.append(dict(name=name, g=g, which=which, **at))
        tiles = len(g.tiles) if g else 0
        if name == "loadx":
            at["back"] += len(load_tiles(g))
        if name == "ln" and which != 4:
            at["norm"] += 1
            at["diag"] += tiles
        if name == "ln" and which == 4:
            at["fwd"] += tiles
        if name == "ffn" and which == 2 and not g.sample:
            at["fwd"] += len(GROUPS[0].tiles)
        if name == "ffn":
            at["mult"] += F // P
            at["half"] += KD * len(FFN_PARTS)
            at["n"] += 2 * (F // P) + KD * len(FFN_PARTS)
        if name == "memkv":
            at["n"] += 2 * KD
            at["pt"] += 7
        if name == "mix":
            at["n"] += len(MIX_TILES)
            at["tok"] += tiles
        if name in ("mixout", "memq", "memo"):
            at["n"] += KD
        if name == "idx":
            at["idx"] += len(idx_jobs(g))
        if name == "att":
            at["p"] += len(att_jobs(g))
            at["s"] += len(att_jobs(g))
            at["pt"] += len(att_jobs(g))
            at["o"] += len(att_jobs(g)) // 4
        if name == "mematt":
            at["s"] += tiles
            at["p"] += tiles
            at["pt"] += tiles
            at["o"] += 8 + g.sample
    return stages, at["n"]


def att_jobs(g):
    return [(t, col, rows, keys, kvg, hh) for t, col, rows, keys in att_tiles(g)
            for kvg in range(2) for hh in (0, 2, 1, 3)]


def load_tiles(g):
    rows0 = g.index * HALF
    memory = [("mem_prompt", t * P, P, t * P) for t in range(N_MEM // P)] if g.sample else []
    return memory + [("x_sample", 0, rows, col) if rows == DEC else ("x_prompt", rows0 + col, rows, col)
                     for col, rows in g.tiles]


def half(i, m):
    return i * 2 + m // 2


def encoder_step(nc, ins, outs):
    STAGES, NT = schedule()
    ctx = ExitStack()
    with ctx:
        at = [(nc.sbuf_base + 31) // 32 * 32]

        def region(size):
            start = at[0]
            at[0] += (size + 31) // 32 * 32
            return start

        def place(name, shape, dtype, offset):
            return nc.alloc_sbuf_tensor_at(name, shape, dtype, offset=offset)

        GC = 544
        r_xh = region(KD * GC * 4)
        r_xl = region(KD * GC * 4)
        r_hh = region(KD * GC * 4)
        r_hl = region(KD * GC * 4)
        r_y = region(KD * GC * 4)
        XH = place("XH", [P, KD, GC], F32R, r_xh)
        XL = place("XL", [P, KD, GC], F32R, r_xl)
        HH = place("HH", [P, KD, GC], F32R, r_hh)
        HL = place("HL", [P, KD, GC], F32R, r_hl)
        Y = place("Y", [P, KD, GC], F32, r_y)
        QX = place("QX", [P, KD, GC], F32, r_hh)
        YCH = place("YCH", [P, KC, GC], F32R, r_hl)
        YCL = place("YCL", [P, KC, GC], F32R, r_hl + KC * GC * 4)
        QIS = place("QIS", [P, HEADS, GC], F32R, r_xl)
        KIC = place("KIC", [P, 2, SEQ], F32R, r_xh + KC * GC * 4)
        KISC = place("KISC", [P, 2, SKEYS], F32R, r_xh)
        QA0 = place("QA0", [P, KC, GC], F32, r_xh)
        PT = place("PT", [P, 8, 4, P], F32, r_xl)
        QM = place("QM", [P, KD, GC], F32, r_hh)
        PTM = place("PTM", [P, 2, 4, GC], F32, r_hl)

        WRAW = place("WRAW", [P, 2, KD, P], F32, region(2 * D * 4))
        WH = place("WH", [P, RING, KD, P], F32R, region(RING * D * 4))
        WL = place("WL", [P, RING, KD, P], F32R, region(RING * D * 4))
        KPA = place("KPA", [P, SEQ], F32, region(SEQ * 4))
        KPB = place("KPB", [P, SEQ], F32, region(SEQ * 4))
        r_ks = region(SKEYS * 4)
        KSA = place("KSA", [P, SKEYS], F32, r_ks)
        MVS = place("MVS", [P, 2, D], F32, r_ks)
        QA1 = place("QA1", [P, KC, HALF], F32, r_ks)
        KSB = place("KSB", [P, SKEYS], F32, region(SKEYS * 4))
        r_kip = region(SEQ * 4)
        KIP = place("KIP", [P, SEQ], F32, r_kip)
        CK = place("CK", [P, 4, 192], F32, r_kip)
        KIS = place("KIS", [P, SKEYS], F32, region(SKEYS * 4))
        VP = place("VP", [P, 8, P], F32, region(SEQ * 4))
        VS = place("VS", [P, 5, P], F32, region(5 * P * 4))
        MKT = place("MKT", [P, KD, N_MEM], F32, region(KD * N_MEM * 4))
        MV = place("MV", [P, 2, D], F32, region(2 * D * 4))
        r_sc = region(SCORE_COLS * 4)
        SC = place("SC", [P, SCORE_COLS], F32, r_sc)
        r_t = region(16384)
        PR = place("PR", [P, 4, 1024], F32, r_t)
        YT = place("YT", [P, 2, KD, P], F32, r_sc)
        YOUT = place("YOUT", [P, 2, D], F32, r_sc + 8192)
        XT = place("XT", [P, 4, D], F32, r_t)
        GB = place("GB", [P, 2, D], F32, r_t + 8192)
        FG = place("FG", [P, 2, GC], F32, r_t)
        FP_ = place("FP", [P, GC], F32, r_t + 2 * GC * 4)
        CSUM = place("CSUM", [P, GC], F32, r_t + 3 * GC * 4)
        QSUM = place("QSUM", [P, GC], F32, r_t + 4 * GC * 4)
        SQ = place("SQ", [P, 2, GC], F32, r_t + 5 * GC * 4)
        DIAG = place("DIAG", [P, 5, P], F32, r_t)
        KVT = place("KVT", [P, 3, GC], F32, r_t)
        TOK = place("TOK", [P, 2, 328], F32, r_t + 3 * GC * 4)
        HB = place("HB", [P, GC], F32, r_t + 9152)
        UB = place("UB", [P, 548], F32, r_t + 9152 + 2176)
        CB = place("CB", [P, 548], F32, r_t + 9152 + 2176 + 2208)
        RB = place("RB", [P, 4, 512], F32, r_t + 4096)
        MKTOK = place("MKTOK", [P, 2, D], F32, r_t)
        MVT = place("MVT", [P, KD, N_MEM], F32, r_sc)
        CMKT = place("CMKT", [P, KD, N_MEM], F32, r_sc + 8192)
        CMK = place("CMK", [P, 2, D], F32, r_t + 8192)
        PM = place("PM", [P, 2, 4, N_MEM], F32, r_t)
        MKTS = place("MKTS", [P, KD, N_MEM], F32, r_t + 8192)

        ident = place("ident", [P, P], F32, region(512))
        MEAN1 = place("MEAN1", [P, P], F32, region(512))
        MEAN8 = place("MEAN8", [P, P], F32, region(512))
        MSQ = place("MSQ", [P, 5], F32, region(32))
        VAR = place("VAR", [P, 5], F32, region(32))
        INV = place("INV", [P, 5], F32, region(32))
        GCOL = place("GCOL", [P, 3, KD], F32, region(96))
        BCOL = place("BCOL", [P, 3, KD], F32, region(96))
        DM = place("DM", [P, 256], F32, region(1024))
        WI = place("WI", [P, 5, 8], F32, region(160))
        CW = place("CW", [P, 3, KC], F32, region(64))
        CPREV = place("CPREV", [P, KC, 2], F32, region(32))
        TAILP = place("TAILP", [P, KC, 2], F32, region(32))
        TAILS = place("TAILS", [P, KC, 2], F32, region(32))
        ST = place("ST", [P, 2, 12], F32, region(96))
        MVAR = place("MVAR", [P, 2, 2], F32, region(32))
        VE = place("VE", [P, 2], F32, region(32))
        RSTD = place("RSTD", [P, 2], F32, region(32))
        MHALF = place("MHALF", [P, 1], F32, region(32))
        M8 = place("M8", [P, 8], F32, region(32))
        MX = place("MX", [P, 2, 4], F32, region(32))
        NM = place("NM", [P, 2, 4], F32, region(32))
        RS = place("RS", [P, 2, 4], F32, region(32))
        RR = place("RR", [P, 2, 4], F32, region(32))
        assert at[0] <= nc.sbuf_usable_end, (at[0], nc.sbuf_usable_end)

        LIN = ctx.enter_context(nc.psum_tensor("LIN", [P, 2, 2, 512], F32))
        TR = ctx.enter_context(nc.psum_tensor("TR", [P, 2, 1024], F32))

        spill_q = [nc.dram_tensor(f"spill_q{i}", [P, KC, GC], F32, kind="Internal").ap() for i in range(2)]
        mem_keys = nc.dram_tensor("mem_keys", [P, KD, N_MEM], F32, kind="Internal").ap()
        spill_y = [nc.dram_tensor(f"spill_y{i}", [P, KD, GC], F32, kind="Internal").ap() for i in range(2)]
        spill_ch = [nc.dram_tensor(f"spill_ch{i}", [P, KC, GC], F32, kind="Internal").ap() for i in range(2)]
        spill_cl = [nc.dram_tensor(f"spill_cl{i}", [P, KC, GC], F32, kind="Internal").ap() for i in range(2)]

        def sem(name):
            return ctx.enter_context(nc.semaphore(name))

        raw_loaded = [sem(f"raw_loaded{i}") for i in range(2)]
        hi_split = sem("hi_split")
        lo_split = sem("lo_split")
        product = sem("product")
        product_read = [sem(f"product_read{i}") for i in range(2)]
        pe_end = sem("pe_end")
        act_end = sem("act_end")
        dve_end = sem("dve_end")
        pool_end = sem("pool_end")
        consts = sem("consts")
        masks = sem("masks")
        moved = sem("moved")
        spilled = sem("spilled")
        xt_loaded = [sem(f"xt_loaded{i}") for i in range(4)]
        xt_stored = [sem(f"xt_stored{i}") for i in range(2)]
        yt_loaded = [sem(f"yt_loaded{i}") for i in range(2)]
        yout_stored = [sem(f"yout_stored{i}") for i in range(2)]
        back_done = sem("back_done")
        back_hi = sem("back_hi")
        back_lo = sem("back_lo")
        fwd_done = sem("fwd_done")
        fwd_read = sem("fwd_read")
        shift_done = sem("shift_done")
        centred = sem("centred")
        squared = sem("squared")
        square_added = sem("square_added")
        moments_done = sem("moments_done")
        mean_done = sem("mean_done")
        spread_ready = sem("spread_ready")
        inv_ready = sem("inv_ready")
        diagonal = sem("diagonal")
        inv_done = sem("inv_done")
        normed = sem("normed")
        x_hi = sem("x_hi")
        x_lo = sem("x_lo")
        x_lo_dve = sem("x_lo_dve")
        var_ready = sem("var_ready")
        rstd_ready = sem("rstd_ready")
        xt_ready = sem("xt_ready")
        multiplied = sem("multiplied")
        hidden_hi = sem("hidden_hi")
        hidden_lo = sem("hidden_lo")
        added = sem("added")
        dve_step = sem("dve_step")
        tok_done = sem("tok_done")
        tok_read = sem("tok_read")
        tok_stored = [sem(f"tok_stored{i}") for i in range(2)]
        yc_hi = sem("yc_hi")
        yc_lo = sem("yc_lo")
        keys_hi = sem("keys_hi")
        keys_lo = sem("keys_lo")
        query_hi = sem("query_hi")
        query_lo = sem("query_lo")
        idx_done = sem("idx_done")
        relu_done = sem("relu_done")
        idx_added = sem("idx_added")
        s_done = sem("s_done")
        nm_ready = sem("nm_ready")
        exp_done = sem("exp_done")
        p_ready = sem("p_ready")
        pt_done = sem("pt_done")
        pt_read = sem("pt_read")
        o_done = sem("o_done")
        o_hi = sem("o_hi")
        o_lo = sem("o_lo")
        gb_loaded = sem("gb_loaded")
        ck_loaded = sem("ck_loaded")
        mem_loaded = sem("mem_loaded")

        block = ctx.enter_context(nc.Block())

        gate_w = [ins[f"ffn{k}_gate"][0].rearrange("(c p) f -> p c f", p=P) for k in (1, 2)]
        up_w = [ins[f"ffn{k}_up"][0].rearrange("(c p) f -> p c f", p=P) for k in (1, 2)]
        down_w = [ins[f"ffn{k}_down"][0].rearrange("(c p) d -> p c d", p=P) for k in (1, 2)]
        mix_w = ins["w_mix_in"][0].rearrange("(c p) f -> p c f", p=P)

        def square(name):
            return ins[name][0].rearrange("(c p) f -> p c f", p=P)

        def low_wait(engine, norm, j):
            if j in DVE_LOW:
                engine.wait_ge(x_lo_dve, len(DVE_LOW) * norm + DVE_LOW.index(j) + 1)
            else:
                engine.wait_ge(x_lo, len(POOL_LOW) * norm + POOL_LOW.index(j) + 1)

        def mean_of(g, slot):
            return TR[:, slot, :].rearrange("p (a b) -> p a b", a=2)[:, 0:g.parts, 0:g.width]

        @block.sync
        def _(sp):
            def load(i, m, src, nk=KD, cols=P):
                if m >= 2:
                    sp.wait_ge(lo_split, i * 4 + (m - 1))
                sp.dma_start(WRAW[:, m % 2, 0:nk, 0:cols], src).then_inc(raw_loaded[m % 2], 16)

            for st in STAGES:
                n0, name = st["n"], st["name"]
                if name == "memkv":
                    for j in range(16):
                        load(0, j, square(("w_mem_k", "w_mem_v")[j // 8])[:, :, bass.ts(j % 8, P)])
                elif name == "mix":
                    for j, (_, _, c0, m) in enumerate(MIX_TILES):
                        load(0, n0 + j, mix_w[:, :, c0:c0 + m], cols=m)
                elif name in ("mixout", "memq", "memo"):
                    w = square({"mixout": "w_mix_out", "memq": "w_mem_q", "memo": "w_mem_o"}[name])
                    for j in range(8):
                        load(0, n0 + j, w[:, :, bass.ts(j, P)])
                elif name == "ffn":
                    k = st["which"] - 1
                    n = n0
                    for f0, nf in FFN_PARTS:
                        with sp.Fori(0, nf // 2) as i:
                            for j in range(4):
                                w = (gate_w, up_w)[j % 2][k]
                                load(i, n + j, w[:, :, bass.ts(i * 2 + (f0 + j // 2), P)])
                        n += 2 * nf
                        with sp.Fori(0, KD // 4) as i:
                            for j in range(4):
                                load(i, n + j,
                                     down_w[k][:, f0:f0 + nf, bass.ts(i * 4 + j, P)], nk=nf)
                        n += KD

        @block.tensor
        def _(pe):
            def begin(s):
                if s and not (STAGES[s - 1]["name"] == "ln" and STAGES[s - 1]["which"] != 4):
                    pe.wait_ge(act_end, s)
                    pe.wait_ge(dve_end, s)
                    pe.wait_ge(pool_end, s)

            def norm_before(s):
                return STAGES[s - 1]["norm"] if s and STAGES[s - 1]["name"] == "ln" and STAGES[s - 1]["which"] != 4 \
                    else None

            def column_mean(g, slot, matrix, src):
                for a in range(g.parts):
                    last = pe.matmul(TR[:, slot, 512 * a:512 * a + g.width], matrix[:, :],
                                     src[:, a * g.width:(a + 1) * g.width], start=True, stop=True)
                return last

            def linear(g, i, n, nk, hi, lo, m=(P,), hidden=None, normal=None):
                for t in range(len(m)):
                    pe.wait_ge(lo_split, i * 4 + (n + t + 1))
                    pe.wait_ge(product_read[(n + t) % 2], half(i, n + t))
                for c in range(nk):
                    if hidden is not None:
                        pe.wait_ge(hidden_lo, hidden + c + 1)
                    if normal is not None:
                        low_wait(pe, normal, c)
                    for t, outputs in enumerate(m):
                        w, slot = (n + t) % RING, (n + t) % 2
                        for wt, x in ((WH, hi), (WH, lo), (WL, hi)):
                            for a in range(g.parts):
                                last = pe.matmul(LIN[0:outputs, slot, a, 0:g.width], wt[:, w, c, 0:outputs],
                                                 x[:, c, a * g.width:(a + 1) * g.width],
                                                 start=(c == 0 and wt is WH and x is hi),
                                                 stop=(c == nk - 1 and wt is WL))
                        if c == nk - 1:
                            last.then_inc(product, 1)

            def loads_of(b):
                loaded = [st["back"] + t for st in STAGES if st["name"] == "loadx" for t in range(len(load_tiles(st["g"])))]
                return sum(1 for x in loaded if x <= b and x % 4 == b % 4)

            def to_feature(b, rows, slot):
                if b >= 2:
                    pe.wait_ge(back_lo, b - 1)
                for d in range(KD):
                    last = pe.transpose(TR[:, b % 2, d * P:d * P + rows], XT[0:rows, slot, d * P:(d + 1) * P],
                                        ident[0:rows, 0:rows])
                last.then_inc(back_done, 1)

            for s, st in enumerate(STAGES):
                begin(s)
                name, g, n0 = st["name"], st["g"], st["n"]
                if s == 0:
                    pe.wait_ge(consts, 3)
                if name == "loadx":
                    for t, (_, _, rows, _) in enumerate(load_tiles(g)):
                        b = st["back"] + t
                        pe.wait_ge(xt_loaded[b % 4], 16 * loads_of(b))
                        to_feature(b, rows, b % 4)
                elif name == "memkv":
                    for j in range(16):
                        linear(MEMORY, 0, j, KD, HH, HL)
                    for k in range(4):
                        if k == 0:
                            pe.wait_ge(product_read[1], KD // 2)
                            pe.wait_ge(product_read[0], KD // 2)
                        if k == 2:
                            pe.wait_ge(product_read[1], KD)
                            pe.wait_ge(product_read[0], KD)
                            pe.wait_ge(pt_read, 1)
                        if k == 3:
                            pe.wait_ge(pt_read, 2)
                        src = MKT if k < 2 else MVT
                        for d in range(KD):
                            last = pe.transpose(TR[:, k % 2, d * P:(d + 1) * P], src[:, d, (k % 2) * P:(k % 2 + 1) * P],
                                                ident[:, :])
                        last.then_inc(pt_done, 1)
                    pe.wait_ge(ck_loaded, 48)
                    for k in range(2):
                        pe.wait_ge(pt_read, 3 + k)
                        for q in range(8):
                            d, b = 4 * k + q // 2, q % 2
                            last = pe.transpose(TR[:, k, q * P:(q + 1) * P], CMK[:, b, d * P:(d + 1) * P], ident[:, :])
                        last.then_inc(pt_done, 1)
                    pe.wait_ge(pt_read, 6)
                    for q in range(4):
                        pe.transpose(TR[:, 0, q * P:(q + 1) * P], CK[:, q, 0:P], ident[:, :])
                        last = pe.transpose(TR[0:64, 1, q * P:(q + 1) * P], CK[:, q, P:P + 64], ident[:, :])
                    last.then_inc(pt_done, 1)
                elif name == "ffn":
                    n = n0

                    def beside(t):
                        if st["which"] == 2 and not g.sample:
                            rows = GROUPS[0].tiles[t][1]
                            pe.wait_ge(yt_loaded[t % 2], 16 * (t // 2 + 1))
                            if t >= 2:
                                pe.wait_ge(fwd_read, t - 1)
                            for d in range(KD):
                                last = pe.transpose(TR[0:rows, t % 2, d * P:(d + 1) * P], YT[:, t % 2, d, 0:rows], ident[:, :])
                            last.then_inc(fwd_done, 1)

                    for part, (f0, nf) in enumerate(FFN_PARTS):
                        peeled = part == 0 and norm_before(s) is not None
                        if peeled:
                            linear(g, 0, n, KD, XH, XL, m=(P, P), normal=norm_before(s))
                            linear(g, 0, n + 2, KD, XH, XL)
                            linear(g, 0, n + 3, KD, XH, XL)
                        with pe.Fori(0, nf // 2 - peeled) as i:
                            for j in range(4):
                                linear(g, i, n + 4 * peeled + j, KD, XH, XL)
                        n += 2 * nf
                        beside(2 * part)
                        if part < len(FFN_PARTS) - 1 or st["which"] == 2:
                            with pe.Fori(0, KD // 4) as i:
                                for j in range(4):
                                    linear(g, i, n + j, nf, HH, HL, hidden=st["mult"] + f0)
                        else:
                            for j in range(KD):
                                linear(g, 0, n + j, nf, HH, HL, hidden=st["mult"] + f0)
                                if j == 1:
                                    pe.wait_ge(added, st["half"] + KD * part + 1)
                                    column_mean(g, 0, MEAN1, Y[:, 0, :]).then_inc(shift_done, 1)
                        if part < len(FFN_PARTS) - 1:
                            beside(2 * part + 1)
                        n += KD
                elif name == "ln" and st["which"] != 4:
                    column_mean(g, 1, MEAN8, CSUM).then_inc(mean_done, 1)
                    for t, col in enumerate(g.full_tiles):
                        for at_, sums in ((MEAN_AT, CSUM), (POWER_AT, QSUM)):
                            last = pe.matmul(LIN[:, 0, 0, at_ + t:at_ + t + 1], sums[:, col:col + P], MEAN8[:, 0:1],
                                             start=True, stop=True)
                    last.then_inc(moments_done, 1)
                    for t, (col, rows) in enumerate(g.tiles):
                        pe.wait_ge(diagonal, st["diag"] + t + 1)
                        last = pe.matmul(TR[:, 0, col:col + rows], MEAN1[:, :], DIAG[:, t, P - rows:P], start=True, stop=True)
                    last.then_inc(inv_done, 1)
                elif name == "ln":
                    for t, (col, rows) in enumerate(g.tiles):
                        if t >= 2:
                            pe.wait_ge(fwd_read, st["fwd"] + t - 1)
                        for d in range(KD):
                            last = pe.transpose(LIN[0:rows, t % 2, d // 4, (d % 4) * P:(d % 4 + 1) * P],
                                                Y[:, d, col:col + rows], ident[:, :])
                        last.then_inc(fwd_done, 1)
                elif name == "mix":
                    for j, (kind, i, _, m) in enumerate(MIX_TILES):
                        if j == 0:
                            linear(g, 0, n0, KD, XH, XL, (m, MIX_TILES[1][3]), normal=norm_before(s))
                        elif j >= 2:
                            linear(g, 0, n0 + j, KD, XH, XL, (m,))
                        if j == 10:
                            pe.wait_ge(product_read[(n0 + 1) % 2], (n0 + 1) // 2 + 1)
                            pe.wait_ge(product_read[n0 % 2], (n0 + 2) // 2 + 1)
                            for t, (col, rows) in enumerate(g.tiles):
                                k = st["tok"] + t
                                if k >= 2:
                                    pe.wait_ge(tok_read, k - 1)
                                pe.transpose(TR[0:rows, k % 2, 0:P], KVT[:, 1, col:col + rows], ident[:, :])
                                pe.transpose(TR[0:rows, k % 2, P:2 * P], KVT[:, 2, col:col + rows], ident[:, :])
                                pe.transpose(TR[0:rows, k % 2, 2 * P:2 * P + KIW], KVT[0:KIW, 0, col:col + rows],
                                             ident[0:KIW, 0:KIW]).then_inc(tok_done, 1)
                elif name == "idx":
                    for a, (t, rows, k0, w, h) in enumerate(idx_jobs(g)):
                        k = st["idx"] + a
                        kmat = KISC if rows == DEC else KIC
                        pe.wait_ge(keys_lo, 3 if not g.sample else 2 if rows == DEC else 1)
                        pe.wait_ge(query_lo, HEADS * g.index + h + 1)
                        if k >= 4:
                            pe.wait_ge(relu_done, k - 3)
                        for part in range(2):
                            last = pe.matmul(LIN[0:rows, (k % 4) // 2, k % 2, 0:w],
                                             QIS[:, h, g.tiles[t][0]:g.tiles[t][0] + rows],
                                             kmat[:, part, k0:k0 + w], start=(part == 0), stop=(part == 1))
                        last.then_inc(idx_done, 1)
                elif name == "att":
                    s0, pt0, o0 = st["s"], st["pt"], st["o"]
                    jobs = att_jobs(g)

                    def scores(a):
                        t, col, rows, keys, kvg, hh = jobs[a]
                        h, lo = 4 * kvg + hh, 64 * (hh % 2)
                        if a >= 2:
                            pe.wait_ge(nm_ready, s0 + a - 1)
                        same = (kvg == 0) == (lo == 0)
                        kmat = (KSA if same else KSB) if rows == DEC else (KPA if same else KPB)
                        for k0 in range(0, keys, 512):
                            w = min(512, keys - k0)
                            last = pe.matmul(LIN[0:rows, a % 2, k0 // 512, 0:w],
                                             (QA0 if g.sample else QA1)[lo:lo + 64, h // 2, col:col + rows],
                                             kmat[lo:lo + 64, k0:k0 + w], start=True, stop=True)
                        last.then_inc(s_done, 1)

                    def turn(a):
                        t, col, rows, keys, kvg, hh = jobs[a]
                        pe.wait_ge(p_ready, st["p"] + a + 1)
                        alone = keys > 512 or a and jobs[a - 1][3] > 512
                        if a >= 1 or pt0:
                            pe.wait_ge(pt_read, pt0 + a if alone else pt0 + max(a - 1, 0))
                        at_ = 512 * (a % 2) * (keys <= 512)
                        for kb in range(0, keys, P):
                            w = min(P, keys - kb)
                            last = pe.transpose(TR[0:w, 0, at_ + kb:at_ + kb + rows],
                                                PR[0:rows, a % 4, kb:kb + w], ident[0:rows, 0:rows])
                        last.then_inc(pt_done, 1)

                    def values(q):
                        t, col, rows, keys, kvg, _ = jobs[4 * q]
                        pe.wait_ge(pt_read, pt0 + 4 * q + 4)
                        if q >= 2:
                            pe.wait_ge(o_lo, o0 + q - 1)
                        vmat = VS if rows == DEC else VP
                        nb = (keys + P - 1) // P
                        for kb in range(nb):
                            w = min(P, keys - kb * P)
                            for odd in range(2):
                                last = pe.matmul(TR[64 * odd:64 * odd + 64, 1, 512 * (q % 2):512 * (q % 2) + 2 * rows]
                                                 .rearrange("p (a b) -> p a b", a=2),
                                                 vmat[0:w, kb, 64 * kvg:64 * kvg + 64],
                                                 PT[0:w, kb, 2 * odd:2 * odd + 2, 0:rows],
                                                 start=(kb == 0), stop=(kb == nb - 1))
                        last.then_inc(o_done, 1)

                    scores(0)
                    scores(1)
                    for a in range(len(jobs)):
                        if a + 2 < len(jobs):
                            scores(a + 2)
                        if a % 4 == 0 and a:
                            values(a // 4 - 1)
                        turn(a)
                    values(len(jobs) // 4 - 1)
                elif name in ("mixout", "memq", "memo"):
                    src = (HH, HL) if name == "mixout" else (XH, XL)
                    for j in range(8):
                        if name != "memq":
                            linear(g, 0, n0 + j, KD, *src)
                        elif j == 0:
                            linear(g, 0, n0, KD, *src, m=(P, P), normal=norm_before(s))
                        elif j >= 2:
                            linear(g, 0, n0 + j, KD, *src)
                        if j == 1 and name != "memq":
                            pe.wait_ge(product_read[n0 % 2], n0 // 2 + 1)
                            column_mean(g, 0, MEAN1, Y[:, 0, :]).then_inc(shift_done, 1)
                elif name == "mematt":
                    def scores(t):
                        col, rows = g.tiles[t]
                        kmat = MKTS if rows == DEC else MKT
                        if rows == DEC:
                            pe.wait_ge(mem_loaded, 32)
                        if t >= 2:
                            pe.wait_ge(exp_done, st["s"] + t - 1)
                        for h in range(4):
                            for e in range(2):
                                last = pe.matmul(LIN[0:rows, t % 2, h // 2, 256 * (h % 2):256 * (h % 2) + 256],
                                                 QM[:, 2 * h + e, col:col + rows], kmat[:, 2 * h + e, :],
                                                 start=(e == 0), stop=(e == 1))
                        last.then_inc(s_done, 1)

                    def turn(u):
                        rows = g.tiles[u][1]
                        pe.wait_ge(p_ready, st["p"] + u + 1)
                        if u >= 2:
                            pe.wait_ge(pt_read, st["pt"] + u - 1)
                        for q in range(8):
                            last = pe.transpose(TR[:, u % 2, q * P:q * P + rows],
                                                PM[0:rows, u % 2, q % 4, (q // 4) * P:(q // 4 + 1) * P],
                                                ident[0:rows, 0:rows])
                        last.then_inc(pt_done, 1)

                    scores(0)
                    scores(1)
                    for t in range(len(g.tiles)):
                        if t + 2 < len(g.tiles):
                            scores(t + 2)
                        turn(t)
                    pe.wait_ge(exp_done, st["s"] + len(g.tiles))
                    for o in range(8):
                        if o >= 2:
                            pe.wait_ge(o_lo, st["o"] + o - 1)
                        else:
                            pe.wait_ge(pt_read, st["pt"] + 4)
                        for mb in range(2):
                            last = pe.matmul(LIN[:, o % 2, 0, :], MV[:, mb, o * P:(o + 1) * P],
                                             PTM[:, mb, o // 2, 0:HALF], start=(mb == 0), stop=(mb == 1))
                        last.then_inc(o_done, 1)
                    if g.sample:
                        pe.wait_ge(pt_read, st["pt"] + 5)
                        for o in range(8):
                            for mb in range(2):
                                last = pe.matmul(LIN[:, 0, 1, o * DEC:(o + 1) * DEC], MVS[:, mb, o * P:(o + 1) * P],
                                                 PTM[:, mb, o // 2, HALF:HALF + DEC], start=(mb == 0), stop=(mb == 1))
                        last.then_inc(o_done, 1)
                pe.drain().then_inc(pe_end, 1)

        @block.scalar
        def _(act):
            moves = [0]

            def begin(s):
                if s:
                    act.wait_ge(pe_end, s)
                    act.wait_ge(dve_end, s)
                    act.wait_ge(pool_end, s)

            def move(dst, src):
                act.dma_start(dst, src).then_inc(moved, 16)
                moves[0] += 16

            def all_moved():
                act.wait_ge(moved, moves[0])

            def split_hi(i, n):
                if n >= NT:
                    return
                act.wait_ge(raw_loaded[n % 2], half(i, n) * 16 + 16)
                if n >= RING:
                    act.wait_ge(product, i * 4 + (n - RING + 1))
                act.activation(WH[:, n % RING, :, :], WRAW[:, n % 2, :, :], ACT.Copy).then_inc(hi_split, 1)

            def evac(g, i, n, dst, m=P, func=ACT.Copy, scale=1.0):
                act.wait_ge(product, i * 4 + (n + 1))
                return act.activation(g.folded(dst), LIN[0:m, n % 2, 0:g.parts, 0:g.width], func, scale=scale)

            def from_feature(b, col, rows, memory=False):
                act.wait_ge(back_done, b + 1)
                src = TR[:, b % 2, :].rearrange("p (d t) -> p d t", d=KD)[:, :, 0:rows]
                if memory:
                    act.activation(HH[:, :, col:col + rows], src, ACT.Copy).then_inc(back_hi, 1)
                    return
                act.activation(XH[:, :, col:col + rows], src, ACT.Copy)
                act.activation(Y[:, :, col:col + rows], src, ACT.Copy, scale=ALPHA).then_inc(back_hi, 1)

            def store_out(g, t, buf, stored):
                col, rows = g.tiles[t]
                row = g.index * HALF + col
                dst = outs["y_sample"][0] if rows == DEC else outs["y_prompt"][0, row:row + rows, :]
                act.dma_start(dst, buf[0:rows, t % 2, :]).then_inc(stored[t % 2], 16)

            def square(g, norm, j):
                act.wait_ge(centred, KD * norm + j + 1)
                if j >= 2:
                    act.wait_ge(square_added, (KD - 1) * norm + max(1, j - 2))
                act.activation(SQ[:, j % 2, 0:g.cols], Y[:, j, 0:g.cols], ACT.Square).then_inc(squared, 1)

            for s, st in enumerate(STAGES):
                begin(s)
                name, g, n0, which = st["name"], st["g"], st["n"], st["which"]
                if name == "loadx":
                    tiles = load_tiles(g)

                    def load_tile(t):
                        src, row, rows, _ = tiles[t]
                        b = st["back"] + t
                        act.dma_start(XT[0:rows, b % 4, :], ins[src][0, row:row + rows, :]).then_inc(xt_loaded[b % 4], 16)

                    for t in range(2 if s else 0, 4):
                        load_tile(t)
                    if s == 0:
                        for j in range(2):
                            split_hi(0, j)
                    for t, (src, _, rows, col) in enumerate(tiles):
                        from_feature(st["back"] + t, col, rows, src == "mem_prompt")
                        if t + 4 < len(tiles):
                            load_tile(t + 4)
                        if s == 0 and t == 4:
                            split_hi(0, 2)
                    all_moved()
                elif name == "memkv":
                    for j in range(16):
                        split_hi(0, j + AHEAD)
                        evac(MEMORY, 0, j, (MKT if j < KD else MVT)[:, j % KD, :]).then_inc(product_read[j % 2], 1)
                        if j == 4:
                            act.dma_start(CK[:, :, 0:P], ins["cache_k"][0, 0].rearrange("(q p) h d -> p q (h d)", p=P))\
                                .then_inc(ck_loaded, 16)
                            act.dma_start(CK[:, :, P:P + 64], ins["cache_idx_k"][0, 0].rearrange("(q p) d -> p q d", p=P))\
                                .then_inc(ck_loaded, 16)
                            act.dma_start(CMK[:, :, :], ins["cache_mem_k"][0, 0].rearrange("(b p) h d -> p b (h d)", p=P))\
                                .then_inc(ck_loaded, 16)
                            for i in range(4):
                                move(VS[:, i, :], ins["cache_v"][0, 0, i * P:(i + 1) * P].rearrange("p h d -> p (h d)"))
                        if 6 <= j < 9:
                            with nc.allow_non_contiguous_dma("small constants"):
                                k = j - 6
                                move(GCOL[:, k, :], ins[f"ln{k + 1}_g"][0].rearrange("(c p) -> p c", p=P))
                                move(BCOL[:, k, :], ins[f"ln{k + 1}_b"][0].rearrange("(c p) -> p c", p=P))
                        if 9 <= j < 9 + KC:
                            with nc.allow_non_contiguous_dma("small constants"):
                                i = j - 9
                                move(CW[:, :, i], ins["conv_w"][0, :, i * P:(i + 1) * P].rearrange("j p -> p j"))
                                move(CPREV[:, i, :], ins["cache_conv"][0, 0, :, i * P:(i + 1) * P].rearrange("r p -> p r"))
                    for k in range(4):
                        act.wait_ge(pt_done, k + 1)
                        act.activation((MKTOK if k < 2 else MV)[:, k % 2, :], TR[:, k % 2, :], ACT.Copy).then_inc(pt_read, 1)
                    act.wait_ge(pt_read, 4)
                    for buf, out in ((MKTOK, outs["mem_k"]), (MV, outs["mem_v"])):
                        move(out[0, 0].rearrange("(b p) h d -> p b (h d)", p=P), buf[:, :, :])
                    for k in range(2):
                        act.wait_ge(pt_done, k + 5)
                        act.activation(CMKT[:, 4 * k:4 * k + 4, :].rearrange("p a b -> p (a b)"), TR[:, k, :], ACT.Copy)\
                            .then_inc(pt_read, 1)
                    act.wait_ge(pt_read, 6)
                    move(mem_keys[:, :, :], CMKT[:, :, :])
                    act.wait_ge(pt_done, 7)
                    act.activation(KSA[:, 0:PAST], TR[:, 0, 0:PAST], ACT.Copy)
                    act.activation(KIS[0:64, 0:PAST], TR[0:64, 1, 0:PAST], ACT.Copy).then_inc(pt_read, 1)
                    act.wait_ge(pt_read, 7)
                    move(KSB[0:64, 0:PAST], KSA[64:128, 0:PAST])
                    move(KSB[64:128, 0:PAST], KSA[0:64, 0:PAST])
                    move(KIS[64:128, 0:PAST], KIS[0:64, 0:PAST])
                elif name == "ffn":
                    if which == 2 and not g.sample:
                        for r, nm in enumerate(("g", "b")):
                            act.dma_start(GB[:, r, :], ins[f"ln4_{nm}"][0:1, :].to_broadcast([P, D])).then_inc(gb_loaded, 16)
                    n = n0
                    late = which == 2 and not g.sample

                    def load_y(t):
                        if t >= 2:
                            act.wait_ge(fwd_done, t - 1)
                        col, rows = GROUPS[0].tiles[t]
                        act.dma_start(YT[:, t % 2, :, 0:rows], spill_y[0][:, :, col:col + rows]).then_inc(yt_loaded[t % 2], 16)

                    def store_y(t):
                        act.wait_ge(xt_ready, t + 1)
                        store_out(GROUPS[0], t, YOUT, yout_stored)

                    def beside(t):
                        if late:
                            store_y(t)
                            if t + 2 < len(GROUPS[0].tiles):
                                load_y(t + 2)

                    if late:
                        load_y(0)
                        load_y(1)
                    for part, (f0, nf) in enumerate(FFN_PARTS):
                        halves = st["half"] + KD * part
                        if halves:
                            act.wait_ge(added, halves)
                        else:
                            all_moved()

                        with act.Fori(0, nf // 2) as i:
                            for j in range(4):
                                split_hi(i, n + j + AHEAD)
                                evac(g, i, n + j, FG[:, j % 2, 0:g.cols], func=ACT.Copy if j % 2 else ACT.Silu)\
                                    .then_inc(product_read[(n + j) % 2], 1)
                                if j % 2:
                                    act.wait_ge(multiplied, i * 2 + (st["mult"] + f0 + j // 2 + 1))
                                    act.activation(HH[:, bass.ds(i * 2 + j // 2, 1), 0:g.cols].rearrange("p a b -> p (a b)"),
                                                   FP_[:, 0:g.cols], ACT.Copy).then_inc(hidden_hi, 1)
                        n += 2 * nf
                        if part:
                            beside(2 * part - 1)
                        centre = which == 1 and part == len(FFN_PARTS) - 1

                        def down(i, n, halves, j0=0):
                            for j in range(4):
                                split_hi(i, n + j + AHEAD)
                                if halves + j >= 2:
                                    act.wait_ge(added, i * 4 + (halves + j - 1))
                                evac(g, i, n + j, FG[:, j % 2, 0:g.cols], scale=0.5)\
                                    .then_inc(product_read[(n + j) % 2], 1)
                                if centre and j0 + j >= 1:
                                    square(g, st["norm"], j0 + j - 1)

                        if halves == 0 or n + KD + AHEAD > NT or centre:
                            for k in range(KD // 4):
                                down(0, n + 4 * k, halves + 4 * k, 4 * k)
                            if centre:
                                square(g, st["norm"], KD - 1)
                        else:
                            with act.Fori(0, KD // 4) as i:
                                down(i, n, halves)
                        n += KD
                        beside(2 * part)
                    if late:
                        for k in range(2):
                            act.wait_ge(yout_stored[k], 16 * ((len(GROUPS[0].tiles) + 1 - k) // 2))
                    all_moved()
                elif name == "ln" and which != 4:
                    norm = st["norm"]
                    for j in range(KD):
                        act.wait_ge(normed, KD * norm + j + 1)
                        act.activation(XH[:, j, 0:g.cols], Y[:, j, 0:g.cols], ACT.Copy).then_inc(x_hi, 1)
                    for j in range(KD // 2):
                        low_wait(act, norm, j)
                        act.activation(Y[:, j, 0:g.cols], Y[:, j, 0:g.cols], ACT.Copy, scale=ALPHA)
                elif name == "ln":
                    for t, (col, rows) in enumerate(g.tiles):
                        k = st["fwd"] + t
                        act.wait_ge(xt_ready, k + 1)
                        store_out(g, t, XT, xt_stored)
                    for k2 in range(2):
                        act.wait_ge(xt_stored[k2], 16 * ((len(g.tiles) + 1 - k2) // 2))
                elif name == "mix":
                    c0 = g.index * HALF
                    for j, (kind, i, _, m) in enumerate(MIX_TILES):
                        n = n0 + j
                        split_hi(0, n + AHEAD)
                        if kind in ("kiw", "k", "v"):
                            evac(g, 0, n, KVT[0:m, j, 0:g.cols], m).then_inc(product_read[n % 2], 1)
                            act.wait_ge(product_read[n % 2], n // 2 + 1)
                            if kind == "kiw":
                                for b in (0, 64):
                                    move(KIP[b:b + 64, c0:c0 + HALF], KVT[0:64, 0, 0:HALF])
                                    if g.sample:
                                        move(KIS[b:b + 64, PAST:SKEYS], KVT[0:64, 0, HALF:])
                            if kind == "k":
                                move(KPA[:, c0:c0 + HALF], KVT[:, 1, 0:HALF])
                                for b in (0, 64):
                                    move(KPB[b:b + 64, c0:c0 + HALF], KVT[64 - b:128 - b, 1, 0:HALF])
                                    if g.sample:
                                        move(KSB[b:b + 64, PAST:SKEYS], KVT[64 - b:128 - b, 1, HALF:])
                                if g.sample:
                                    move(KSA[:, PAST:SKEYS], KVT[:, 1, HALF:])
                        elif kind == "qi":
                            evac(g, 0, n, QX[:, 4 + i, 0:g.cols]).then_inc(product_read[n % 2], 1)
                        elif kind == "q":
                            evac(g, 0, n, QX[:, i, 0:g.cols]).then_inc(product_read[n % 2], 1)
                        elif kind == "h":
                            q = KC * g.index + i
                            if q >= 1:
                                act.wait_ge(yc_lo, q)
                            evac(g, 0, n, HB[:, 0:g.cols]).then_inc(product_read[n % 2], 1)
                        elif kind == "b":
                            q = KC * g.index + i
                            act.wait_ge(product_read[n % 2], n // 2 + 1)
                            act.activation(YCH[:, i, 0:g.cols], HB[:, 0:g.cols], ACT.Copy).then_inc(yc_hi, 1)
                        if j == 10:
                            for t, (col, rows) in enumerate(g.tiles):
                                k = st["tok"] + t
                                act.wait_ge(tok_done, k + 1)
                                if k >= 2:
                                    act.wait_ge(tok_stored[k % 2], 48 * (k // 2))
                                act.activation(TOK[0:rows, k % 2, :], TR[0:rows, k % 2, 0:328], ACT.Copy)
                                v = VS[0:rows, 4, :] if rows == DEC else VP[:, 4 * g.index + t, :]
                                act.activation(v, TR[0:rows, k % 2, P:2 * P], ACT.Copy)
                                act.activation(WI[0:rows, t, :], TR[0:rows, k % 2, 320:328], ACT.Copy, scale=WI_SCALE)\
                                    .then_inc(tok_read, 1)
                                act.wait_ge(tok_read, k + 1)
                                sfx = "sample" if rows == DEC else "prompt"
                                r0 = 0 if rows == DEC else c0 + col
                                act.dma_start(outs[f"k_{sfx}"][0, 0, r0:r0 + rows].rearrange("t h d -> t (h d)"),
                                              TOK[0:rows, k % 2, 0:P]).then_inc(tok_stored[k % 2], 16)
                                act.dma_start(outs[f"v_{sfx}"][0, 0, r0:r0 + rows].rearrange("t h d -> t (h d)"),
                                              TOK[0:rows, k % 2, P:2 * P]).then_inc(tok_stored[k % 2], 16)
                                act.dma_start(outs[f"ik_{sfx}"][0, 0, r0:r0 + rows],
                                              TOK[0:rows, k % 2, 2 * P:2 * P + 64]).then_inc(tok_stored[k % 2], 16)
                    k = st["tok"] + len(g.tiles)
                    act.wait_ge(tok_stored[0], 48 * ((k + 1) // 2))
                    act.wait_ge(tok_stored[1], 48 * (k // 2))
                    all_moved()
                elif name == "idx":
                    def query_high(h):
                        if h < HEADS:
                            lo = 64 * (h % 2)
                            act.activation(QIS[lo:lo + 64, h, c0:g.cols], QX[lo:lo + 64, 4 + h // 2, c0:g.cols], ACT.Copy)\
                                .then_inc(query_hi, 1)

                    c0 = g.tiles[score_tiles(g)[0][0]][0]
                    keys = HALF * (g.index + 1)
                    query_high(0)
                    act.activation(KIC[:, 0, 0:keys], KIP[:, 0:keys], ACT.Copy).then_inc(keys_hi, 1)
                    query_high(1)
                    if g.sample:
                        for t in range(2):
                            src, row, rows, _ = load_tiles(GROUPS[1])[t]
                            slot = (st["back"] + t) % 4
                            act.dma_start(XT[0:rows, slot, :], ins[src][0, row:row + rows, :]).then_inc(xt_loaded[slot], 16)
                    if g.sample:
                        act.activation(KISC[:, 0, :], KIS[:, :], ACT.Copy).then_inc(keys_hi, 1)
                    for a, (t, rows, k0, w, h) in enumerate(idx_jobs(g)):
                        k = st["idx"] + a
                        if a < 2 * HEADS and a % 2 == 0:
                            query_high(h + 2)
                        act.wait_ge(idx_done, k + 1)
                        if k >= 4:
                            act.wait_ge(idx_added, k - 3)
                        act.activation(RB[0:rows, k % 4, 0:w], LIN[0:rows, (k % 4) // 2, k % 2, 0:w],
                                       ACT.Relu).then_inc(relu_done, 1)
                    tail = "sample" if g.sample else "prompt"
                    with nc.allow_non_contiguous_dma("two rows of the conv input"):
                        for i in range(KC):
                            move(outs[f"conv_{tail}"][0, 0, :, i * P:(i + 1) * P].rearrange("r p -> p r"),
                                 (TAILS if g.sample else TAILP)[:, i, :])
                elif name == "att":
                    s0, pt0, o0 = st["s"], st["pt"], st["o"]
                    jobs = att_jobs(g)

                    def exponent(a):
                        t, col, rows, keys, kvg, hh = jobs[a]
                        q = a % 2
                        act.wait_ge(nm_ready, s0 + a + 1)
                        act.activation(PR[0:rows, a % 4, 0:keys], PR[0:rows, a % 4, 0:keys], ACT.Exp, bias=NM[0:rows, q, 0:1],
                                       scale=-1.0, accum_out=RS[0:rows, q, 0:1]).then_inc(exp_done, 1)

                    def out_hi(q):
                        t, col, rows, keys, kvg, _ = jobs[4 * q]
                        act.wait_ge(o_done, o0 + q + 1)
                        o = TR[:, 1, 512 * (q % 2):512 * (q % 2) + 2 * rows].rearrange("p (a b) -> p a b", a=2)
                        act.activation(HH[:, 4 + 2 * kvg:6 + 2 * kvg, col:col + rows], o, ACT.Copy).then_inc(o_hi, 1)

                    exponent(0)
                    for a in range(len(jobs)):
                        if a + 1 < len(jobs):
                            exponent(a + 1)
                        if a % 4 == 0 and a:
                            out_hi(a // 4 - 1)
                        t, col, rows, keys, kvg, hh = jobs[a]
                        act.wait_ge(pt_done, pt0 + a + 1)
                        slot = (0, 2, 1, 3)[hh]
                        full = keys // P
                        src = TR[:, 0, 512 * (a % 2) * (keys <= 512):].rearrange("p (k q) -> p k q", q=P)
                        last = act.activation(PT[:, 0:full, slot, 0:rows], src[:, 0:full, 0:rows], ACT.Copy)
                        if keys % P:
                            last = act.activation(PT[0:keys % P, full, slot, 0:rows], src[0:keys % P, full, 0:rows], ACT.Copy)
                        last.then_inc(pt_read, 1)
                    out_hi(len(jobs) // 4 - 1)
                    all_moved()
                elif name in ("mixout", "memo"):
                    for j in range(8):
                        split_hi(0, n0 + j + AHEAD)
                        if j >= 1:
                            square(g, st["norm"], j - 1)
                    square(g, st["norm"], KD - 1)
                elif name == "memq":
                    if g.sample:
                        act.dma_start(MKTS[:, :, :], mem_keys[:, :, :]).then_inc(mem_loaded, 16)
                        act.dma_start(MVS[:, :, :], ins["cache_mem_v"][0, 0].rearrange("(b p) h d -> p b (h d)", p=P))\
                            .then_inc(mem_loaded, 16)
                    for j in range(8):
                        n = n0 + j
                        split_hi(0, n + AHEAD)
                        evac(g, 0, n, QM[:, j, 0:g.cols]).then_inc(product_read[n % 2], 1)
                elif name == "mematt":

                    def exponent(t):
                        rows = g.tiles[t][1]
                        act.wait_ge(nm_ready, st["s"] + t + 1)
                        for h in range(4):
                            last = act.activation(PM[0:rows, t % 2, h, :],
                                                  LIN[0:rows, t % 2, h // 2, 256 * (h % 2):256 * (h % 2) + 256],
                                                  ACT.Exp, bias=NM[0:rows, t % 2, h:h + 1], scale=MEM_SCALE,
                                                  accum_out=RS[0:rows, t % 2, h:h + 1])
                        last.then_inc(exp_done, 1)

                    exponent(0)
                    exponent(1)
                    for t, (col, rows) in enumerate(g.tiles):
                        act.wait_ge(pt_done, st["pt"] + t + 1)
                        act.activation(PTM[:, :, :, col:col + rows].rearrange("p a b q -> p (a b) q"),
                                       TR[:, t % 2, :].rearrange("p (k q) -> p k q", k=8)[:, :, 0:rows], ACT.Copy)\
                            .then_inc(pt_read, 1)
                        if t + 2 < len(g.tiles):
                            exponent(t + 2)
                    for o in range(8):
                        act.wait_ge(o_done, st["o"] + o + 1)
                        act.activation(XH[:, o, 0:HALF], LIN[:, o % 2, 0, :], ACT.Copy).then_inc(o_hi, 1)
                    if g.sample:
                        act.wait_ge(o_done, st["o"] + 9)
                        act.activation(XH[:, :, HALF:HALF + DEC], LIN[:, 0, 1, 0:KD * DEC].rearrange("p (o t) -> p o t", o=KD),
                                       ACT.Copy).then_inc(o_hi, 1)
                act.drain().then_inc(act_end, 1)

        @block.vector
        def _(dve):
            steps = [0]

            def begin(s):
                if s:
                    dve.wait_ge(pe_end, s)
                    dve.wait_ge(act_end, s)
                    dve.wait_ge(pool_end, s)

            def link(ins_):
                steps[0] += 1
                ins_.then_inc(dve_step, 1)
                dve.wait_ge(dve_step, steps[0])

            def low(b, col, rows, memory=False):
                dve.wait_ge(back_hi, b + 1)
                src = TR[:, b % 2, :].rearrange("p (d t) -> p d t", d=KD)[:, :, 0:rows]
                hi, lo = (HH, HL) if memory else (XH, XL)
                dve.tensor_tensor(lo[:, :, col:col + rows], src, hi[:, :, col:col + rows].bitcast(F32), ALU.subtract)\
                    .then_inc(back_lo, 1)

            def select(g):
                for t, rows, keys, rounds in score_tiles(g):
                    at_ = SCORE_AT[(g.index, t)]
                    sc = SC[0:rows, at_:at_ + keys]
                    with dve.Fori(0, rounds):
                        dve.max(M8[0:rows, :], sc)
                        dve.drain()
                        dve.match_replace(sc, M8[0:rows, :], sc, TAKEN)
                        dve.drain()
                    dve.tensor_scalar(sc, sc, CUT, FAR, ALU.is_gt, ALU.mult)

            def after(ins_):
                steps[0] += 1
                ins_.then_inc(dve_step, 1)
                return steps[0]

            def final_norm(k, t, rows, src, buf, stored):
                q = t % 2
                dve.wait_ge(fwd_done, k + 1)
                for h in range(2):
                    last = dve.bn_stats(ST[0:rows, q, 6 * h:6 * h + 6], src[:, 512 * h:512 * h + 512])
                link(last)
                link(dve.bn_aggr(MVAR[0:rows, q, :], ST[0:rows, q, :]))
                dve.tensor_scalar(VE[0:rows, q:q + 1], MVAR[0:rows, q, 1:2], EPS, None, ALU.add).then_inc(var_ready, 1)
                if t >= 2:
                    dve.wait_ge(stored[q], 16 * (t // 2))
                dve.scalar_tensor_tensor(buf[0:rows, q, :], src, MVAR[0:rows, q, 0:1], GB[0:rows, 0, :],
                                         ALU.subtract, ALU.mult).then_inc(fwd_read, 1)
                dve.wait_ge(fwd_read, k + 1)
                dve.wait_ge(rstd_ready, k + 1)
                dve.scalar_tensor_tensor(buf[0:rows, q, :], buf[0:rows, q, :], RSTD[0:rows, q:q + 1], GB[0:rows, 1, :],
                                         ALU.mult, ALU.add).then_inc(xt_ready, 1)

            def statistics(g, norm, whole):
                summed = 0
                for j in range(KD + 1):
                    if j >= 2:
                        k = j - 1
                        dve.wait_ge(squared, KD * norm + j)
                        if k >= 2:
                            dve.wait_ge(square_added, (KD - 1) * norm + k - 1)
                        before = SQ[:, 0, 0:g.cols] if k == 1 else QSUM[:, 0:g.cols]
                        dve.tensor_tensor(QSUM[:, 0:g.cols], before, SQ[:, k % 2, 0:g.cols], ALU.add)\
                            .then_inc(square_added, 1)
                    if j < KD:
                        whole(j)
                        if j == 0:
                            continue
                        if j == 1:
                            dve.wait_ge(shift_done, norm + 1)
                        for k in range(0 if j == 1 else j, j + 1):
                            y = Y[:, k, 0:g.cols]
                            dve.tensor_tensor(g.folded(y), g.folded(y), mean_of(g, 0), ALU.subtract).then_inc(centred, 1)
                    if j < KD:
                        dve.wait_ge(centred, KD * norm + j + 1)
                        if j >= 2:
                            dve.wait_ge(dve_step, summed)
                        before = Y[:, 0, 0:g.cols] if j == 1 else CSUM[:, 0:g.cols]
                        summed = after(dve.tensor_tensor(CSUM[:, 0:g.cols], before, Y[:, j, 0:g.cols], ALU.add))

            for s, st in enumerate(STAGES):
                begin(s)
                name, g, n0, which = st["name"], st["g"], st["n"], st["which"]
                if name == "memkv":
                    for j in range(16):
                        dve.wait_ge(hi_split, j + AHEAD + 1)
                        dve.tensor_tensor(WL[:, (j + AHEAD) % RING, :, :], WRAW[:, (j + AHEAD) % 2, :, :],
                                          WH[:, (j + AHEAD) % RING, :, :].bitcast(F32), ALU.subtract).then_inc(lo_split, 1)
                elif name == "loadx":
                    for t, (src, _, rows, col) in enumerate(load_tiles(g)):
                        low(st["back"] + t, col, rows, src == "mem_prompt")
                elif name == "ffn":
                    if which == 1 and g.index == 1:
                        select(GROUPS[0])
                    if which == 2 and g.index == 0:
                        select(GROUPS[1])
                    if which == 2 and g.index == 1:
                        dve.wait_ge(gb_loaded, 32)
                        for t, (_, rows) in enumerate(GROUPS[0].tiles):
                            final_norm(t, t, rows, TR[0:rows, t % 2, :], YOUT, yout_stored)
                    if which == 1:
                        last_part = st["half"] + KD * (len(FFN_PARTS) - 1)
                        statistics(g, st["norm"], lambda j: dve.wait_ge(added, last_part + j + 1))
                elif name == "ln" and which != 4:
                    norm = st["norm"]

                    def less_mean(j):
                        y = g.folded(Y[:, j, 0:g.cols])
                        return after(dve.tensor_tensor(y, y, mean_of(g, 1), ALU.subtract))

                    def low_part(j):
                        dve.wait_ge(x_hi, KD * norm + j + 1)
                        dve.tensor_tensor(XL[:, j, 0:g.cols], Y[:, j, 0:g.cols], XH[:, j, 0:g.cols].bitcast(F32),
                                          ALU.subtract).then_inc(x_lo_dve, 1)

                    def add_bias(j):
                        dve.wait_ge(dve_step, scaled[j])
                        dve.tensor_scalar(Y[:, j, 0:g.cols], Y[:, j, 0:g.cols], BCOL[:, which - 1, j:j + 1], None, ALU.add)\
                            .then_inc(normed, 1)

                    dve.wait_ge(mean_done, norm + 1)
                    less = [less_mean(j) for j in range(5)]
                    k = len(g.full_tiles)
                    mean, power = LIN[:, 0, 0, MEAN_AT:MEAN_AT + k], LIN[:, 0, 0, POWER_AT:POWER_AT + k]
                    dve.wait_ge(moments_done, norm + 1)
                    link(dve.tensor_copy(MSQ[:, 0:k], mean))
                    link(dve.tensor_tensor(MSQ[:, 0:k], MSQ[:, 0:k], MSQ[:, 0:k], ALU.mult))
                    link(dve.tensor_tensor(VAR[:, 0:k], power, MSQ[:, 0:k], ALU.subtract))
                    dve.tensor_scalar(VAR[:, 0:k], VAR[:, 0:k], 0.0, EPS, ALU.max, ALU.add).then_inc(spread_ready, 1)
                    less += [less_mean(5)]
                    dve.wait_ge(inv_ready, norm + 1)
                    for t in range(k):
                        dve.tensor_scalar(DIAG[:, t, :], ident[:, :], INV[:, t:t + 1], float(P), ALU.mult, ALU.mult)\
                            .then_inc(diagonal, 1)
                    less += [less_mean(j) for j in (6, 7)]
                    dve.wait_ge(inv_done, norm + 1)
                    scaled = []
                    for j in range(KD):
                        dve.wait_ge(dve_step, less[j])
                        y = Y[:, j, 0:g.cols]
                        scaled.append(after(dve.scalar_tensor_tensor(y, y, GCOL[:, which - 1, j:j + 1], TR[:, 0, 0:g.cols],
                                                                     ALU.mult, ALU.mult)))
                        if j == 1:
                            low_part(0)
                        if j <= 1:
                            add_bias(j)
                        elif j >= 3:
                            add_bias(j - 1)
                    add_bias(KD - 1)
                    low_part(KD - 1)
                    for j in range(KD // 2, KD):
                        low_wait(dve, norm, j)
                        dve.tensor_scalar(Y[:, j, 0:g.cols], Y[:, j, 0:g.cols], ALPHA, None, ALU.mult)
                elif name == "ln":
                    for t, (_, rows) in enumerate(g.tiles):
                        final_norm(st["fwd"] + t, t, rows, LIN[0:rows, t % 2, :, :].rearrange("p a b -> p (a b)"), XT, xt_stored)
                elif name == "mix":
                    if g.sample:
                        link(dve.memset(UB[:, 0:2], 0.0))
                    for j, (kind, i, _, m) in enumerate(MIX_TILES):
                        n = n0 + j
                        q = KC * g.index + i
                        ps = LIN[:, n % 2, :, :]
                        if kind == "c":
                            if g.sample:
                                if i:
                                    link(dve.memset(UB[:, 0:2], 0.0))
                                link(dve.tensor_copy(UB[:, 514:516], CPREV[:, i, :]))
                            else:
                                link(dve.tensor_copy(UB[:, 0:2], TAILP[:, i, :]))
                            dve.wait_ge(product, n + 1)
                            dve.wait_ge(product_read[(n - 1) % 2], (n - 1) // 2 + 1)
                            if g.sample:
                                dve.tensor_tensor(UB[:, 2:274], ps[:, 0, 0:272], HB[:, 0:272], ALU.mult)
                                dve.tensor_tensor(UB[:, 274:514], ps[:, 1, 0:240], HB[:, 272:512], ALU.mult)
                                last = dve.tensor_tensor(UB[:, 516:548], ps[:, 1, 240:272], HB[:, 512:544], ALU.mult)
                                wc = 546
                            else:
                                last = dve.tensor_tensor(UB[:, 2:514], ps[:, 0, 0:512], HB[:, 0:512], ALU.mult)
                                wc = 512
                            last.then_inc(product_read[n % 2], 1)
                            dve.wait_ge(product_read[n % 2], n // 2 + 1)
                            if g.sample:
                                dve.tensor_copy(TAILS[:, i, :], UB[:, 546:548])
                            dve.tensor_copy(TAILP[:, i, :], UB[:, 512:514])
                            link(dve.tensor_scalar(CB[:, 0:wc], UB[:, 0:wc], CW[:, 0, i:i + 1], None, ALU.mult))
                            for tap in (1, 2):
                                link(dve.scalar_tensor_tensor(CB[:, 0:wc], UB[:, tap:tap + wc], CW[:, tap, i:i + 1],
                                                              CB[:, 0:wc], ALU.mult, ALU.add))
                        elif kind == "b":
                            dve.wait_ge(product, n + 1)
                            if g.sample:
                                dve.tensor_tensor(HB[:, 0:272], ps[:, 0, 0:272], CB[:, 0:272], ALU.mult)
                                dve.tensor_tensor(HB[:, 272:512], ps[:, 1, 0:240], CB[:, 272:512], ALU.mult)
                                last = dve.tensor_tensor(HB[:, 512:544], ps[:, 1, 240:272], CB[:, 514:546], ALU.mult)
                            else:
                                last = dve.tensor_tensor(HB[:, 0:512], ps[:, 0, 0:512], CB[:, 0:512], ALU.mult)
                            last.then_inc(product_read[n % 2], 1)
                            dve.wait_ge(yc_hi, q + 1)
                            dve.tensor_tensor(YCL[:, i, 0:g.cols], HB[:, 0:g.cols], YCH[:, i, 0:g.cols].bitcast(F32),
                                              ALU.subtract).then_inc(yc_lo, 1)
                elif name == "idx":

                    def query_low(h):
                        if h < HEADS:
                            lo = 64 * (h % 2)
                            dve.wait_ge(query_hi, HEADS * g.index + h + 1)
                            dve.tensor_tensor(QIS[64 - lo:128 - lo, h, c0:g.cols], QX[lo:lo + 64, 4 + h // 2, c0:g.cols],
                                              QIS[lo:lo + 64, h, c0:g.cols].bitcast(F32), ALU.subtract).then_inc(query_lo, 1)

                    c0 = g.tiles[score_tiles(g)[0][0]][0]
                    keys = HALF * (g.index + 1)
                    query_low(0)
                    dve.wait_ge(keys_hi, 1 if g.sample else 3)
                    dve.tensor_tensor(KIC[:, 1, 0:keys], KIP[:, 0:keys], KIC[:, 0, 0:keys].bitcast(F32), ALU.subtract)\
                        .then_inc(keys_lo, 1)
                    query_low(1)
                    if g.sample:
                        dve.wait_ge(keys_hi, 2)
                        dve.tensor_tensor(KISC[:, 1, :], KIS[:, :], KISC[:, 0, :].bitcast(F32), ALU.subtract)\
                            .then_inc(keys_lo, 1)
                    for a, (t, rows, k0, w, h) in enumerate(idx_jobs(g)):
                        k = st["idx"] + a
                        if a < 2 * HEADS and a % 2 == 0:
                            query_low(h + 2)
                        sc = SC[0:rows, SCORE_AT[(g.index, t)] + k0:SCORE_AT[(g.index, t)] + k0 + w]
                        dve.wait_ge(relu_done, k + 1)
                        wt = WI[0:rows, t, h:h + 1]
                        if h == 0:
                            scores = dve.tensor_scalar(sc, RB[0:rows, k % 4, 0:w], wt, None, ALU.mult)
                        else:
                            dve.wait_ge(idx_added, k - 1)
                            scores = dve.scalar_tensor_tensor(sc, RB[0:rows, k % 4, 0:w], wt, sc, ALU.mult, ALU.add)
                        scores.then_inc(idx_added, 1)
                    dve.wait_ge(idx_added, st["idx"] + len(idx_jobs(g)))
                    for t, rows, keys, _ in score_tiles(g):
                        if rows == P:
                            dve.memset(SC[0:CHUNK, SCORE_AT[(g.index, t)] + keys - CHUNK:SCORE_AT[(g.index, t)] + keys], CLOSED)
                elif name == "att":
                    s0, pt0, o0 = st["s"], st["pt"], st["o"]
                    jobs = att_jobs(g)

                    def peak(a):
                        t, col, rows, keys, kvg, hh = jobs[a]
                        q = a % 2
                        if (g.index, t) in SCORE_AT:
                            at_ = SCORE_AT[(g.index, t)]
                            mask = SC[0:rows, at_:at_ + keys]
                        else:
                            mask = DM[:, 256 - keys:256]
                        dve.wait_ge(s_done, s0 + a + 1)
                        if a >= 4:
                            dve.wait_ge(pt_done, pt0 + a - 3)
                        dve.tensor_tensor_reduce(
                            PR[0:rows, a % 4, 0:keys], LIN[0:rows, q, :, :].rearrange("p a b -> p (a b)")[:, 0:keys], mask,
                            -ATT_SCALE, 3.0e38, ALU.add, ALU.min, NM[0:rows, q, 0:1]).then_inc(nm_ready, 1)

                    def out_lo(q):
                        t, col, rows, keys, kvg, _ = jobs[4 * q]
                        dve.wait_ge(o_hi, o0 + q + 1)
                        o = TR[:, 1, 512 * (q % 2):512 * (q % 2) + 2 * rows].rearrange("p (a b) -> p a b", a=2)
                        dve.tensor_tensor(HL[:, 4 + 2 * kvg:6 + 2 * kvg, col:col + rows], o,
                                          HH[:, 4 + 2 * kvg:6 + 2 * kvg, col:col + rows].bitcast(F32), ALU.subtract)\
                            .then_inc(o_lo, 1)

                    peak(0)
                    peak(1)
                    for a in range(len(jobs)):
                        t, col, rows, keys, kvg, hh = jobs[a]
                        q = a % 2
                        dve.wait_ge(exp_done, s0 + a + 1)
                        link(dve.reciprocal(RR[0:rows, q, 0:1], RS[0:rows, q, 0:1]))
                        dve.tensor_scalar(PR[0:rows, a % 4, 0:keys], PR[0:rows, a % 4, 0:keys], RR[0:rows, q, 0:1], None, ALU.mult)\
                            .then_inc(p_ready, 1)
                        if a + 2 < len(jobs):
                            peak(a + 2)
                        if a % 4 == 0 and a:
                            out_lo(a // 4 - 1)
                    out_lo(len(jobs) // 4 - 1)
                elif name in ("mixout", "memo"):
                    def add_product(j):
                        n = n0 + j
                        dve.wait_ge(product, n + 1)
                        y = g.folded(Y[:, j, 0:g.cols])
                        dve.tensor_tensor(y, LIN[:, n % 2, 0:g.parts, 0:g.width], y, ALU.add).then_inc(product_read[n % 2], 1)
                        dve.wait_ge(product_read[n % 2], n // 2 + 1)

                    statistics(g, st["norm"], add_product)
                elif name == "mematt":

                    def peaks(t):
                        rows = g.tiles[t][1]
                        dve.wait_ge(s_done, st["s"] + t + 1)
                        if t >= 2:
                            dve.wait_ge(exp_done, st["s"] + t - 1)
                        link(dve.tensor_reduce(MX[0:rows, t % 2, :],
                                               LIN[0:rows, t % 2, :, :].rearrange("p a (b c) -> p (a b) c", b=2), AX_X, ALU.max))
                        dve.tensor_scalar(NM[0:rows, t % 2, :], MX[0:rows, t % 2, :], -MEM_SCALE, None, ALU.mult).then_inc(nm_ready, 1)

                    peaks(0)
                    peaks(1)
                    for t, (_, rows) in enumerate(g.tiles):
                        dve.wait_ge(exp_done, st["s"] + t + 1)
                        link(dve.reciprocal(RR[0:rows, t % 2, :], RS[0:rows, t % 2, :]))
                        for h in range(4):
                            last = dve.tensor_scalar(PM[0:rows, t % 2, h, :], PM[0:rows, t % 2, h, :], RR[0:rows, t % 2, h:h + 1],
                                                     None, ALU.mult)
                        last.then_inc(p_ready, 1)
                        if t + 2 < len(g.tiles):
                            peaks(t + 2)
                    for o in range(8):
                        dve.wait_ge(o_hi, st["o"] + o + 1)
                        dve.tensor_tensor(XL[:, o, 0:HALF], LIN[:, o % 2, 0, :], XH[:, o, 0:HALF].bitcast(F32), ALU.subtract)\
                            .then_inc(o_lo, 1)
                    if g.sample:
                        dve.wait_ge(o_hi, st["o"] + 9)
                        dve.tensor_tensor(XL[:, :, HALF:HALF + DEC], LIN[:, 0, 1, 0:KD * DEC].rearrange("p (o t) -> p o t", o=KD),
                                          XH[:, :, HALF:HALF + DEC].bitcast(F32), ALU.subtract).then_inc(o_lo, 1)
                dve.drain().then_inc(dve_end, 1)

        @block.gpsimd
        def _(pool):
            def begin(s):
                if s:
                    pool.wait_ge(pe_end, s)
                    pool.wait_ge(act_end, s)
                    pool.wait_ge(dve_end, s)

            def split_lo(i, n):
                if n >= NT:
                    return
                pool.wait_ge(hi_split, i * 4 + (n + 1))
                pool.tensor_tensor(WL[:, n % RING, :, :], WRAW[:, n % 2, :, :], WH[:, n % RING, :, :].bitcast(F32),
                                   ALU.subtract).then_inc(lo_split, 1)

            pool.memset(ident[:, :], 0.0).then_inc(consts, 1)
            pool.memset(DM[:, :], 0.0).then_inc(consts, 1)
            pool.wait_ge(consts, 2)
            pool.affine_select(out=ident[:, :], in_=ident[:, :], compare_op=ALU.not_equal, fill=1.0, base=0,
                               pattern=[[-1, P]], channel_multiplier=1).then_inc(consts, 1)
            pool.memset(DM[0:CHUNK, 256 - CHUNK:256], FAR).then_inc(masks, 1)
            pool.memset(MHALF[:, :], -0.5).then_inc(masks, 1)
            pool.memset(MEAN1[:, :], 1.0 / P).then_inc(masks, 1)
            pool.memset(MEAN8[:, :], 1.0 / D).then_inc(masks, 1)
            pool.wait_ge(masks, 4)
            moves = [0]

            def move(dst, src):
                pool.dma_start(dst, src).then_inc(spilled, 16)
                moves[0] += 16

            def all_moved():
                pool.wait_ge(spilled, moves[0])

            def root(k, t, rows):
                pool.wait_ge(var_ready, k + 1)
                pool.tensor_tensor(RSTD[0:rows, t % 2:t % 2 + 1], VE[0:rows, t % 2:t % 2 + 1], MHALF[0:rows, :], ALU.pow)\
                    .then_inc(rstd_ready, 1)

            def reload_queries(g):
                move((QA0 if g.sample else QA1)[:, :, 0:g.cols], spill_q[g.index][:, :, 0:g.cols])

            for s, st in enumerate(STAGES):
                begin(s)
                name, g, n0, which = st["name"], st["g"], st["n"], st["which"]
                if s == 0:
                    for j in range(AHEAD):
                        split_lo(0, j)
                elif name == "idx":
                    move(spill_q[g.index][:, :, 0:g.cols], QX[:, 0:KC, 0:g.cols])
                    move(spill_y[g.index][:, :, 0:g.cols], Y[:, :, 0:g.cols])
                    move(spill_ch[g.index][:, :, 0:g.cols], YCH[:, :, 0:g.cols].bitcast(F32))
                    move(spill_cl[g.index][:, :, 0:g.cols], YCL[:, :, 0:g.cols].bitcast(F32))
                    if not g.sample:
                        reload_queries(GROUPS[0])
                    all_moved()
                elif name == "att":
                    if not g.sample:
                        move(spill_y[0][:, :, 0:GC], Y[:, :, 0:GC])
                        all_moved()
                    move(Y[:, :, 0:g.cols], spill_y[g.index][:, :, 0:g.cols])
                    move(HH[:, 0:KC, 0:g.cols].bitcast(F32), spill_ch[g.index][:, :, 0:g.cols])
                    move(HL[:, 0:KC, 0:g.cols].bitcast(F32), spill_cl[g.index][:, :, 0:g.cols])
                    all_moved()
                elif name in ("mix", "mixout", "memq", "memo"):
                    for j in range(len(MIX_TILES) if name == "mix" else 8):
                        split_lo(0, n0 + j + AHEAD)
                elif name == "ffn":
                    n = n0
                    if which == 2 and g.sample:
                        reload_queries(GROUPS[1])

                    def beside(t):
                        if which == 2 and not g.sample:
                            root(t, t, GROUPS[0].tiles[t][1])

                    for part, (f0, nf) in enumerate(FFN_PARTS):
                        with pool.Fori(0, nf // 2) as i:
                            for f in range(2):
                                split_lo(i, n + 2 * f + AHEAD)
                                split_lo(i, n + 2 * f + 1 + AHEAD)
                                pool.wait_ge(product_read[(n + 1) % 2], half(i, n + 2 * f + 1) + 1)
                                pool.tensor_tensor(FP_[:, 0:g.cols], FG[:, 0, 0:g.cols], FG[:, 1, 0:g.cols], ALU.mult)\
                                    .then_inc(multiplied, 1)
                                pool.wait_ge(hidden_hi, i * 2 + (st["mult"] + f0 + f + 1))
                                pool.tensor_tensor(HL[:, bass.ds(i * 2 + f, 1), 0:g.cols].rearrange("p a b -> p (a b)"),
                                                   FP_[:, 0:g.cols],
                                                   HH[:, bass.ds(i * 2 + f, 1), 0:g.cols].rearrange("p a b -> p (a b)")
                                                   .bitcast(F32), ALU.subtract).then_inc(hidden_lo, 1)
                                pool.wait_ge(hidden_lo, i * 2 + (st["mult"] + f0 + f + 1))
                        n += 2 * nf
                        beside(2 * part)

                        def down(i, n, d):
                            for j in range(4):
                                split_lo(i, n + j + AHEAD)
                                pool.wait_ge(product_read[(n + j) % 2], half(i, n + j) + 1)
                                y = Y[:, bass.ds(i * 4 + (d + j), 1), 0:g.cols].rearrange("p a b -> p (a b)")
                                pool.tensor_tensor(y, FG[:, j % 2, 0:g.cols], y, ALU.add).then_inc(added, 1)

                        if n + KD + AHEAD > NT:
                            for k in range(KD // 4):
                                down(0, n + 4 * k, 4 * k)
                        else:
                            with pool.Fori(0, KD // 4) as i:
                                down(i, n, 0)
                        n += KD
                        if part < len(FFN_PARTS) - 1:
                            beside(2 * part + 1)
                    all_moved()
                elif name == "ln" and which != 4:
                    norm = st["norm"]
                    pool.wait_ge(spread_ready, norm + 1)
                    k = len(g.full_tiles)
                    pool.tensor_tensor(INV[:, 0:k], VAR[:, 0:k], MHALF[:, :].to_broadcast([P, k]), ALU.pow).then_inc(inv_ready, 1)
                    for j in POOL_LOW:
                        pool.wait_ge(x_hi, KD * norm + j + 1)
                        pool.tensor_tensor(XL[:, j, 0:g.cols], Y[:, j, 0:g.cols], XH[:, j, 0:g.cols].bitcast(F32),
                                           ALU.subtract).then_inc(x_lo, 1)
                elif name == "ln":
                    for t, (_, rows) in enumerate(g.tiles):
                        root(st["fwd"] + t, t, rows)
                pool.drain().then_inc(pool_end, 1)


_INS = ["x_prompt", "x_sample", "cache_conv", "cache_k", "cache_v", "cache_idx_k", "cache_mem_k", "cache_mem_v",
        "mem_prompt", "ffn1_gate", "ffn1_up", "ffn1_down", "ln1_g", "ln1_b", "w_mix_in", "conv_w", "w_mix_out",
        "ln2_g", "ln2_b", "w_mem_q", "w_mem_k", "w_mem_v", "w_mem_o", "ln3_g", "ln3_b",
        "ffn2_gate", "ffn2_up", "ffn2_down", "ln4_g", "ln4_b"]
_OUTS = [("y_prompt", (1, SEQ, D)), ("y_sample", (1, DEC, D)), ("conv_prompt", (1, 1, 2, DCONV)),
         ("k_prompt", (1, 1, SEQ, 2, DH)), ("v_prompt", (1, 1, SEQ, 2, DH)), ("ik_prompt", (1, 1, SEQ, DH)),
         ("mem_k", (1, 1, N_MEM, 4, 256)), ("mem_v", (1, 1, N_MEM, 4, 256)), ("conv_sample", (1, 1, 2, DCONV)),
         ("k_sample", (1, 1, DEC, 2, DH)), ("v_sample", (1, 1, DEC, 2, DH)), ("ik_sample", (1, 1, DEC, DH))]


def kernel(**inputs):
    import numpy as _np
    import concourse.bacc as _bacc
    from concourse.bass_utils import run_bass_kernel_spmd as _run

    nc = _bacc.Bacc("TRN2", target_bir_lowering=False, num_devices=1)
    arrays, ins, outs = {}, {}, {}
    for name in _INS:
        a = _np.ascontiguousarray(inputs[name])
        arrays[f"in_{name}"] = a
        ins[name] = nc.dram_tensor(f"in_{name}", a.shape, mybir.dt.from_np(a.dtype), kind="ExternalInput").ap()
    for name, shape in _OUTS:
        outs[name] = nc.dram_tensor(f"out_{name}", shape, F32, kind="ExternalOutput").ap()
    encoder_step(nc, ins, outs)
    r = _run(nc, [arrays], core_ids=[0])
    return tuple(r.results[0][f"out_{name}"] for name, _ in _OUTS)
```
